# Optimizing a Trainium2 kernel written in Bass

```python
import jax, jax.numpy as jnp
from jax import lax
import numpy as np
import math
import jax
import jax.numpy as jnp

D_MODEL = 1024
BATCH = 1
SEQ = 512
DEPTH = 1

D_MIX = D_MODEL
D_CONV = D_MIX // 2
CONV_GROUPS = 8
CONV_GROUP_DIM = D_CONV // CONV_GROUPS
CONV_WIDTH = 3
GDN_HEADS = 4
GDN_HEAD_DIM = (D_MIX - D_CONV) // GDN_HEADS
GDN_WIDTH = GDN_HEADS * GDN_HEAD_DIM
GDN_CONV_WIDTH = 4
GDN_CHUNK = 64
D_FF = 2816
NORM_EPS = 1e-6
D_IN_PROJ = 3 * D_CONV + 4 * GDN_WIDTH + 2 * GDN_HEADS


def rmsnorm(x, w, eps=NORM_EPS):
    xf = x.astype(jnp.float32)
    y = xf * lax.rsqrt(jnp.mean(xf * xf, axis=-1, keepdims=True) + eps)
    return (y * w.astype(jnp.float32)).astype(x.dtype)

def l2norm(x, eps=NORM_EPS):
    return x * lax.rsqrt(jnp.sum(x * x, axis=-1, keepdims=True) + eps)

def swiglu_ffn(x, w_in, w_out):
    gate, up = jnp.split(x @ w_in, 2, axis=-1)
    return (jax.nn.silu(gate) * up) @ w_out

def causal_depthwise_conv(x, w):
    K, C = w.shape
    return lax.conv_general_dilated(
        x, w[:, None, :].astype(x.dtype), window_strides=(1,), padding=[(K - 1, 0)],
        dimension_numbers=('NWC', 'WIO', 'NWC'), feature_group_count=C)

def short_conv_mixer(b_gate, c_gate, h, conv_w, out_gain):
    y = b_gate * causal_depthwise_conv(c_gate * h, conv_w)
    bsz, t, _ = y.shape
    y = rmsnorm(y.reshape(bsz, t, CONV_GROUPS, CONV_GROUP_DIM),
                out_gain.reshape(CONV_GROUPS, CONV_GROUP_DIM))
    return y.reshape(bsz, t, D_CONV)

def gated_delta_rule_chunked(q, k, v, g, beta):
    bsz, t, nh, dk = q.shape
    dv = v.shape[-1]
    c = GDN_CHUNK
    n = t // c
    q = q * (dk ** -0.5)
    to_chunks = lambda a: a.reshape(bsz, n, c, nh, a.shape[-1]).transpose(0, 3, 1, 2, 4)
    q, k, v = to_chunks(q), to_chunks(k), to_chunks(v)
    beta = beta.reshape(bsz, n, c, nh).transpose(0, 3, 1, 2)
    g = jnp.cumsum(g.reshape(bsz, n, c, nh).transpose(0, 3, 1, 2), axis=-1)
    k_beta = k * beta[..., None]
    v_beta = v * beta[..., None]
    causal = jnp.tril(jnp.ones((c, c), dtype=bool))
    strict = jnp.tril(jnp.ones((c, c), dtype=bool), -1)
    gdiff = g[..., :, None] - g[..., None, :]
    decay = jnp.exp(jnp.where(causal, gdiff, -jnp.inf))
    lower = jnp.where(strict, jnp.einsum('bhncd,bhnsd->bhncs', k_beta, k) * decay, 0.0)
    rhs = jnp.concatenate([v_beta, k_beta * jnp.exp(g)[..., None]], axis=-1)
    sol = lax.linalg.triangular_solve(lower, rhs, left_side=True, lower=True, unit_diagonal=True)
    u, w = sol[..., :dv], sol[..., dv:]
    attn_intra = jnp.where(causal, jnp.einsum('bhncd,bhnsd->bhncs', q, k) * decay, 0.0)
    q_dec = q * jnp.exp(g)[..., None]
    k_dec = k * jnp.exp(g[..., -1:] - g)[..., None]
    g_last = jnp.exp(g[..., -1])
    xs = tuple(jnp.moveaxis(a, 2, 0) for a in (q_dec, k_dec, u, w, attn_intra, g_last))

    def step(state, inp):
        q_c, k_c, u_c, w_c, a_c, gl = inp
        v_new = u_c - jnp.einsum('bhck,bhkv->bhcv', w_c, state)
        o_c = jnp.einsum('bhck,bhkv->bhcv', q_c, state) + jnp.einsum('bhcs,bhsv->bhcv', a_c, v_new)
        state = state * gl[..., None, None] + jnp.einsum('bhck,bhcv->bhkv', k_c, v_new)
        return state, o_c

    s0 = jnp.zeros((bsz, nh, dk, dv), jnp.float32)
    _, o = lax.scan(step, s0, xs)
    return o.transpose(1, 0, 3, 2, 4).reshape(bsz, t, nh, dv)

def gated_deltanet_mixer(q, k, v, z, b, a, conv_w, A_log, dt_bias, norm_w):
    bsz, t, _ = q.shape
    qkv = jax.nn.silu(causal_depthwise_conv(jnp.concatenate([q, k, v], axis=-1), conv_w))
    q, k, v = jnp.split(qkv.astype(jnp.float32), 3, axis=-1)
    heads = lambda a_: a_.reshape(bsz, t, GDN_HEADS, GDN_HEAD_DIM)
    q, k, v = l2norm(heads(q)), l2norm(heads(k)), heads(v)
    beta = jax.nn.sigmoid(b.astype(jnp.float32))
    g = -jnp.exp(A_log.astype(jnp.float32)) * jax.nn.softplus(a.astype(jnp.float32) + dt_bias.astype(jnp.float32))
    o = gated_delta_rule_chunked(q, k, v, g, beta)
    o = rmsnorm(o, norm_w) * jax.nn.silu(heads(z).astype(jnp.float32))
    return o.reshape(bsz, t, GDN_WIDTH).astype(z.dtype)

def first_inputs(seed: int = 0) -> dict:
    key = jax.random.key(seed)
    ks = jax.random.split(key, 20)
    nrm = lambda k_, shape, fan_in: jax.random.normal(k_, shape, jnp.float32) * (fan_in ** -0.5)
    gain = lambda k_, shape: 1.0 + 0.05 * jax.random.normal(k_, shape, jnp.float32)
    L = DEPTH
    return {
        'x': jax.random.normal(ks[0], (BATCH, SEQ, D_MODEL), jnp.float32),
        'ffn1_norm': gain(ks[1], (L, D_MODEL)),
        'ffn1_w_in': nrm(ks[2], (L, D_MODEL, 2 * D_FF), D_MODEL),
        'ffn1_w_out': nrm(ks[3], (L, D_FF, D_MODEL), D_FF),
        'mix_norm': gain(ks[4], (L, D_MODEL)),
        'w_mix_in': nrm(ks[5], (L, D_MODEL, D_IN_PROJ), D_MODEL),
        'conv_short_w': nrm(ks[6], (L, CONV_WIDTH, D_CONV), CONV_WIDTH),
        'conv_out_norm': gain(ks[7], (L, D_CONV)),
        'gdn_conv_w': nrm(ks[8], (L, GDN_CONV_WIDTH, 3 * GDN_WIDTH), GDN_CONV_WIDTH),
        'gdn_A_log': jnp.log(jax.random.uniform(ks[9], (L, GDN_HEADS), jnp.float32, 1.0, 16.0)),
        'gdn_dt_bias': 1.0 + 0.1 * jax.random.normal(ks[10], (L, GDN_HEADS), jnp.float32),
        'gdn_out_norm': gain(ks[11], (L, GDN_HEAD_DIM)),
        'w_mix_out': nrm(ks[12], (L, D_MIX, D_MODEL), D_MIX),
        'ffn2_norm': gain(ks[13], (L, D_MODEL)),
        'ffn2_w_in': nrm(ks[14], (L, D_MODEL, 2 * D_FF), D_MODEL),
        'ffn2_w_out': nrm(ks[15], (L, D_FF, D_MODEL), D_FF),
        'final_norm': gain(ks[16], (D_MODEL,)),
    }

def first_block(x, ffn1_norm, ffn1_w_in, ffn1_w_out, mix_norm, w_mix_in, conv_short_w, conv_out_norm,
              gdn_conv_w, gdn_A_log, gdn_dt_bias, gdn_out_norm, w_mix_out, ffn2_norm, ffn2_w_in,
              ffn2_w_out, final_norm):
    sizes = [D_CONV, D_CONV, D_CONV, GDN_WIDTH, GDN_WIDTH, GDN_WIDTH, GDN_WIDTH, GDN_HEADS, GDN_HEADS]
    splits = np.cumsum(sizes)[:-1].tolist()
    h = x
    for layer in range(DEPTH):
        h = h + 0.5 * swiglu_ffn(rmsnorm(h, ffn1_norm[layer]), ffn1_w_in[layer], ffn1_w_out[layer])
        u = rmsnorm(h, mix_norm[layer]) @ w_mix_in[layer]
        cb, cc, ch, gq, gk, gv, gz, gb, ga = jnp.split(u, splits, axis=-1)
        y_conv = short_conv_mixer(cb, cc, ch, conv_short_w[layer], conv_out_norm[layer])
        y_gdn = gated_deltanet_mixer(gq, gk, gv, gz, gb, ga, gdn_conv_w[layer], gdn_A_log[layer],
                                     gdn_dt_bias[layer], gdn_out_norm[layer])
        h = h + jnp.concatenate([y_conv, y_gdn], axis=-1) @ w_mix_out[layer]
        h = h + 0.5 * swiglu_ffn(rmsnorm(h, ffn2_norm[layer]), ffn2_w_in[layer], ffn2_w_out[layer])
    return rmsnorm(h, final_norm)


DEPTH_2 = 2

N_A_LAYERS = DEPTH_2 // 2
N_B_LAYERS = DEPTH_2 - N_A_LAYERS
MEM_LEN = 256
MEM_HEADS = 4
MEM_HEAD_DIM = 64
MEM_W = MEM_HEADS * MEM_HEAD_DIM
MIX_W = D_MODEL
MAIN_W = MIX_W - MEM_W
GLA_HEADS = 4
GLA_DV = MAIN_W // GLA_HEADS
GLA_DK = GLA_DV // 2
GLA_RANK = 16
GLA_GATE_NORM = 16.0
GLA_CHUNK = 16
NSA_HEADS = 12
NSA_GROUPS = 4
NSA_HEAD_DIM = MAIN_W // NSA_HEADS
NSA_REP = NSA_HEADS // NSA_GROUPS
CMP_BLOCK = 32
CMP_STRIDE = 16
CMP_HIDDEN = 128
SEL_BLOCK = 64
SEL_TOPK = 16
WINDOW = 512
Q_BLOCK = 64
REL_BUCKETS = 32
REL_MAX_DIST = 128
FFN_DIM = 2816
EPS = 1e-6
GLA_SIZES = (GLA_HEADS * GLA_DK, GLA_HEADS * GLA_DK, GLA_HEADS * GLA_DV, GLA_HEADS * GLA_DV, GLA_RANK, MEM_W)
GLA_IN = sum(GLA_SIZES)
NSA_SIZES = (NSA_HEADS * NSA_HEAD_DIM, NSA_HEADS * 3, MEM_W)
NSA_IN = sum(NSA_SIZES)
SHARED_KV_W = 6 * NSA_GROUPS * NSA_HEAD_DIM


def rmsnorm_2(x, g):
    xf = x.astype(jnp.float32)
    y = xf * lax.rsqrt(jnp.mean(xf * xf, axis=-1, keepdims=True) + EPS)
    return (y * g.astype(jnp.float32)).astype(x.dtype)

def split_cols(x, sizes):
    out = []
    start = 0
    for n in sizes:
        out.append(x[..., start:start + n])
        start += n
    return out

def rel_bucket(dist):
    dist = jnp.maximum(dist, 0)
    max_exact = REL_BUCKETS // 2
    large = max_exact + (jnp.log(jnp.maximum(dist, 1).astype(jnp.float32) / max_exact)
                         / math.log(REL_MAX_DIST / max_exact) * (REL_BUCKETS - max_exact)).astype(jnp.int32)
    large = jnp.minimum(large, REL_BUCKETS - 1)
    return jnp.where(dist < max_exact, dist, large)

def masked_softmax(s, mask):
    s = jnp.where(mask, s.astype(jnp.float32), -1e30)
    m = jnp.max(s, axis=-1, keepdims=True)
    p = jnp.where(mask, jnp.exp(s - m), 0.0)
    return p / jnp.maximum(jnp.sum(p, axis=-1, keepdims=True), 1e-30)

def gla_mixer(q, k, v, log_a, g_out, out_norm):
    dtype = v.dtype
    B, S = q.shape[0], q.shape[1]
    C = GLA_CHUNK
    N = S // C

    def chunked(t):
        return t.reshape(B, N, C, GLA_HEADS, t.shape[-1]).transpose(0, 3, 1, 2, 4).astype(jnp.float32)

    qc = chunked(q) * GLA_DK ** -0.5
    kc = chunked(k)
    vc = chunked(v)
    b = lax.cumsum(chunked(log_a), axis=3)
    causal = jnp.tril(jnp.ones((C, C), dtype=bool))
    diff = b[..., :, None, :] - b[..., None, :, :]
    decay = jnp.exp(jnp.where(causal[:, :, None], diff, -jnp.inf))
    attn = jnp.einsum('bhnid,bhnjd,bhnijd->bhnij', qc, kc, decay)
    o_intra = jnp.einsum('bhnij,bhnjv->bhniv', attn, vc)
    b_last = b[..., -1:, :]
    q_in = qc * jnp.exp(b)
    k_out = kc * jnp.exp(b_last - b)
    a_last = jnp.exp(b_last[..., 0, :])

    def step(state, inp):
        qi, ki, vi, ai = inp
        o = jnp.einsum('bhcd,bhdv->bhcv', qi, state)
        state = ai[..., None] * state + jnp.einsum('bhcd,bhcv->bhdv', ki, vi)
        return state, o

    xs = (jnp.moveaxis(q_in, 2, 0), jnp.moveaxis(k_out, 2, 0), jnp.moveaxis(vc, 2, 0), jnp.moveaxis(a_last, 2, 0))
    state0 = jnp.zeros((B, GLA_HEADS, GLA_DK, GLA_DV), jnp.float32)
    _, o_inter = lax.scan(step, state0, xs)
    o = o_intra + jnp.moveaxis(o_inter, 0, 2)
    o = o.transpose(0, 2, 3, 1, 4).reshape(B, S, GLA_HEADS, GLA_DV)
    o = rmsnorm_2(o, out_norm) * jax.nn.silu(g_out.astype(jnp.float32))
    return o.reshape(B, S, GLA_HEADS * GLA_DV).astype(dtype)

def mem_attention(q, mem_kv):
    B, S = q.shape[0], q.shape[1]
    M = mem_kv.shape[1]
    k, v = split_cols(mem_kv, (MEM_W, MEM_W))
    qh = q.reshape(B, S, MEM_HEADS, MEM_HEAD_DIM)
    kh = k.reshape(B, M, MEM_HEADS, MEM_HEAD_DIM)
    vh = v.reshape(B, M, MEM_HEADS, MEM_HEAD_DIM)
    s = jnp.einsum('bshd,bmhd->bhsm', qh, kh).astype(jnp.float32) * MEM_HEAD_DIM ** -0.5
    p = jax.nn.softmax(s, axis=-1)
    o = jnp.einsum('bhsm,bmhd->bshd', p, vh.astype(jnp.float32))
    return o.reshape(B, S, MEM_W).astype(q.dtype)

def shared_kv(h, kv_norm, w_kv, cmp_pos, cmp_w1, cmp_b1, cmp_w2, cmp_b2):
    B, S = h.shape[0], h.shape[1]
    G, Dh = NSA_GROUPS, NSA_HEAD_DIM
    kv = (rmsnorm_2(h, kv_norm) @ w_kv).reshape(B, S, 6, G, Dh).transpose(2, 0, 3, 1, 4)
    NC = (S - CMP_BLOCK) // CMP_STRIDE + 1
    win = jnp.arange(NC)[:, None] * CMP_STRIDE + jnp.arange(CMP_BLOCK)[None, :]

    def compress(t, j):
        blocks = t[:, :, win] + cmp_pos[j]
        flat = blocks.reshape(B, G, NC, CMP_BLOCK * Dh)
        return jax.nn.silu(flat @ cmp_w1[j] + cmp_b1[j]) @ cmp_w2[j] + cmp_b2[j]

    kc = compress(kv[0], 0)
    vc = compress(kv[1], 1)
    return (kc, vc, kv[2], kv[3], kv[4], kv[5])

def nsa_mixer(q, gates, shared, rel_bias):
    kc, vc, ks, vs, kw, vw = shared
    B, S = q.shape[0], q.shape[1]
    G, R, Dh = NSA_GROUPS, NSA_REP, NSA_HEAD_DIM
    NC = kc.shape[2]
    NSB = S // SEL_BLOCK
    n_sel = min(SEL_TOPK, NSB)
    qg = (q * Dh ** -0.5).reshape(B, S, G, R, Dh).transpose(0, 2, 3, 1, 4)
    gg = gates.reshape(B, S, G, R, 3).transpose(0, 2, 3, 1, 4)
    kb = ks.reshape(B, G, NSB, SEL_BLOCK, Dh)
    vb = vs.reshape(B, G, NSB, SEL_BLOCK, Dh)
    kw_p = jnp.pad(kw, ((0, 0), (0, 0), (WINDOW, 0), (0, 0)))
    vw_p = jnp.pad(vw, ((0, 0), (0, 0), (WINDOW, 0), (0, 0)))
    cmp_start = jnp.arange(NC) * CMP_STRIDE
    cmp_end = cmp_start + CMP_BLOCK - 1
    sel_idx = jnp.arange(NSB)
    sel_start = sel_idx * SEL_BLOCK
    overlap = ((cmp_start[:, None] < sel_start[None, :] + SEL_BLOCK)
               & (cmp_end[:, None] >= sel_start[None, :])).astype(jnp.float32)
    tbl = rel_bias.astype(jnp.float32).reshape(REL_BUCKETS, G, R)
    g_idx = jnp.arange(G)[None, :, None, None]

    def common_bias(dist):
        return tbl[rel_bucket(dist)].transpose(2, 3, 0, 1)

    def group_bias(dist):
        return jnp.moveaxis(tbl[rel_bucket(dist), g_idx], -1, 2)

    def block(c):
        t0 = c * Q_BLOCK
        t = t0 + jnp.arange(Q_BLOCK)
        qb = lax.dynamic_slice_in_dim(qg, t0, Q_BLOCK, axis=3)
        gb = lax.dynamic_slice_in_dim(gg, t0, Q_BLOCK, axis=3)
        d_c = t[:, None] - cmp_end[None, :]
        s_c = jnp.einsum('bgrqd,bgkd->bgrqk', qb, kc).astype(jnp.float32) + common_bias(d_c)
        p_c = masked_softmax(s_c, d_c >= 0)
        o_c = jnp.einsum('bgrqk,bgkd->bgrqd', p_c, vc.astype(jnp.float32))
        imp = jnp.einsum('bgrqk,kj->bgqj', p_c, overlap)
        cur = (t // SEL_BLOCK)[:, None]
        jj = sel_idx[None, :]
        forced = (jj == 0) | (jj == cur) | (jj == cur - 1)
        score = jnp.where(forced, 1e4, jnp.where(jj <= cur, imp, -1.0))
        _, idx = lax.top_k(score, n_sel)
        gather = jax.vmap(jax.vmap(lambda blk, ix: blk[ix]))
        k_sel = gather(kb, idx).reshape(B, G, Q_BLOCK, n_sel * SEL_BLOCK, Dh)
        v_sel = gather(vb, idx).reshape(B, G, Q_BLOCK, n_sel * SEL_BLOCK, Dh)
        pos = (idx[..., None] * SEL_BLOCK + jnp.arange(SEL_BLOCK)).reshape(B, G, Q_BLOCK, n_sel * SEL_BLOCK)
        d_s = t[None, None, :, None] - pos
        s_s = jnp.einsum('bgrqd,bgqkd->bgrqk', qb, k_sel).astype(jnp.float32) + group_bias(d_s)
        p_s = masked_softmax(s_s, (d_s >= 0)[:, :, None])
        o_s = jnp.einsum('bgrqk,bgqkd->bgrqd', p_s, v_sel.astype(jnp.float32))
        kwb = lax.dynamic_slice_in_dim(kw_p, t0, WINDOW + Q_BLOCK, axis=2)
        vwb = lax.dynamic_slice_in_dim(vw_p, t0, WINDOW + Q_BLOCK, axis=2)
        s_pos = t0 - WINDOW + jnp.arange(WINDOW + Q_BLOCK)
        d_w = t[:, None] - s_pos[None, :]
        mask_w = (d_w >= 0) & (d_w < WINDOW) & (s_pos[None, :] >= 0)
        s_w = jnp.einsum('bgrqd,bgkd->bgrqk', qb, kwb).astype(jnp.float32) + common_bias(d_w)
        p_w = masked_softmax(s_w, mask_w)
        o_w = jnp.einsum('bgrqk,bgkd->bgrqd', p_w, vwb.astype(jnp.float32))
        o = gb[..., 0:1] * o_c + gb[..., 1:2] * o_s + gb[..., 2:3] * o_w
        return o.astype(q.dtype)

    out = lax.map(block, jnp.arange(S // Q_BLOCK))
    return out.transpose(1, 0, 4, 2, 3, 5).reshape(B, S, NSA_HEADS * Dh)

def conv_ffn(x, w_up, conv_w, conv_b, w_down):
    S = x.shape[1]
    u = x @ w_up
    u_pad = jnp.pad(u, ((0, 0), (CONV_WIDTH - 1, 0), (0, 0)))
    hc = conv_b
    for j in range(CONV_WIDTH):
        hc = hc + conv_w[j] * u_pad[:, j:j + S]
    a, b = split_cols(hc, (FFN_DIM, FFN_DIM))
    return (jax.nn.silu(a) * b) @ w_down

def second_inputs(seed: int = 0) -> dict:
    key = jax.random.key(seed)
    ks = jax.random.split(key, 26)
    f32 = jnp.float32

    def nrm(k, shape, scale):
        return jax.random.normal(k, shape, f32) * scale

    def gain(k, shape):
        return 1.0 + 0.02 * jax.random.normal(k, shape, f32)

    res = (2.0 * DEPTH_2) ** -0.5
    return {
        'x': nrm(ks[0], (BATCH, SEQ, D_MODEL), 1.0),
        'mem': nrm(ks[1], (BATCH, MEM_LEN, D_MODEL), 1.0),
        'norm_mix': gain(ks[2], (DEPTH_2, D_MODEL)),
        'norm_mem': gain(ks[3], (DEPTH_2, D_MODEL)),
        'w_mem_kv': nrm(ks[4], (DEPTH_2, D_MODEL, 2 * MEM_W), D_MODEL ** -0.5),
        'w_out': nrm(ks[5], (DEPTH_2, MIX_W, D_MODEL), MIX_W ** -0.5 * res),
        'norm_ffn': gain(ks[6], (DEPTH_2, D_MODEL)),
        'w_up': nrm(ks[7], (DEPTH_2, D_MODEL, 2 * FFN_DIM), D_MODEL ** -0.5),
        'conv_w': nrm(ks[8], (DEPTH_2, CONV_WIDTH, 2 * FFN_DIM), CONV_WIDTH ** -0.5),
        'conv_b': nrm(ks[9], (DEPTH_2, 2 * FFN_DIM), 0.01),
        'w_down': nrm(ks[10], (DEPTH_2, FFN_DIM, D_MODEL), FFN_DIM ** -0.5 * res),
        'gla_w_in': nrm(ks[11], (N_A_LAYERS, D_MODEL, GLA_IN), D_MODEL ** -0.5),
        'gla_w_gate_up': nrm(ks[12], (N_A_LAYERS, GLA_RANK, GLA_HEADS * GLA_DK), GLA_RANK ** -0.5),
        'gla_b_gate': nrm(ks[13], (N_A_LAYERS, GLA_HEADS * GLA_DK), 0.01),
        'gla_out_norm': gain(ks[14], (N_A_LAYERS, GLA_DV)),
        'nsa_w_in': nrm(ks[15], (N_B_LAYERS, D_MODEL, NSA_IN), D_MODEL ** -0.5),
        'kv_norm': gain(ks[16], (D_MODEL,)),
        'w_kv_shared': nrm(ks[17], (D_MODEL, SHARED_KV_W), D_MODEL ** -0.5),
        'cmp_pos': nrm(ks[18], (2, CMP_BLOCK, NSA_HEAD_DIM), 0.1),
        'cmp_w1': nrm(ks[19], (2, CMP_BLOCK * NSA_HEAD_DIM, CMP_HIDDEN), (CMP_BLOCK * NSA_HEAD_DIM) ** -0.5),
        'cmp_b1': nrm(ks[20], (2, CMP_HIDDEN), 0.01),
        'cmp_w2': nrm(ks[21], (2, CMP_HIDDEN, NSA_HEAD_DIM), CMP_HIDDEN ** -0.5),
        'cmp_b2': nrm(ks[22], (2, NSA_HEAD_DIM), 0.01),
        'rel_bias': nrm(ks[23], (REL_BUCKETS, NSA_HEADS), 0.5),
        'final_norm': gain(ks[24], (D_MODEL,)),
    }

def second_block(x, mem, norm_mix, norm_mem, w_mem_kv, w_out, norm_ffn, w_up, conv_w, conv_b, w_down,
              gla_w_in, gla_w_gate_up, gla_b_gate, gla_out_norm, nsa_w_in, kv_norm, w_kv_shared,
              cmp_pos, cmp_w1, cmp_b1, cmp_w2, cmp_b2, rel_bias, final_norm):
    B, S = x.shape[0], x.shape[1]
    h = x
    shared = None
    for i in range(DEPTH_2):
        if i == N_A_LAYERS:
            shared = shared_kv(h, kv_norm, w_kv_shared, cmp_pos, cmp_w1, cmp_b1, cmp_w2, cmp_b2)
        xn = rmsnorm_2(h, norm_mix[i])
        mem_kv = rmsnorm_2(mem, norm_mem[i]) @ w_mem_kv[i]
        if i < N_A_LAYERS:
            q, k, v, g, lr, mq = split_cols(xn @ gla_w_in[i], GLA_SIZES)
            log_a = jax.nn.log_sigmoid((lr @ gla_w_gate_up[i] + gla_b_gate[i]).astype(jnp.float32)) / GLA_GATE_NORM
            main = gla_mixer(q.reshape(B, S, GLA_HEADS, GLA_DK), k.reshape(B, S, GLA_HEADS, GLA_DK),
                             v.reshape(B, S, GLA_HEADS, GLA_DV), log_a.reshape(B, S, GLA_HEADS, GLA_DK),
                             g.reshape(B, S, GLA_HEADS, GLA_DV), gla_out_norm[i])
        else:
            q, gl, mq = split_cols(xn @ nsa_w_in[i - N_A_LAYERS], NSA_SIZES)
            gates = jax.nn.sigmoid(gl.astype(jnp.float32)).reshape(B, S, NSA_HEADS, 3)
            main = nsa_mixer(q.reshape(B, S, NSA_HEADS, NSA_HEAD_DIM), gates, shared, rel_bias)
        mo = mem_attention(mq, mem_kv)
        h = h + jnp.concatenate([main.astype(xn.dtype), mo.astype(xn.dtype)], axis=-1) @ w_out[i]
        h = h + conv_ffn(rmsnorm_2(h, norm_ffn[i]), w_up[i], conv_w[i], conv_b[i], w_down[i])
    return rmsnorm_2(h, final_norm)


def setup_inputs(seed=0):
    out = dict(first_inputs(seed))
    for name, value in second_inputs(seed + 1).items():
        if name != "x":
            out[name + "_2"] = value
    return out


def reference(
    x, ffn1_norm, ffn1_w_in, ffn1_w_out, mix_norm, w_mix_in, conv_short_w, conv_out_norm,
    gdn_conv_w, gdn_A_log, gdn_dt_bias, gdn_out_norm, w_mix_out, ffn2_norm, ffn2_w_in,
    ffn2_w_out, final_norm, mem_2, norm_mix_2, norm_mem_2, w_mem_kv_2, w_out_2, norm_ffn_2,
    w_up_2, conv_w_2, conv_b_2, w_down_2, gla_w_in_2, gla_w_gate_up_2, gla_b_gate_2,
    gla_out_norm_2, nsa_w_in_2, kv_norm_2, w_kv_shared_2, cmp_pos_2, cmp_w1_2, cmp_b1_2,
    cmp_w2_2, cmp_b2_2, rel_bias_2, final_norm_2,
):
    x = first_block(
        x, ffn1_norm, ffn1_w_in, ffn1_w_out, mix_norm, w_mix_in, conv_short_w, conv_out_norm,
        gdn_conv_w, gdn_A_log, gdn_dt_bias, gdn_out_norm, w_mix_out, ffn2_norm, ffn2_w_in,
        ffn2_w_out, final_norm,
    )
    return second_block(
        x, mem_2, norm_mix_2, norm_mem_2, w_mem_kv_2, w_out_2, norm_ffn_2, w_up_2, conv_w_2,
        conv_b_2, w_down_2, gla_w_in_2, gla_w_gate_up_2, gla_b_gate_2, gla_out_norm_2,
        nsa_w_in_2, kv_norm_2, w_kv_shared_2, cmp_pos_2, cmp_w1_2, cmp_b1_2, cmp_w2_2, cmp_b2_2,
        rel_bias_2, final_norm_2,
    )


_drawn_inputs = setup_inputs


def setup_inputs(seed=0):
    import zlib

    import numpy as np

    out = dict(_drawn_inputs(seed))
    spreads = {}
    factors = {'gdn_A_log': 2.868,
     'gdn_dt_bias': 8.0,
     'gdn_out_norm': 3.243,
     'norm_mix_2': 4.145,
     'norm_mem_2': 8.0,
     'norm_ffn_2': 4.966,
     'conv_b_2': 8.0,
     'gla_b_gate_2': 8.0,
     'gla_out_norm_2': 8.0,
     'kv_norm_2': 8.0,
     'cmp_pos_2': 16.49,
     'cmp_b1_2': 64.0,
     'cmp_b2_2': 200.0,
     'final_norm_2': 22.635,
     'rel_bias_2': 3.527}
    for name, (base, spread) in spreads.items():
        noise = np.random.default_rng([zlib.crc32(name.encode()), seed]).standard_normal(out[name].shape)
        drawn = base * np.exp(spread * noise) if base else spread * noise
        out[name] = jnp.asarray(drawn.astype(out[name].dtype))
    for name, factor in factors.items():
        out[name] = (out[name] * factor).astype(out[name].dtype)
    return out
```

```python
import concourse.bass as bass
import numpy as np
from concourse import mybir
from contextlib import ExitStack

ALU = mybir.AluOpType
ACT = mybir.ActivationFunctionType
AX = mybir.AxisListType.X
F32 = mybir.dt.float32
BF16 = mybir.dt.bfloat16
I32 = mybir.dt.int32

P = 128
S = 512
D = 1024
KD = D // P
TT = S // P
FF = 2816
NF = FF // P
M = 256
EPS = 1e-6
SLOT = 2048
CREDIT = 2
CREDIT_PE = 8
CREDIT_EV = 8


class Dense:

    def __init__(self, name, iters, panels, tiles, xs, need):
        self.name, self.iters, self.panels, self.tiles, self.xs, self.need = name, iters, panels, tiles, xs, need
        self.segments = []
        for t, tile in enumerate(tiles):
            for j in sorted({term[0] for term in tile["terms"]}):
                self.segments.append((t, j))


class Plan:

    def __init__(self, stages):
        self.order = stages
        self.stages = {s.name: s for s in stages}
        n, segments, landed = 0, 0, [0, 0]
        evac = {"act": 0, "dve": 0}
        bank_last = {}
        for s in stages:
            assert s.iters == 1 or len(s.panels) % 2 == 0, s.name
            s.panel0, s.seg0, s.landed0, s.evac0 = n, segments, list(landed), dict(evac)
            s.slot = [(n + j) % 2 for j in range(len(s.panels))]
            s.landed_step = [16 * sum(len(p) for p, q in zip(s.panels, s.slot) if q == k) for k in (0, 1)]
            s.evac_step = {e: sum(t["by"] == e for t in s.tiles) for e in evac}
            s.before = {t["bank"]: bank_last[t["bank"]] for t in s.tiles if t["bank"] in bank_last}
            for t, tile in enumerate(s.tiles):
                bank_last[tile["bank"]] = (tile["by"], self.evac(s, s.iters - 1, t))
            n += s.iters * len(s.panels)
            segments += s.iters * len(s.segments)
            landed = [a + s.iters * b for a, b in zip(landed, s.landed_step)]
            evac = {e: evac[e] + s.iters * s.evac_step[e] for e in evac}
        self.panels = n

    def landed(self, s, i, j):
        here = 16 * sum(len(s.panels[q]) for q in range(j + 1) if s.slot[q] == s.slot[j])
        return s.landed0[s.slot[j]] + i * s.landed_step[s.slot[j]] + here

    def full(self, s, i, t):
        at = max(k for k, (u, _) in enumerate(s.segments) if u == t)
        return CREDIT_PE + s.seg0 + i * len(s.segments) + at + 1

    def used(self, s, i, j):
        at = max(k for k, (_, p) in enumerate(s.segments) if p == j)
        return CREDIT_PE + s.seg0 + i * len(s.segments) + at + 1

    def evac(self, s, i, t):
        e = s.tiles[t]["by"]
        return CREDIT_EV + s.evac0[e] + i * s.evac_step[e] + sum(x["by"] == e for x in s.tiles[:t + 1])


def param_layout():
    names = [("ffn1_norm", 8), ("mix_norm", 8), ("ffn2_norm", 8), ("final_norm", 8), ("norm_mix_2", 16),
             ("norm_mem_2", 16), ("norm_ffn_2", 16), ("kv_norm_2", 8), ("final_norm_2", 8), ("cmp_b1_2", 2),
             ("gdn_out_norm", 1), ("conv_short_w", 12), ("conv_out_norm", 4),
             ("gdn_conv_w", 48), ("conv_w_2", 264), ("conv_b_2", 88)]
    at, first = {}, 0
    for name, n in names:
        at[name] = (first, n)
        first += n
    return at, first


PAR_AT, NPAR = param_layout()
NPT = -(-NPAR // P)
NPAR_DMA = sum((f + n - 1) // P - f // P + 1 for f, n in PAR_AT.values())


def build(nc, A, out):
    with ExitStack() as ctx:
        sems = {}

        def sem(name):
            if name not in sems:
                sems[name] = ctx.enter_context(nc.semaphore(name))
            return sems[name]

        def sb(name, shape, dt=F32):
            return ctx.enter_context(nc.sbuf_tensor(name, shape, dt))

        hT = sb("hT", [P, KD, S])
        xH = sb("xH", [P, 10, S], BF16)
        xL = sb("xL", [P, 10, S], BF16)
        raw = sb("raw", [P, 2, SLOT])
        wH = sb("wH", [P, 2, SLOT], BF16)
        wL = sb("wL", [P, 2, SLOT], BF16)
        par = sb("par", [P, NPT * P])
        ident = sb("ident", [P, P])
        ones = sb("ones", [P, P])
        eps = sb("eps", [P, 1])
        ones64 = sb("ones64", [P, P])
        lvl = sb("lvl", [P, 7, P])
        pick = sb("pick", [4, 4, P])
        hv = sb("hv", [4, 4])
        col = sb("col", [P, 8, 16])
        sq = sb("sq", [P, 2, S])
        rstd = sb("rstd", [P, S])
        xn = sb("xn", [P, 2, S])
        R = 2048
        arena = sb("arena", [P, 14 * R])

        def region(a, n=1):
            return arena[:, a * R:(a + n) * R]

        gH = region(0, 3)[:, 0:NF * S // 2].bitcast(BF16).rearrange("p (f s) -> p f s", s=S)
        gL = region(3, 3)[:, 0:NF * S // 2].bitcast(BF16).rearrange("p (f s) -> p f s", s=S)
        sg = region(6).rearrange("p (b s) -> p b s", s=S)
        prod = region(7).rearrange("p (b s) -> p b s", s=S)
        cv = region(8).rearrange("p (b s) -> p b s", s=S)
        rows = region(9, 2).rearrange("p (t c) -> p t c", c=D)
        stage = region(13)[:, 0:NPT * P].rearrange("p (t c) -> p t c", c=P)

        bank = [ctx.enter_context(nc.psum_tensor(f"bank{b}", [P, S], F32)) for b in range(8)]

        memH = region(8)[:, 0:1024].bitcast(BF16).rearrange("p (k m) -> p k m", m=M)
        memL = region(8)[:, 1024:2048].bitcast(BF16).rearrange("p (k m) -> p k m", m=M)

        def panel(w, k, c0, cols, step=0, row0=0, nrow=P, first=0, pitch=None):
            def src(i):
                at = c0 + i * step if step else c0
                return w[row0:row0 + k * nrow, bass.ds(at, cols)].rearrange("(k p) n -> p k n", p=nrow)
            return (nrow, first, (k, cols, pitch), src)

        def features(b, j, cols, at, width=P, k=KD, nk=P, x0=0, by="dve"):
            return {"bank": b, "rows": width, "cols": S, "token": False, "by": by,
                    "terms": [(j, nk, q * cols + at, width, x0 + q) for q in range(k)]}

        def up_stage(name, w, need, by=("act", "act", "dve", "dve")):
            return Dense(name, NF // 2, [[panel(w, KD, 0, 256, 256)], [panel(w, KD, FF, 256, 256)]],
                         [features(b, b // 2, 256, P * (b % 2), by=by[b]) for b in range(4)], (xH, xL), need)

        def down_stage(name, w, need):
            half = NF // 2
            panels = [[panel(w, half, P * (j // 2), P, 256, row0=(j % 2) * half * P)] for j in range(4)]
            tiles = [{"bank": m, "rows": P, "cols": S, "token": False, "by": "dve",
                      "terms": [(2 * m + hh, P, q * P, P, hh * half + q) for hh in range(2) for q in range(half)]}
                     for m in range(2)]
            return Dense(name, KD // 2, panels, tiles, (gH, gL), need)

        def tokens(b, j, cols, t, k=KD, by="dve"):
            return {"bank": b, "rows": P, "at": 0, "token": True, "by": by, "x": slice(t * P, (t + 1) * P),
                    "terms": [(j, P, q * cols, cols, q) for q in range(k)]}

        def mem_stage(l):
            w = A["w_mem_kv_2"][l]
            tiles = [features(u, 0, 256, P * u, by="act") for u in range(2)]
            for tile in tiles:
                tile["cols"] = M
            return Dense(f"mem{l}_kv", 1, [[panel(w, KD, 0, 256)], [panel(w, KD, 256, 256)]],
                         tiles + [tokens(2 + u, 1, 256, u, by="dve") for u in range(2)],
                         (memH, memL), ("mem_ready", l + 1))

        def out_stage(name, w, need):
            return Dense(name, 2, [[panel(w, KD, 0, 256, 512)], [panel(w, KD, 256, 256, 512)]],
                         [features(b, b // 2, 256, P * (b % 2)) for b in range(4)], (xH, xL), need)

        XFILL = [8, 8, 8, 8, 8, 10, 8, 8, 8, 14, 8]

        def xfill(k):
            return ("x_ready", sum(XFILL[:k + 1]))

        w_mix = A["w_mix_in"][0]
        stages = [up_stage("ffn0_up", A["ffn1_w_in"][0], xfill(0)),
                  down_stage("ffn0_down", A["ffn1_w_out"][0], ("act_ready", NF + CREDIT)),
                  Dense("mix_ba", 1, [[panel(w_mix, KD, 7 * 512, 8)]],
                        [features(0, 0, 8, 0, width=4, by="act"), features(1, 0, 8, 4, width=4, by="dve")],
                        (xH, xL), xfill(1)),
                  Dense("mix_in", 7, [[panel(w_mix, KD, 0, 256, 512)], [panel(w_mix, KD, 256, 256, 512)]],
                        [features(b, b // 2, 256, P * (b % 2), by=("act", "dve")[b % 2]) for b in range(4)],
                        (xH, xL), xfill(1)),
                  out_stage("mix_out", A["w_mix_out"][0], xfill(2)),
                  up_stage("ffn1_up", A["ffn2_w_in"][0], xfill(3)),
                  down_stage("ffn1_down", A["ffn2_w_out"][0], ("act_ready", 2 * NF + CREDIT)),
                  mem_stage(0)]
        w_gla = A["gla_w_in_2"][0]
        GQ, GK, GV, GG, GR, GM = 0, 384, 768, 1536, 2304, 2320
        stages += [
            Dense("gla_rest", 1, [[panel(w_gla, KD, GR, 16)], [panel(w_gla, KD, GM, 256)]],
                  [features(0, 0, 16, 0, width=16, by="act")] +
                  [features(1 + u, 1, 256, P * u, by="dve") for u in range(2)], (xH, xL), xfill(4)),
            Dense("gla_q", 1, [[panel(w_gla, KD, GQ + 192 * j, 192)] for j in range(2)],
                  [features(b, b // 2, 192, 96 * (b % 2), width=96, by="act") for b in range(4)], (xH, xL), xfill(4)),
            Dense("gla_k", 1, [[panel(w_gla, KD, GK + 192 * j, 192)] for j in range(2)],
                  [features(b, b // 2, 192, 96 * (b % 2), width=96, by="dve") for b in range(4)], (xH, xL), xfill(4)),
            Dense("gla_v", 1, [[panel(w_gla, KD, GV + 256 * j, 256)] for j in range(3)],
                  [tokens(t, j, 256, t, by=("act", "dve")[t % 2]) for j in range(3) for t in range(TT)],
                  (xH, xL), xfill(4)),
            Dense("gla_g", 2, [[panel(w_gla, KD, GG + 192 * j, 192, 384)] for j in range(2)],
                  [features(b, b // 2, 192, 96 * (b % 2), width=96, by="act") for b in range(4)],
                  (xH, xL), xfill(4)),
            Dense("gla_out", 4, [[panel(A["w_out_2"][0], 8, P * j, P, 256, nrow=96),
                                  panel(A["w_out_2"][0], 2, P * j, P, 256, row0=768, first=1024)] for j in range(2)],
                  [{"bank": j, "rows": P, "cols": S, "token": False, "by": "dve",
                    "terms": [(j, 96, q * P, P, q) for q in range(8)] +
                             [(j, P, 1024 + q * P, P, 8 + q) for q in range(2)]} for j in range(2)],
                  (xH, xL), xfill(5)),
            up_stage("ffn2_up", A["w_up_2"][0], xfill(6), by=("dve",) * 4),
            down_stage("ffn2_down", A["w_down_2"][0], ("act_ready", 3 * NF + CREDIT)),
            mem_stage(1)]
        w_kv, w_nsa = A["w_kv_shared_2"], A["nsa_w_in_2"][0]

        def head_pairs(j):
            parts = []
            for u in range(2):
                t = 2 * j + u
                for half in range(2):
                    head = t + 3 * (t // 3) + 3 * half
                    parts.append(panel(w_nsa, KD, 64 * head, 64, first=128 * u + 64 * half, pitch=256))
            return parts

        stages += [
            Dense("kv_f", 1, [[panel(w_kv, KD, c, 256)] for c in (0, 256, 512, 1024)],
                  [features(t % 4, t // 2, 256, P * (t % 2), by=("act", "dve")[t % 2]) for t in range(8)],
                  (xH, xL), xfill(7)),
            Dense("kv_t", 1, [[panel(w_kv, KD, c, 256)] for c in (768, 1280)],
                  [tokens(t, j, 256, t, by=("act", "dve")[t % 2]) for j in range(2) for t in range(TT)],
                  (xH, xL), xfill(7)),
            Dense("nsa_q", 1, [head_pairs(j) for j in range(3)],
                  [features(t % 4, t // 2, 256, P * (t % 2), by=("act", "dve")[t % 2]) for t in range(6)],
                  (xH, xL), xfill(8)),
            Dense("nsa_g", 1, [[panel(w_nsa, KD, 768, 36)], [panel(w_nsa, KD, 804, 256)]],
                  [tokens(t, 0, 36, t, by="act") for t in range(TT)] +
                  [features(t, 1, 256, P * t, by="dve") for t in range(2)], (xH, xL), xfill(8)),
            out_stage("nsa_out", A["w_out_2"][1], xfill(9)),
            up_stage("ffn3_up", A["w_up_2"][1], xfill(10), by=("dve",) * 4),
            down_stage("ffn3_down", A["w_down_2"][1], ("act_ready", 4 * NF + CREDIT))]
        plan = Plan(stages)
        nc_block = ctx.enter_context(nc.Block())

        ffn_index = {"ffn0_up": 0, "ffn1_up": 1, "ffn2_up": 2, "ffn3_up": 3}
        FILLS = ["norm", "norm", "mixer", "norm", "norm", "mixer", "norm", "norm", "norm", "mixer", "norm"]

        def xbase(f):
            return sum(XFILL[:f])

        def nfill(f):
            return sum(n for n, kind in zip(XFILL[:f], FILLS[:f]) if kind == "norm")

        def h_from(name):
            s = plan.stages[name]
            n = len(s.tiles)
            return lambda k: (sem("evac_dve"), plan.evac(s, k // n, k % n))

        def rounds(eng, s, body):
            if s.iters == 1:
                body(0)
            else:
                with eng.Fori(0, s.iters) as i:
                    body(i)

        def load_panels(sp, name):
            s = plan.stages[name]

            def body(i):
                for j, dmas in enumerate(s.panels):
                    n = s.panel0 + i * len(s.panels) + j
                    sp.wait_ge(sem("w_hi"), n - 1 + CREDIT)
                    sp.wait_ge(sem("w_lo"), n - 1 + CREDIT)
                    for nrow, first, shape, src in dmas:
                        k, cols, pitch = shape
                        if pitch:
                            dst = raw[0:nrow, s.slot[j], 0:k * pitch].rearrange("p (k n) -> p k n", n=pitch)
                            dst = dst[:, :, first:first + cols]
                        else:
                            dst = raw[0:nrow, s.slot[j], first:first + k * cols]
                            dst = dst.rearrange("p (k n) -> p k n", n=cols)
                        sp.dma_start(dst, src(i))\
                          .then_inc(sem(f"w_landed{s.slot[j]}"), 16)
            rounds(sp, s, body)

        def split_hi(act, slot, landed, n, free):
            act.wait_ge(sem(f"w_landed{slot}"), landed)
            act.wait_ge(sem("pe_segment"), free)
            nc.scalar.activation(wH[:, slot, :], raw[:, slot, :], ACT.Copy).then_inc(sem("w_hi"), 1)

        def next_hi(act, s, i, j):
            np_ = len(s.panels)
            n = s.panel0 + i * np_ + j + 1
            after = plan.order.index(s) + 1
            if j > 0:
                free = plan.used(s, i, j - 1)
            elif s.iters > 1:
                free = plan.used(s, i - 1, np_ - 1)
            elif after > 1:
                p = plan.order[after - 2]
                free = plan.used(p, p.iters - 1, len(p.panels) - 1)
            else:
                free = CREDIT_PE
            if j + 1 < np_:
                split_hi(act, s.slot[j + 1], plan.landed(s, i, j + 1), n, free)
            elif s.iters > 1 and not (isinstance(i, int) and i == s.iters - 1):
                split_hi(act, s.slot[0], plan.landed(s, i + 1, 0), n, free)
            elif after < len(plan.order):
                f = plan.order[after]
                split_hi(act, f.slot[0], plan.landed(f, 0, 0), n, free)

        def split_lo(pool, name):
            s = plan.stages[name]

            def body(i):
                for j in range(len(s.panels)):
                    n = s.panel0 + i * len(s.panels) + j
                    k = s.slot[j]
                    pool.wait_ge(sem("w_hi"), n + 1 + CREDIT)
                    nc.gpsimd.tensor_tensor(wL[:, k, :], raw[:, k, :], wH[:, k, :], ALU.subtract)\
                      .then_inc(sem("w_lo"), 1)
            rounds(pool, s, body)

        def dense_pe(pe, name):
            s = plan.stages[name]
            xh, xl = s.xs
            pe.wait_ge(sem(s.need[0]), s.need[1])
            for by, value in s.before.values():
                pe.wait_ge(sem("evac_" + by), value)

            def body(i):
                seen = -1
                for t, tile in enumerate(s.tiles):
                    acc = bank[tile["bank"]]
                    earlier = [u for u in range(t) if s.tiles[u]["bank"] == tile["bank"]]
                    later = [u for u in range(t, len(s.tiles)) if s.tiles[u]["bank"] == tile["bank"]]
                    if earlier:
                        pe.wait_ge(sem("evac_" + s.tiles[earlier[-1]]["by"]), plan.evac(s, i, earlier[-1]))
                    elif s.iters > 1:
                        pe.wait_ge(sem("evac_" + s.tiles[later[-1]]["by"]), plan.evac(s, i - 1, later[-1]))
                    terms = tile["terms"]
                    for q, (j, nrow, first, width, x) in enumerate(terms):
                        if j > seen:
                            pe.wait_ge(sem("w_lo"), s.panel0 + i * len(s.panels) + j + 1 + CREDIT)
                            seen = j
                        k = s.slot[j]
                        wh, wl = wH[0:nrow, k, first:first + width], wL[0:nrow, k, first:first + width]
                        a, z = q == 0, q == len(terms) - 1
                        if tile["token"]:
                            o = acc[0:tile["rows"], tile["at"]:tile["at"] + width]
                            xa, xb = xh[0:nrow, x, tile["x"]], xl[0:nrow, x, tile["x"]]
                            pe.matmul(o, xa, wh, start=a, stop=False)
                            pe.matmul(o, xa, wl, start=False, stop=False)
                            last = pe.matmul(o, xb, wh, start=False, stop=z)
                        else:
                            o = acc[0:width, 0:tile["cols"]]
                            xa, xb = xh[0:nrow, x, 0:tile["cols"]], xl[0:nrow, x, 0:tile["cols"]]
                            pe.matmul(o, wh, xa, start=a, stop=False)
                            pe.matmul(o, wh, xb, start=False, stop=False)
                            last = pe.matmul(o, wl, xa, start=False, stop=z)
                        if z or terms[q + 1][0] != j:
                            last.then_inc(sem("pe_segment"), 1)
            rounds(pe, s, body)

        def dense_act(act, name, evac):
            s = plan.stages[name]

            def body(i):
                for j in range(len(s.panels)):
                    next_hi(act, s, i, j)
                    for t, tile in enumerate(s.tiles):
                        if max(term[0] for term in tile["terms"]) == j:
                            evac(act, s, i, t)
            after = plan.order.index(s) + 1
            alike = after < len(plan.order) and plan.landed(plan.order[after], 0, 0) == plan.landed(s, s.iters, 0)
            if s.iters > 1 and not alike:
                with act.Fori(0, s.iters - 1) as i:
                    body(i)
                body(s.iters - 1)
            else:
                rounds(act, s, body)

        def dense_dve(dve, name, evac):
            s = plan.stages[name]

            def body(i):
                for t in range(len(s.tiles)):
                    evac(dve, s, i, t)
            rounds(dve, s, body)

        def nothing(eng, s, i, t):
            pass

        def act_fill(s, i, t):
            return ffn_index[s.name] * NF + 2 * i + (t - 2)

        def up_evac_act(act, s, i, t):
            if t < 2:
                act.wait_ge(sem("evac_dve"), plan.evac(s, i - 1, t + 2))
                act.wait_ge(sem("pe_segment"), plan.full(s, i, t))
                nc.scalar.activation(sg[:, t, :], bank[t][:], ACT.Silu).then_inc(sem("evac_act"), 1)
            else:
                act.wait_ge(sem("evac_dve"), plan.evac(s, i, t))
                nc.scalar.activation(gH[:, bass.ds(2 * i + t - 2, 1), :], prod[:, t - 2:t - 1, :], ACT.Copy)\
                  .then_inc(sem("act_hi"), 1)

        def up_evac_dve(dve, s, i, t):
            if t < 2:
                return
            dve.wait_ge(sem("pe_segment"), plan.full(s, i, t))
            dve.wait_ge(sem("evac_act"), plan.evac(s, i, t - 2))
            dve.wait_ge(sem("act_ready"), act_fill(s, i, 2) + CREDIT)
            nc.vector.tensor_tensor(prod[:, t - 2, :], bank[t][:], sg[:, t - 2, :], ALU.mult)\
              .then_inc(sem("evac_dve"), 1)
            if t == 3:
                for u in (2, 3):
                    dve.wait_ge(sem("act_hi"), act_fill(s, i, u) + 1)
                    nc.vector.tensor_tensor(gL[:, bass.ds(2 * i + u - 2, 1), :], prod[:, u - 2:u - 1, :],
                                            gH[:, bass.ds(2 * i + u - 2, 1), :], ALU.subtract)\
                      .then_inc(sem("act_ready"), 1)

        def residual(scale):
            def evac(dve, s, i, t):
                dve.wait_ge(sem("pe_segment"), plan.full(s, i, t))
                h = hT[:, bass.ds(len(s.tiles) * i + t, 1), :]
                b = bank[s.tiles[t]["bank"]][:].rearrange("p (o s) -> p o s", o=1)
                nc.vector.scalar_tensor_tensor(out=h, in0=b, scalar=scale, in1=h, op0=ALU.mult, op1=ALU.add)\
                  .then_inc(sem("evac_dve"), 1)
            return evac

        def norm_act(act, r, ready, split=True):
            for k in range(KD):
                act.wait_ge(*ready(k))
                if 8 * r + k >= 2:
                    act.wait_ge(sem("sq_summed"), 8 * r + k - 1)
                nc.scalar.activation(sq[:, k % 2, :], hT[:, k, :], ACT.Square).then_inc(sem("sq"), 1)
            act.wait_ge(sem("sq_summed"), 8 * r + 8)
            nc.scalar.activation(rstd[:], bank[7][:], ACT.Sqrt, bias=eps[:], scale=1.0 / D)\
              .then_inc(sem("rms"), 1)

        def norm_pe(pe, r):
            for k in range(KD):
                pe.wait_ge(sem("sq"), 8 * r + k + 1)
                pe.matmul(bank[7][:], ones[:], sq[:, k % 2, :], start=k == 0, stop=k == KD - 1)\
                  .then_inc(sem("sq_summed"), 1)

        def norm_dve(dve, r):
            dve.wait_ge(sem("rms"), r + 1)
            nc.vector.reciprocal(rstd[:], rstd[:]).then_inc(sem("rstd"), 1)
            dve.wait_ge(sem("rstd"), r + 1)

        def scaled_act(act, f, free=None):
            if free:
                act.wait_ge(sem("pe_segment"), free)
            for k in range(KD):
                act.wait_ge(sem("xn"), nfill(f) + k + 1)
                nc.scalar.activation(xH[:, k, :], xn[:, k % 2, :], ACT.Copy).then_inc(sem("x_hi"), 1)

        def scaled_dve(dve, f, gain, at=0):
            def norm(k):
                if k >= 2:
                    dve.wait_ge(sem("x_ready"), xbase(f) + k - 1)
                nc.vector.scalar_tensor_tensor(out=xn[:, k % 2, :], in0=hT[:, k, :], in1=rstd[:], op0=ALU.mult,
                                               scalar=column(gain, at + k), op1=ALU.mult).then_inc(sem("xn"), 1)
            norm(0)
            for k in range(KD):
                if k + 1 < KD:
                    norm(k + 1)
                dve.wait_ge(sem("x_hi"), xbase(f) + k + 1)
                nc.vector.tensor_tensor(xL[:, k, :], xn[:, k % 2, :], xH[:, k, :], ALU.subtract)\
                  .then_inc(sem("x_ready"), 1)

        def column(name, k=0):
            c = PAR_AT[name][0] + k
            return par[:, c:c + 1]

        def load_sp(sp):
            for name, (first, n) in PAR_AT.items():
                src = A[name]
                dims = " ".join("abcd"[:len(src.shape)])
                flat = src.rearrange(f"{dims} -> ({dims})") if len(src.shape) > 1 else src
                flat = flat.rearrange("(r c) -> r c", c=P)
                at = 0
                while at < n:
                    tile, row = divmod(first + at, P)
                    k = min(n - at, P - row)
                    sp.dma_start(stage[row:row + k, tile, :], flat[at:at + k]).then_inc(sem("par_staged"), 16)
                    at += k

        def constants_pool(pool):
            nc.gpsimd.memset(ident[:], 0.0).then_inc(sem("zeroed"), 1)
            nc.gpsimd.memset(ones[:], 1.0).then_inc(sem("const"), 1)
            nc.gpsimd.memset(eps[:], EPS).then_inc(sem("const"), 1)
            pool.wait_ge(sem("zeroed"), 1)
            nc.gpsimd.affine_select(out=ident[:], in_=ident[:], compare_op=ALU.not_equal, fill=1.0, base=0,
                                    pattern=[[-1, P]], channel_multiplier=1).then_inc(sem("const"), 1)

        NCONST = 3

        def turn(pe, o, i, k=P):
            return pe.transpose(o, i, ident[0:k, 0:k])

        def load_pe(pe):
            pe.wait_ge(sem("const"), NCONST)
            pe.wait_ge(sem("x_landed"), 16)
            for k in range(KD):
                if k >= 4:
                    pe.wait_ge(sem("h_act" if k % 2 == 0 else "h_dve"), (k - 4) // 2 + 1)
                for t in range(TT):
                    last = turn(pe, bank[4 + k % 4][:, t * P:(t + 1) * P], rows[:, t, k * P:(k + 1) * P])
                last.then_inc(sem("x_turned"), 1)
            pe.wait_ge(sem("par_staged"), 16 * NPAR_DMA)
            for t in range(NPT):
                k = min(P, NPAR - t * P)
                last = turn(pe, bank[t // 4][:, t % 4 * P:t % 4 * P + k], stage[0:k, t, :], k)
            last.then_inc(sem("par_turned"), 1)
            pe.wait_ge(sem("h_dve"), KD // 2)

        def load_act(act):
            act.sem_inc(sem("w_hi"), CREDIT)
            act.sem_inc(sem("evac_act"), CREDIT_EV)
            for k in range(0, KD, 2):
                act.wait_ge(sem("x_turned"), k + 1)
                nc.scalar.activation(hT[:, k, :], bank[4 + k % 4][:], ACT.Copy).then_inc(sem("h_act"), 1)

        def load_dve(dve):
            dve.sem_inc(sem("evac_dve"), CREDIT_EV)
            dve.sem_inc(sem("pe_segment"), CREDIT_PE)
            dve.sem_inc(sem("act_ready"), CREDIT)
            for k in range(1, KD, 2):
                dve.wait_ge(sem("x_turned"), k + 1)
                nc.vector.tensor_copy(hT[:, k, :], bank[4 + k % 4][:]).then_inc(sem("h_dve"), 1)
            dve.wait_ge(sem("par_turned"), 1)
            for t in range(0, NPT, 4):
                n = min(4 * P, NPAR - t * P)
                nc.vector.tensor_copy(par[:, t * P:t * P + n], bank[t // 4][:, 0:n]).then_inc(sem("par"), 1)
            dve.wait_ge(sem("par"), -(-NPT // 4))

        ab = region(13)[0:4].rearrange("p (r s) -> p r s", s=S)
        U = region(0, 14).rearrange("p (t s) -> p t s", s=S)
        B = region(0, 14).rearrange("p (r b c) -> p r b c", b=16, c=P)
        H4 = region(0, 14).rearrange("p (r h s) -> p r h s", h=4, s=S)
        Q, K, V, Z = 7, 8, 9, 6
        GBC, DEC, KB, NT, AT = 10, 11, 12, 13, 0
        T0, T1, YR, NM, VB = 1, 2, 3, 4, 5
        KBG, KDEC, UU, WT, OT, QD = 12, 11, 3, 4, 13, 10
        BETA, GC, EG, BG, DL, GL = range(6)
        HD = 128

        def constants2_pool(pool):
            nc.gpsimd.memset(ones64[:], 0.0).then_inc(sem("zeroed"), 1)
            nc.gpsimd.memset(lvl[:], 0.0).then_inc(sem("zeroed"), 1)
            nc.gpsimd.memset(pick[:], 1.0).then_inc(sem("zeroed"), 1)
            pool.wait_ge(sem("zeroed"), 4)
            for half in range(2):
                nc.gpsimd.memset(ones64[64 * half:64 * half + 64, 64 * half:64 * half + 64], 1.0)\
                  .then_inc(sem("const2"), 1)
                pool.wait_ge(sem("const2"), half + 1)
            nc.gpsimd.affine_select(out=pick[:], in_=pick[:], compare_op=ALU.is_equal, fill=0.0, base=0,
                                    pattern=[[-1, 4], [0, P]], channel_multiplier=1).then_inc(sem("const2"), 1)
            for n in range(7):
                w = 1 << n
                v = lvl[:, n, :].rearrange("p (b h r) -> p b h r", h=2, r=w)[:, :, 1, :]
                nb = P // (2 * w)
                nc.gpsimd.memset(v, 1.0).then_inc(sem("lvl"), 1)
                pool.wait_ge(sem("lvl"), 3 * n + 1)
                nc.gpsimd.affine_select(out=v, in_=v, compare_op=ALU.is_ge, fill=0.0, base=0,
                                        pattern=[[-2 * w, nb], [0, w]], channel_multiplier=1).then_inc(sem("lvl"), 1)
                pool.wait_ge(sem("lvl"), 3 * n + 2)
                nc.gpsimd.affine_select(out=v, in_=v, compare_op=ALU.is_ge, fill=0.0, base=w - 1,
                                        pattern=[[2 * w, nb], [0, w]], channel_multiplier=-1)\
                  .then_inc(sem("lvl"), 1)

        def ba_evac_act(act, s, i, t):
            if t == 0:
                act.wait_ge(sem("pe_segment"), plan.full(s, i, t))
                nc.scalar.activation(ab[:, 0, :], bank[0][0:4, :], ACT.Sigmoid).then_inc(sem("evac_act"), 1)
            else:
                act.wait_ge(sem("hv_landed"), 32)
                nc.scalar.activation(hv[:, 2:3], hv[:, 0:1], ACT.Exp).then_inc(sem("decay_act"), 1)
                act.wait_ge(sem("evac_dve"), plan.evac(s, i, t))
                nc.scalar.activation(ab[:, 2, :], ab[:, 1, :], ACT.Abs).then_inc(sem("decay_act"), 1)
                act.wait_ge(sem("decay_act"), 2)
                nc.scalar.activation(ab[:, 2, :], ab[:, 2, :], ACT.Exp, scale=-1.0).then_inc(sem("decay_act"), 1)
                act.wait_ge(sem("decay_act"), 3)
                nc.scalar.activation(ab[:, 2, :], ab[:, 2, :], ACT.Ln, bias=1.0).then_inc(sem("decay_act"), 1)

        def ba_evac_dve(dve, s, i, t):
            if t == 0:
                return
            dve.wait_ge(sem("pe_segment"), plan.full(s, i, t))
            dve.wait_ge(sem("hv_landed"), 32)
            nc.vector.tensor_scalar(ab[:, 1, :], bank[1][0:4, :], hv[:, 1:2], None, ALU.add)\
              .then_inc(sem("evac_dve"), 1)
            dve.wait_ge(sem("decay_act"), 1)
            nc.vector.tensor_scalar(hv[:, 3:4], hv[:, 2:3], -1.0, None, ALU.mult).then_inc(sem("decay_dve"), 1)
            dve.wait_ge(sem("decay_act"), 4)
            nc.vector.scalar_tensor_tensor(out=ab[:, 1, :], in0=ab[:, 1, :], scalar=0.0, in1=ab[:, 2, :],
                                           op0=ALU.max, op1=ALU.add).then_inc(sem("decay_dve"), 1)
            dve.wait_ge(sem("decay_dve"), 2)
            nc.vector.tensor_scalar(ab[:, 2, :], ab[:, 1, :], hv[:, 3:4], None, ALU.mult)\
              .then_inc(sem("decay_dve"), 1)
            dve.wait_ge(sem("decay_dve"), 3)
            for c in range(TT):
                nc.vector.tensor_tensor_scan(ab[:, 3, c * P:(c + 1) * P], ones[0:4, 0:P],
                                             ab[:, 2, c * P:(c + 1) * P], 0.0, ALU.mult, ALU.add)\
                  .then_inc(sem("decay_dve"), 1)

        DECAY = 3 + TT

        def in_evac(eng_name):
            def evac(eng, s, i, t):
                if s.tiles[t]["by"] != eng_name:
                    return
                eng.wait_ge(sem("pe_segment"), plan.full(s, i, t))
                o = U[:, bass.ds(4 * i + t, 1), :]
                b = bank[t][:].rearrange("p (o s) -> p o s", o=1)
                if eng_name == "act":
                    nc.scalar.activation(o, b, ACT.Copy).then_inc(sem("evac_act"), 1)
                else:
                    nc.vector.tensor_copy(o, b).then_inc(sem("evac_dve"), 1)
            return evac

        def stage_end(name):
            s = plan.stages[name]
            ends = {}
            for t, tile in enumerate(s.tiles):
                ends[tile["by"]] = plan.evac(s, s.iters - 1, t)
            return [(sem("evac_" + by), v) for by, v in ends.items()]

        def wait_all(eng, pairs):
            for p in pairs:
                eng.wait_ge(*p)

        def squares(act, n, src):
            if n >= 2:
                act.wait_ge(sem("sum_mix"), n - 1)
            nc.scalar.activation(sq[:, n % 2, :], src, ACT.Square).then_inc(sem("sq_mix"), 1)

        def sum_features(pe, n, b, weights):
            pe.wait_ge(sem("sq_mix"), n + 1)
            pe.matmul(b[:], weights[:], sq[:, n % 2, :], start=True, stop=True).then_inc(sem("sum_mix"), 1)

        def blocks(ap, n=4):
            return ap.rearrange("p (b c) -> p b c", b=n)

        def repeat(ap, n):
            return ap.unsqueeze(1).broadcast_to([P, n, P])

        OUTB = [0, 1, 6, 7]
        LEVELS = 7

        def gdn_act(act):
            wait_all(act, stage_end("mix_in"))
            for t in range(12):
                nc.scalar.activation(U[:, 28 + t, :], U[:, 12 + t, :], ACT.Copy,
                                     scale=column("gdn_conv_w", 36 + t)).then_inc(sem("qkv_tap"), 1)
                if t % 3 == 2:
                    c = t // 3
                    act.wait_ge(sem("sc_in"), c + 1)
                    nc.scalar.activation(U[:, 4 + c, :], U[:, 8 + c, :], ACT.Copy,
                                         scale=column("conv_short_w", 8 + c)).then_inc(sem("sc_tap"), 1)
            nc.scalar.activation(H4[:, Z], H4[:, Z], ACT.Silu).then_inc(sem("z_silu"), 1)
            for t in range(12):
                act.wait_ge(sem("qkv_conv"), 12 * (t // 4 + 1))
                nc.scalar.activation(U[:, 28 + t, :], U[:, 28 + t, :], ACT.Silu).then_inc(sem("qkv_silu"), 1)
            for t in range(8):
                act.wait_ge(sem("qkv_silu"), t + 1)
                squares(act, t, U[:, 28 + t, :])
            for t in range(4):
                act.wait_ge(sem("sc_y"), t + 1)
                squares(act, 8 + t, U[:, t, :])
                if t == 0:
                    for u in range(8):
                        act.wait_ge(sem("sum_mix"), u + 1)
                        nc.scalar.activation(U[:, 12 + u, :], bank[u][:], ACT.Sqrt, bias=eps[:], scale=1.0)\
                          .then_inc(sem("norm_mix"), 1)
            for t in range(4):
                act.wait_ge(sem("sum_mix"), 8 + t + 1)
                nc.scalar.activation(U[:, 4 + t, :], bank[t][:], ACT.Sqrt, bias=eps[:], scale=1.0 / 64)\
                  .then_inc(sem("norm_mix"), 1)
            for h in range(4):
                act.wait_ge(sem("gdn_sum"), h + 1)
                nc.scalar.activation(H4[:, GBC, h], bank[4 + h][:], ACT.Copy).then_inc(sem("gbc"), 1)
            act.wait_ge(sem("gdn_sum"), 9)
            nc.scalar.activation(col[:, BETA:GC + 1, :].rearrange("p a (h c) -> p a h c", h=4),
                                 bank[7][:, 0:32].rearrange("p (a c h) -> p a h c", a=2, c=4),
                                 ACT.Copy).then_inc(sem("cols"), 1)
            act.wait_ge(sem("cols"), 1)
            nc.scalar.activation(col[:, EG, :], col[:, GC, :], ACT.Exp).then_inc(sem("cols"), 1)
            act.wait_ge(sem("gbc"), 4)
            nc.scalar.activation(col[:, GL, :].rearrange("p (h c) -> p h c", h=4),
                                 H4[:, GBC].rearrange("p h (c s) -> p h c s", s=P)[:, :, :, P - 1],
                                 ACT.Exp).then_inc(sem("cols"), 1)
            act.wait_ge(sem("col_dl"), 1)
            nc.scalar.activation(col[:, DL, :], col[:, DL, :], ACT.Exp).then_inc(sem("cols"), 1)
            act.wait_ge(sem("dec_arg"), 16)
            nc.scalar.activation(B[:, DEC], B[:, DEC], ACT.Exp).then_inc(sem("dec_exp"), 1)
            act.wait_ge(sem("cols"), 4)
            nc.scalar.activation(H4[:, GBC], H4[:, GBC], ACT.Exp).then_inc(sem("gbc_exp"), 1)
            for t in range(4):
                act.wait_ge(sem("sc_out"), t + 1)
                nc.scalar.activation(xH[:, t, :], U[:, t, :], ACT.Copy).then_inc(sem("x_hi"), 1)
            act.wait_ge(sem("cols"), 4)
            for h in range(4):
                act.wait_ge(sem("v_turned"), h + 1)
                for c in range(4):
                    nc.scalar.activation(B[:, V, 4 * h + c], bank[7][:, c * P:(c + 1) * P], ACT.Copy,
                                         scale=col[:, BETA, 4 * h + c:4 * h + c + 1]).then_inc(sem("vb"), 1)
            for n in range(1, LEVELS):
                for g in range(4):
                    act.wait_ge(sem("y_sum"), 4 * n + g + 1)
                    nc.scalar.activation(B[:, YR, 4 * g:4 * g + 4], blocks(bank[g % 2][:]), ACT.Copy)\
                      .then_inc(sem("y"), 1)
            for h in range(4):
                act.wait_ge(sem("uw_sum"), 4 + h + 1)
                nc.scalar.activation(H4[:, WT, h], bank[4 + h][:], ACT.Copy).then_inc(sem("wt"), 1)
            for c in range(TT):
                act.wait_ge(sem("o_sum"), c + 1)
                nc.scalar.activation(H4[:, OT, :, c * P:(c + 1) * P], blocks(bank[2 + c % 2][:]), ACT.Copy)\
                  .then_inc(sem("o_mix"), 1)
            act.wait_ge(sem("o_mix"), 4)
            for h in range(4):
                squares(act, 12 + h, H4[:, OT, h])
            for h in range(4):
                act.wait_ge(sem("sum_mix"), 12 + h + 1)
                nc.scalar.activation(U[:, 20 + h, :], bank[OUTB[h]][:], ACT.Sqrt, bias=eps[:], scale=1.0 / HD)\
                  .then_inc(sem("norm_mix"), 1)
            for h in range(4):
                act.wait_ge(sem("gdn_out"), 4 + h + 1)
                nc.scalar.activation(xH[:, 4 + h, :], H4[:, OT, h], ACT.Copy).then_inc(sem("x_hi"), 1)

        def gdn_dve(dve):
            wait_all(dve, stage_end("mix_in"))
            for t in range(4):
                nc.vector.tensor_tensor(U[:, 8 + t, :], U[:, 4 + t, :], U[:, 8 + t, :], ALU.mult)\
                  .then_inc(sem("sc_in"), 1)
            n = 0
            for g in range(3):
                for tap in range(1, 4):
                    for t in range(4 * g, 4 * g + 4):
                        dve.wait_ge(sem("qkv_tap"), t + 1)
                        if tap > 1:
                            dve.wait_ge(sem("qkv_conv"), n - 3)
                        nc.vector.scalar_tensor_tensor(
                            out=U[:, 28 + t, tap:], in0=U[:, 12 + t, :S - tap],
                            scalar=column("gdn_conv_w", 12 * (3 - tap) + t), in1=U[:, 28 + t, tap:],
                            op0=ALU.mult, op1=ALU.add).then_inc(sem("qkv_conv"), 1)
                        n += 1
            for tap in range(1, 3):
                for t in range(4):
                    dve.wait_ge(sem("sc_tap"), t + 1)
                    if tap > 1:
                        dve.wait_ge(sem("sc_conv"), t + 1)
                    nc.vector.scalar_tensor_tensor(
                        out=U[:, 4 + t, tap:], in0=U[:, 8 + t, :S - tap],
                        scalar=column("conv_short_w", 4 * (2 - tap) + t), in1=U[:, 4 + t, tap:],
                        op0=ALU.mult, op1=ALU.add).then_inc(sem("sc_conv"), 1)
            for t in range(4):
                dve.wait_ge(sem("sc_conv"), 4 + t + 1)
                nc.vector.tensor_tensor(U[:, t, :], U[:, t, :], U[:, 4 + t, :], ALU.mult).then_inc(sem("sc_y"), 1)
            for t in range(8):
                dve.wait_ge(sem("norm_mix"), t + 1)
                nc.vector.reciprocal(U[:, 12 + t, :], U[:, 12 + t, :]).then_inc(sem("inv_mix"), 1)
            for t in range(8):
                dve.wait_ge(sem("inv_mix"), t + 1)
                nc.vector.scalar_tensor_tensor(out=U[:, 28 + t, :], in0=U[:, 28 + t, :],
                                               scalar=HD ** -0.5 if t < 4 else 1.0, in1=U[:, 12 + t, :],
                                               op0=ALU.mult, op1=ALU.mult).then_inc(sem("qk_unit"), 1)
            for h in range(4):
                dve.wait_ge(sem("gdn_sum"), 4 + h + 1)
                dve.wait_ge(sem("qk_unit"), 4 + h + 1)
                nc.vector.tensor_tensor(H4[:, KB, h], H4[:, K, h], bank[h][:], ALU.mult).then_inc(sem("kb"), 1)
            dve.wait_ge(sem("gbc"), 4)
            dve.wait_ge(sem("cols"), 1)
            nc.vector.tensor_tensor(col[:, DL, :].rearrange("p (h c) -> p h c", h=4),
                                    H4[:, GBC].rearrange("p h (c s) -> p h c s", s=P)[:, :, :, P - 1],
                                    col[:, GC, :].rearrange("p (h c) -> p h c", h=4), ALU.subtract)\
              .then_inc(sem("col_dl"), 1)
            for b in range(16):
                nc.vector.tensor_scalar(B[:, DEC, b], B[:, GBC, b], col[:, GC, b:b + 1], 0.0,
                                        ALU.subtract, ALU.min).then_inc(sem("dec_arg"), 1)
            dve.wait_ge(sem("cols"), 2)
            nc.vector.tensor_tensor(col[:, BG, :], col[:, BETA, :], col[:, EG, :], ALU.mult)\
              .then_inc(sem("col_bg"), 1)
            for t in range(4):
                dve.wait_ge(sem("norm_mix"), 8 + t + 1)
                nc.vector.reciprocal(U[:, 4 + t, :], U[:, 4 + t, :]).then_inc(sem("inv_mix"), 1)
            for t in range(4):
                dve.wait_ge(sem("inv_mix"), 8 + t + 1)
                nc.vector.scalar_tensor_tensor(out=U[:, t, :], in0=U[:, t, :], scalar=column("conv_out_norm", t),
                                               in1=U[:, 4 + t, :], op0=ALU.mult, op1=ALU.mult)\
                  .then_inc(sem("sc_out"), 1)
            for t in range(4):
                dve.wait_ge(sem("x_hi"), xbase(2) + t + 1)
                nc.vector.tensor_tensor(xL[:, t, :], U[:, t, :], xH[:, t, :], ALU.subtract)\
                  .then_inc(sem("x_ready"), 1)
            dve.wait_ge(sem("dec"), 1)
            for h in range(4):
                dve.wait_ge(sem("gdn_sum"), 9 + h + 1)
                nc.vector.tensor_tensor(H4[:, NT, h], bank[h][:], H4[:, DEC, h], ALU.mult).then_inc(sem("nt"), 1)
            dve.wait_ge(sem("x_ready"), xbase(2) + 4)
            for h in range(4):
                dve.wait_ge(sem("gdn_sum"), 13 + h + 1)
                nc.vector.tensor_tensor(H4[:, AT, h], bank[4 + h][:], H4[:, DEC, h], ALU.mult).then_inc(sem("at"), 1)
            dve.wait_ge(sem("gbc_exp"), 1)
            nc.vector.tensor_tensor(H4[:, QD], H4[:, Q], H4[:, QD], ALU.mult).then_inc(sem("qd"), 1)
            dve.wait_ge(sem("at"), 4)
            dve.wait_ge(sem("cols"), 4)
            dve.wait_ge(sem("col_bg"), 1)
            for h in range(4):
                dve.wait_ge(sem("k_turned"), h + 1)
                for c in range(4):
                    b = 4 * h + c
                    nc.vector.tensor_scalar(B[:, KBG, b], bank[6][:, c * P:(c + 1) * P], col[:, BG, b:b + 1],
                                            None, ALU.mult)
                    nc.vector.tensor_scalar(B[:, KDEC, b], bank[6][:, c * P:(c + 1) * P], col[:, DL, b:b + 1],
                                            None, ALU.mult).then_inc(sem("kdec"), 1)
            for g in range(4):
                dve.wait_ge(sem("y_sum"), g + 1)
                nc.vector.scalar_tensor_tensor(out=B[:, T0, 4 * g:4 * g + 4], in0=blocks(bank[g % 2][:]), scalar=-1.0,
                                               in1=repeat(ident[:], 4), op0=ALU.mult, op1=ALU.add)\
                  .then_inc(sem("t_new"), 1)
                nc.vector.scalar_tensor_tensor(out=B[:, T1, 4 * g:4 * g + 4], in0=B[:, NM, 4 * g:4 * g + 4],
                                               scalar=-1.0, in1=repeat(ident[:], 4), op0=ALU.mult, op1=ALU.add)\
                  .then_inc(sem("tt_new"), 1)
            for n in range(1, LEVELS):
                for g in range(4):
                    if n < LEVELS - 1:
                        dve.wait_ge(sem("ty_sum"), 4 * (n - 1) + g + 1)
                        o = B[:, T0, 4 * g:4 * g + 4]
                        nc.vector.tensor_tensor(o, o, blocks(bank[2 + g % 2][:]), ALU.subtract)\
                          .then_inc(sem("t_new"), 1)
                    dve.wait_ge(sem("yt_sum"), 4 * (n - 1) + g + 1)
                    o = B[:, T1, 4 * g:4 * g + 4]
                    nc.vector.tensor_tensor(o, o, blocks(bank[4 + g % 2][:]), ALU.subtract)\
                      .then_inc(sem("tt_new"), 1)
            for h in range(4):
                dve.wait_ge(sem("uw_sum"), h + 1)
                nc.vector.tensor_copy(H4[:, UU, h], bank[h][:]).then_inc(sem("uu"), 1)
            VN, ST = H4[:, T0], H4[:, T1]
            dve.wait_ge(sem("uw_sum"), 8)
            for c in range(TT):
                u = B[:, UU, c:16:4]
                if c == 0:
                    dve.wait_ge(sem("uu"), 4)
                    nc.vector.tensor_copy(blocks(VN[:, 0]), u).then_inc(sem("vn"), 1)
                else:
                    dve.wait_ge(sem("ws_sum"), c)
                    nc.vector.tensor_tensor(blocks(VN[:, c % 2]), u, blocks(bank[c % 2][:]), ALU.subtract)\
                      .then_inc(sem("vn"), 1)
                if c == TT - 1:
                    break
                dve.wait_ge(sem("kv_sum"), c + 1)
                for h in range(4):
                    o, b = ST[:, c % 2, h * P:(h + 1) * P], bank[4 + c % 2][:, h * P:(h + 1) * P]
                    if c == 0:
                        nc.vector.tensor_copy(o, b).then_inc(sem("state"), 1)
                    else:
                        if h == 0:
                            dve.wait_ge(sem("state"), 4 * c)
                        nc.vector.scalar_tensor_tensor(out=o, in0=ST[:, (c - 1) % 2, h * P:(h + 1) * P],
                                                       scalar=col[:, GL, 4 * h + c:4 * h + c + 1], in1=b,
                                                       op0=ALU.mult, op1=ALU.add).then_inc(sem("state"), 1)
            for h in range(4):
                dve.wait_ge(sem("norm_mix"), 12 + h + 1)
                nc.vector.reciprocal(U[:, 20 + h, :], U[:, 20 + h, :]).then_inc(sem("inv_mix"), 1)
            for h in range(4):
                dve.wait_ge(sem("inv_mix"), 12 + h + 1)
                nc.vector.scalar_tensor_tensor(out=H4[:, OT, h], in0=H4[:, OT, h], scalar=column("gdn_out_norm"),
                                               in1=U[:, 20 + h, :], op0=ALU.mult, op1=ALU.mult)\
                  .then_inc(sem("gdn_out"), 1)
            dve.wait_ge(sem("z_silu"), 1)
            for h in range(4):
                dve.wait_ge(sem("gdn_out"), h + 1)
                nc.vector.tensor_tensor(H4[:, OT, h], H4[:, OT, h], H4[:, Z, h], ALU.mult).then_inc(sem("gdn_out"), 1)
            for h in range(4):
                dve.wait_ge(sem("x_hi"), xbase(2) + 4 + h + 1)
                nc.vector.tensor_tensor(xL[:, 4 + h, :], H4[:, OT, h], xH[:, 4 + h, :], ALU.subtract)\
                  .then_inc(sem("x_ready"), 1)

        def gdn_pool(pool):
            pool.wait_ge(sem("dec_exp"), 1)
            nc.gpsimd.affine_select(out=B[:, DEC], in_=B[:, DEC], compare_op=ALU.is_ge, fill=0.0, base=0,
                                    pattern=[[0, 16], [1, P]], channel_multiplier=-1).then_inc(sem("dec"), 1)
            pool.wait_ge(sem("nt"), 4)
            for n in range(LEVELS):
                if n >= 2:
                    pool.wait_ge(sem("y_sum"), 4 * (n - 1))
                    pool.wait_ge(sem("tt_new"), 4)
                nc.gpsimd.tensor_tensor(B[:, NM + n % 2], B[:, NT], repeat(lvl[:, n, :], 16), ALU.mult)\
                  .then_inc(sem("nm"), 1)

        def gdn_pe(pe):
            wait_all(pe, stage_end("mix_in"))
            pe.wait_ge(sem("const2"), 3)
            for t in range(8):
                sum_features(pe, t, bank[t], ones)
            for t in range(4):
                pe.wait_ge(sem("norm_mix"), t + 1)
                sum_features(pe, 8 + t, bank[t], ones64)
            pe.wait_ge(sem("decay_dve"), DECAY)
            pe.wait_ge(sem("evac_act"), plan.evac(plan.stages["mix_ba"], 0, 0))
            for h in range(4):
                pe.wait_ge(sem("norm_mix"), 4 + h + 1)
                pe.matmul(bank[4 + h][:], pick[:, h, :], ab[:, 3, :], start=True, stop=True)\
                  .then_inc(sem("gdn_sum"), 1)
            for h in range(4):
                pe.wait_ge(sem("norm_mix"), 8 + h + 1)
                pe.matmul(bank[h][:], pick[:, h, :], ab[:, 0, :], start=True, stop=True)\
                  .then_inc(sem("gdn_sum"), 1)
            pe.wait_ge(sem("gbc"), 4)
            for a, row in ((0, 0), (1, 3)):
                for c in range(TT):
                    last = turn(pe, bank[7][:, 16 * a + 4 * c:16 * a + 4 * c + 4], ab[:, row, c * P:(c + 1) * P], 4)
            last.then_inc(sem("gdn_sum"), 1)
            pe.wait_ge(sem("kb"), 4)
            for h in range(4):
                for c in range(TT):
                    x = slice(c * P, (c + 1) * P)
                    last = pe.matmul(bank[h][:, x], H4[:, K, h, x], H4[:, KB, h, x], start=True, stop=True)
                last.then_inc(sem("gdn_sum"), 1)
            pe.wait_ge(sem("cols"), 1)
            for h in range(4):
                for c in range(TT):
                    x = slice(c * P, (c + 1) * P)
                    last = pe.matmul(bank[4 + h][:, x], H4[:, K, h, x], H4[:, Q, h, x], start=True, stop=True)
                last.then_inc(sem("gdn_sum"), 1)
            pe.wait_ge(sem("at"), 4)
            pe.wait_ge(sem("qkv_silu"), 12)
            for h in range(4):
                if h:
                    pe.wait_ge(sem("kdec"), 4 * h)
                for c in range(TT):
                    last = turn(pe, bank[6][:, c * P:(c + 1) * P], H4[:, K, h, c * P:(c + 1) * P])
                last.then_inc(sem("k_turned"), 1)
                if h:
                    pe.wait_ge(sem("vb"), 4 * h)
                for c in range(TT):
                    last = turn(pe, bank[7][:, c * P:(c + 1) * P], H4[:, V, h, c * P:(c + 1) * P])
                last.then_inc(sem("v_turned"), 1)
            for g in range(4):
                pe.wait_ge(sem("nm"), 1)
                if g >= 2:
                    pe.wait_ge(sem("t_new"), g - 1)
                for b in range(4):
                    last = pe.matmul(bank[g % 2][:, b * P:(b + 1) * P], B[:, NM, 4 * g + b], ident[:],
                                     start=True, stop=True)
                last.then_inc(sem("y_sum"), 1)
            for n in range(1, LEVELS):
                pe.wait_ge(sem("nm"), n + 1)
                for g in range(4):
                    pe.wait_ge(sem("t_new"), 4 * (n - 1) + g + 1)
                    if g >= 2:
                        pe.wait_ge(sem("y"), 4 * (n - 1) + g - 1)
                    elif n == 1:
                        pe.wait_ge(sem("t_new"), 4)
                    for b in range(4):
                        last = pe.matmul(bank[g % 2][:, b * P:(b + 1) * P], B[:, NM + n % 2, 4 * g + b],
                                         B[:, T0, 4 * g + b], start=True, stop=True)
                    last.then_inc(sem("y_sum"), 1)
                for g in range(4):
                    pe.wait_ge(sem("y"), 4 * (n - 1) + g + 1)
                    pe.wait_ge(sem("tt_new"), 4 * (n - 1) + g + 1)
                    if n < LEVELS - 1:
                        pe.wait_ge(sem("t_new"), 4 * n + g - 1)
                        for b in range(4):
                            last = pe.matmul(bank[2 + g % 2][:, b * P:(b + 1) * P], B[:, T1, 4 * g + b],
                                             B[:, YR, 4 * g + b], start=True, stop=True)
                        last.then_inc(sem("ty_sum"), 1)
                    pe.wait_ge(sem("tt_new"), 4 * n + g - 1)
                    for b in range(4):
                        last = pe.matmul(bank[4 + g % 2][:, b * P:(b + 1) * P], B[:, YR, 4 * g + b],
                                         B[:, T1, 4 * g + b], start=True, stop=True)
                    last.then_inc(sem("yt_sum"), 1)
            pe.wait_ge(sem("vb"), 16)
            pe.wait_ge(sem("y"), 4 * (LEVELS - 1))
            pe.wait_ge(sem("tt_new"), 4 * LEVELS)
            pe.wait_ge(sem("kdec"), 16)
            for h in range(4):
                for c in range(TT):
                    last = pe.matmul(bank[h][:, c * P:(c + 1) * P], B[:, T1, 4 * h + c], B[:, V, 4 * h + c],
                                     start=True, stop=True)
                last.then_inc(sem("uw_sum"), 1)
            for h in range(4):
                for c in range(TT):
                    last = pe.matmul(bank[4 + h][:, c * P:(c + 1) * P], B[:, KBG, 4 * h + c], B[:, T1, 4 * h + c],
                                     start=True, stop=True)
                last.then_inc(sem("uw_sum"), 1)
            VN, ST = H4[:, T0], H4[:, T1]
            pe.wait_ge(sem("qd"), 1)
            pe.wait_ge(sem("uu"), 4)
            pe.wait_ge(sem("wt"), 4)
            for c in range(TT):
                if c:
                    pe.wait_ge(sem("state"), 4 * c)
                    if c >= 3:
                        pe.wait_ge(sem("vn"), c - 1)
                    for h in range(4):
                        last = pe.matmul(bank[c % 2][:, h * P:(h + 1) * P], B[:, WT, 4 * h + c],
                                         ST[:, (c - 1) % 2, h * P:(h + 1) * P], start=True, stop=True)
                    last.then_inc(sem("ws_sum"), 1)
                pe.wait_ge(sem("vn"), c + 1)
                if c < TT - 1:
                    for h in range(4):
                        last = pe.matmul(bank[4 + c % 2][:, h * P:(h + 1) * P], B[:, KDEC, 4 * h + c],
                                         VN[:, c % 2, h * P:(h + 1) * P], start=True, stop=True)
                    last.then_inc(sem("kv_sum"), 1)
                if c >= 2:
                    pe.wait_ge(sem("o_mix"), c - 1)
                for h in range(4):
                    o = bank[2 + c % 2][:, h * P:(h + 1) * P]
                    if c:
                        pe.matmul(o, ST[:, (c - 1) % 2, h * P:(h + 1) * P], B[:, QD, 4 * h + c],
                                  start=True, stop=False)
                    last = pe.matmul(o, VN[:, c % 2, h * P:(h + 1) * P], B[:, AT, 4 * h + c], start=c == 0, stop=True)
                last.then_inc(sem("o_sum"), 1)
            for h in range(4):
                sum_features(pe, 12 + h, bank[OUTB[h]], ones)


        def final_dve(dve):
            for k in range(KD):
                nc.vector.scalar_tensor_tensor(out=hT[:, k, :], in0=hT[:, k, :], scalar=column("final_norm", k),
                                               in1=rstd[:], op0=ALU.mult, op1=ALU.mult).then_inc(sem("h_final"), 1)
            dve.wait_ge(sem("h_final"), KD)

        memT = region(7).rearrange("p (k m) -> p k m", m=M)
        mem_rows = region(9).rearrange("p (t c) -> p t c", c=D)
        mem_sq = region(11).rearrange("p (k m) -> p k m", m=M)
        mem_rstd = region(12)[:, 0:M]
        memK = region(6)[:, 1024:1536].rearrange("p (j m) -> p j m", m=M)
        memV = region(6)[:, 1536:2048].rearrange("p (t c) -> p t c", c=M)
        memQ = region(6)[:, 0:1024].rearrange("p (j s) -> p j s", s=S)

        def mem_load(sp, l, after):
            sp.wait_ge(*after)
            sp.dma_start(mem_rows, A["mem_2"][0].rearrange("(t p) c -> p t c", p=P))\
              .then_inc(sem("mem_landed"), 16)

        def mem_pe(pe, l):
            pe.wait_ge(sem("mem_landed"), 16 * (l + 1))
            for b in range(4):
                for u in range(4):
                    k, t = 2 * b + u // 2, u % 2
                    last = turn(pe, bank[b][:, u * P:(u + 1) * P], mem_rows[:, t, k * P:(k + 1) * P])
                last.then_inc(sem("mem_pe"), 1)
            pe.wait_ge(sem("mem_act"), 7 * l + 5)
            for k in range(KD):
                last = pe.matmul(bank[4][:, 0:M], ones[:], mem_sq[:, k, :], start=k == 0, stop=k == KD - 1)
            last.then_inc(sem("mem_pe"), 1)

        def mem_act(act, l):
            for b in range(4):
                act.wait_ge(sem("mem_pe"), 5 * l + b + 1)
                nc.scalar.activation(memT[:, 2 * b:2 * b + 2, :], bank[b][:].rearrange("p (k m) -> p k m", m=M),
                                     ACT.Copy).then_inc(sem("mem_act"), 1)
            act.wait_ge(sem("mem_act"), 7 * l + 4)
            nc.scalar.activation(mem_sq[:], memT[:], ACT.Square).then_inc(sem("mem_act"), 1)
            act.wait_ge(sem("mem_pe"), 5 * l + 5)
            nc.scalar.activation(mem_rstd, bank[4][:, 0:M], ACT.Sqrt, bias=eps[:], scale=1.0 / D)\
              .then_inc(sem("mem_act"), 1)
            act.wait_ge(sem("mem_dve"), 9 * (l + 1))
            nc.scalar.activation(memH[:], mem_sq[:], ACT.Copy).then_inc(sem("mem_act"), 1)

        def mem_dve(dve, l):
            dve.wait_ge(sem("mem_act"), 7 * l + 6)
            nc.vector.reciprocal(mem_rstd, mem_rstd).then_inc(sem("mem_dve"), 1)
            dve.wait_ge(sem("mem_dve"), 9 * l + 1)
            for k in range(KD):
                nc.vector.scalar_tensor_tensor(out=mem_sq[:, k, :], in0=memT[:, k, :],
                                               scalar=column("norm_mem_2", KD * l + k), in1=mem_rstd,
                                               op0=ALU.mult, op1=ALU.mult).then_inc(sem("mem_dve"), 1)
            dve.wait_ge(sem("mem_act"), 7 * l + 7)
            nc.vector.tensor_tensor(memL[:], mem_sq[:], memH[:], ALU.subtract).then_inc(sem("mem_ready"), 1)

        def copy_out(eng, by, dst, src, scale=1.0):
            if by == "act":
                nc.scalar.activation(dst, src, ACT.Copy, scale=scale).then_inc(sem("evac_act"), 1)
            elif scale == 1.0:
                nc.vector.tensor_copy(dst, src).then_inc(sem("evac_dve"), 1)
            else:
                nc.vector.tensor_scalar(dst, src, scale, None, ALU.mult).then_inc(sem("evac_dve"), 1)

        def evac_to(by, place):
            def evac(eng, s, i, t):
                if s.tiles[t]["by"] != by:
                    return
                eng.wait_ge(sem("pe_segment"), plan.full(s, i, t))
                dst, nrow, ncol, scale = place(i, t)
                src = bank[s.tiles[t]["bank"]][0:nrow, 0:ncol]
                if len(dst.shape) == 3:
                    src = src.rearrange("p (o s) -> p o s", o=1)
                copy_out(eng, by, dst, src, scale)
            return evac

        def mem_place(i, t):
            return (memK[:, t, :], P, M, 1.0) if t < 2 else (memV[:, t - 2, :], P, M, 1.0)

        mem_p = region(10).rearrange("p (u m) -> p u m", m=M)
        mem_pt = region(11).rearrange("p (u s) -> p u s", s=S)
        diag = region(7).rearrange("p (u c) -> p u c", c=P)
        mstat = sb("mstat", [P, 2, 3, 4])
        NROUND = 4

        def mem_attn_pe(pe, l, first_wait):
            wait_all(pe, first_wait)
            for r in range(NROUND + 2):
                if r < NROUND:
                    j, tp = divmod(r, 2)
                    n = NROUND * l + r
                    for half in range(2):
                        if n:
                            pe.wait_ge(sem("m_exp"), 4 * n)
                        f = slice(64 * half, 64 * half + 64)
                        for t in range(2):
                            at = (2 * tp + t) * P
                            last = pe.matmul(bank[4 + half][:, t * M:(t + 1) * M], memQ[f, j, at:at + P],
                                             memK[f, j, :], start=True, stop=True)
                        last.then_inc(sem("m_scores"), 1)
                if 1 <= r <= NROUND:
                    q = r - 1
                    n = NROUND * l + q
                    pe.wait_ge(sem("m_diag"), 4 * n + 4)
                    for half in range(2):
                        if n:
                            pe.wait_ge(sem("m_pt"), 2 * (n - 1) + half + 1)
                        for t in range(2):
                            for k in range(2):
                                u = 2 * t + k
                                last = pe.matmul(bank[6 + half][:, u * P:(u + 1) * P],
                                                 mem_p[:, 4 * (q % 2) + 2 * half + t, k * P:(k + 1) * P],
                                                 diag[:, 4 * (q % 2) + 2 * half + t, :], start=True, stop=True)
                        last.then_inc(sem("m_turned"), 1)
                if r >= 2:
                    q = r - 2
                    j, tp = divmod(q, 2)
                    n = NROUND * l + q
                    pe.wait_ge(sem("m_pt"), 2 * n + 2)
                    for half in range(2):
                        for t in range(2):
                            at = (2 * tp + t) * P
                            for k in range(2):
                                c = 64 * (2 * j + half)
                                last = pe.matmul(bank[2 + j][64 * half:64 * half + 64, at:at + P],
                                                 memV[:, k, c:c + 64],
                                                 mem_pt[:, 2 * (q % 2) + half, (2 * t + k) * P:(2 * t + k + 1) * P],
                                                 start=k == 0, stop=k == 1)
                    last.then_inc(sem("m_out"), 1)

        def mem_attn_act(act, l, f, x0):
            for r in range(NROUND + 1):
                if r < NROUND:
                    n = NROUND * l + r
                    for half in range(2):
                        act.wait_ge(sem("m_max"), 2 * n + half + 1)
                        if n >= 2:
                            act.wait_ge(sem("m_turned"), 2 * (n - 1))
                        for t in range(2):
                            u = 2 * half + t
                            nc.scalar.activation(mem_p[:, 4 * (r % 2) + u, :], bank[4 + half][:, t * M:(t + 1) * M],
                                                 ACT.Exp, bias=mstat[:, r % 2, 0, u:u + 1], scale=0.125,
                                                 accum_out=mstat[:, r % 2, 1, u:u + 1]).then_inc(sem("m_exp"), 1)
                if r >= 1:
                    q = r - 1
                    n = NROUND * l + q
                    for half in range(2):
                        act.wait_ge(sem("m_turned"), 2 * n + half + 1)
                        if n >= 2:
                            act.wait_ge(sem("m_out"), n - 1)
                        nc.scalar.activation(mem_pt[:, 2 * (q % 2) + half, :], bank[6 + half][:], ACT.Copy)\
                          .then_inc(sem("m_pt"), 1)
            for j in range(2):
                act.wait_ge(sem("m_out"), NROUND * l + 2 * j + 2)
                nc.scalar.activation(xH[:, x0 + j, :], bank[2 + j][:], ACT.Copy).then_inc(sem("x_hi"), 1)

        def mem_attn_dve(dve, l, f, x0, base):
            for r in range(NROUND):
                n = NROUND * l + r
                st = mstat[:, r % 2]
                for half in range(2):
                    dve.wait_ge(sem("m_scores"), 2 * n + half + 1)
                    if n >= 2:
                        dve.wait_ge(sem("m_exp"), 4 * (n - 1))
                    nc.vector.tensor_reduce(st[:, 0, 2 * half:2 * half + 2],
                                            bank[4 + half][:].rearrange("p (t m) -> p t m", m=M), AX, ALU.max)\
                      .then_inc(sem("m_raw"), 1)
                    dve.wait_ge(sem("m_raw"), 2 * n + half + 1)
                    nc.vector.tensor_scalar(st[:, 0, 2 * half:2 * half + 2], st[:, 0, 2 * half:2 * half + 2],
                                            -0.125, None, ALU.mult).then_inc(sem("m_max"), 1)
                dve.wait_ge(sem("m_exp"), 4 * n + 4)
                nc.vector.reciprocal(st[:, 2, :], st[:, 1, :]).then_inc(sem("m_inv"), 1)
                dve.wait_ge(sem("m_inv"), n + 1)
                if n >= 2:
                    dve.wait_ge(sem("m_turned"), 2 * (n - 1))
                for u in range(4):
                    nc.vector.tensor_scalar(diag[:, 4 * (r % 2) + u, :], ident[:], st[:, 2, u:u + 1], None,
                                            ALU.mult).then_inc(sem("m_diag"), 1)
            for j in range(2):
                dve.wait_ge(sem("x_hi"), base + j + 1)
                nc.vector.tensor_tensor(xL[:, x0 + j, :], bank[2 + j][:], xH[:, x0 + j, :], ALU.subtract)\
                  .then_inc(sem("x_ready"), 1)

        p96 = sb("p96", [96, 6])
        gate_up = sb("gate_up", [16, 384])
        GDK, GDV, NH = 96, 192, 4
        gq = region(0)[0:GDK].rearrange("p (h s) -> p h s", s=S)
        gk = region(1)[0:GDK].rearrange("p (h s) -> p h s", s=S)
        gg = region(2, 2)[0:96].rearrange("p (t s) -> p t s", s=S)
        gv = region(4, 2)[:, 0:3072].rearrange("p (t c) -> p t c", c=768)
        lr = region(5)[0:16, 1024:1536]
        gb = region(9)[0:GDK]
        gx = region(10)[0:GDK]
        gw = region(11)[0:GDK]
        gl2 = region(12)[0:GDK]
        AD = region(12).rearrange("p (b c) -> p b c", c=P)
        A256 = region(13).rearrange("p (h k s) -> p h k s", h=NH, k=2)
        A128 = region(8)[:, 0:1024].rearrange("p (b c) -> p b c", c=P)
        go = region(0, 2)[0:96].rearrange("p (t s) -> p t s", s=S)
        gn = region(9)[0:96].rearrange("p (h s) -> p h s", s=S)
        WIDTHS = [256, 128, 64, 32, 16, 8, 4, 2, 1]

        def v_place(i, t):
            j, tile = divmod(t, TT)
            return (gv[:, tile, 256 * j:256 * j + 256], P, 256, 1.0)

        def rest_place(i, t):
            return (lr, 16, S, 1.0) if t == 0 else (memQ[:, t - 1, :], P, S, 1.0)

        def gate_pe(pe):
            pe.wait_ge(*stage_end("gla_rest")[0])
            pe.wait_ge(sem("gate_landed"), 16 * 7)
            for h in range(NH):
                pe.matmul(bank[4 + h][0:GDK, :], gate_up[:, GDK * h:GDK * (h + 1)], lr, start=True, stop=True)\
                  .then_inc(sem("gate_sum"), 1)

        def gate_dve(dve):
            dve.wait_ge(sem("gate_landed"), 16 * 7)
            for h in range(NH):
                dve.wait_ge(sem("gate_sum"), h + 1)
                nc.vector.tensor_scalar(gb[:, h * S:(h + 1) * S], bank[4 + h][0:GDK, :], p96[:, 2 + h:3 + h], None,
                                        ALU.add).then_inc(sem("gate_dve"), 1)
            dve.wait_ge(sem("gate_act"), 3)
            nc.vector.scalar_tensor_tensor(out=gx, in0=gb, scalar=0.0, in1=gx, op0=ALU.min, op1=ALU.subtract)\
              .then_inc(sem("gate_dve"), 1)
            dve.wait_ge(sem("gate_dve"), NH + 1)
            for h in range(NH):
                nc.vector.tensor_tensor_scan(gb[:, h * S:(h + 1) * S],
                                             ones[0:GDK, 0:1].broadcast_to([GDK, S]),
                                             gx[:, h * S:(h + 1) * S], 0.0, ALU.mult, ALU.add)\
                  .then_inc(sem("gate_dve"), 1)
            dve.wait_ge(sem("gate_dve"), 2 * NH + 1)

        def gate_act(act):
            act.wait_ge(sem("gate_dve"), NH)
            nc.scalar.activation(gx, gb, ACT.Abs).then_inc(sem("gate_act"), 1)
            act.wait_ge(sem("gate_act"), 1)
            nc.scalar.activation(gx, gx, ACT.Exp, scale=-1.0).then_inc(sem("gate_act"), 1)
            act.wait_ge(sem("gate_act"), 2)
            nc.scalar.activation(gx, gx, ACT.Ln, bias=1.0).then_inc(sem("gate_act"), 1)

        def halves(ap, w):
            v = ap.rearrange("p (b h r) -> p b h r", h=2, r=w)
            return v[:, :, 0, :], v[:, :, 1, :]

        def gla_dve(dve):
            wait_all(dve, stage_end("gla_k") + stage_end("gla_q"))
            for n, w in enumerate(WIDTHS):
                nb = NH * S // (2 * w)
                b0, b1 = halves(gb, w)
                x0, x1 = halves(gx, w)
                ref = b0[:, :, w - 1:w].broadcast_to([GDK, nb, w])
                if n:
                    dve.wait_ge(sem("lvl_w"), 2 * n)
                nc.vector.tensor_tensor(x1, b1, ref, ALU.subtract).then_inc(sem("lvl_x"), 1)
                nc.vector.tensor_tensor(x0, ref, b0, ALU.subtract).then_inc(sem("lvl_x"), 1)
                dve.wait_ge(sem("lvl_exp"), n + 1)
                if n:
                    dve.wait_ge(sem("a_sum"), A_AFTER[n - 1])
                q1 = halves(region(0)[0:GDK], w)[1]
                k0 = halves(region(1)[0:GDK], w)[0]
                w0, w1 = halves(gw, w)
                nc.vector.tensor_tensor(w1, q1, x1, ALU.mult).then_inc(sem("lvl_w"), 1)
                nc.vector.tensor_tensor(w0, k0, x0, ALU.mult).then_inc(sem("lvl_w"), 1)
                if n:
                    take_levels(dve, n - 1)
            take_levels(dve, len(WIDTHS) - 1)
            take_levels(dve, len(WIDTHS))

        def take_levels(dve, n):
            base = A_AFTER[n - 1] if n else 0
            if n == 0:
                for h in range(NH):
                    dve.wait_ge(sem("a_sum"), base + h + 1)
                    nc.vector.tensor_copy(A256[:, h], bank[h][:].rearrange("p (k s) -> p k s", k=2))\
                      .then_inc(sem("a_out"), 1)
            elif n == 1:
                for g in range(2):
                    dve.wait_ge(sem("a_sum"), base + g + 1)
                    nc.vector.tensor_copy(A128[:, 4 * g:4 * g + 4], blocks(bank[4 + g][:])).then_inc(sem("a_out"), 1)
            else:
                mask = lvl[:, 8 - n, :] if n < len(WIDTHS) else ident[:]
                for h in range(NH):
                    dve.wait_ge(sem("a_sum"), base + h + 1)
                    if n == 2:
                        dve.wait_ge(sem("ad_zero"), 1)
                    else:
                        dve.wait_ge(sem("a_out"), A_AFTER[n - 2] + h + 1)
                    nc.vector.copy_predicated(AD[:, 4 * h:4 * h + 4], repeat(mask.bitcast(mybir.dt.uint32), 4),
                                              blocks(bank[(4 * n + h) % 8][:])).then_inc(sem("a_out"), 1)

        A_AFTER = [4, 6]
        for _ in range(len(WIDTHS) - 1):
            A_AFTER.append(A_AFTER[-1] + NH)

        def gla_act(act):
            for n in range(len(WIDTHS)):
                act.wait_ge(sem("lvl_x"), 2 * n + 2)
                nc.scalar.activation(gx, gx, ACT.Exp, scale=1.0 / 16).then_inc(sem("lvl_exp"), 1)
            for t in range(8):
                act.wait_ge(sem("go_sum"), t + 1)
                nc.scalar.activation(go[:, t, :], bank[t % 4][0:96, :], ACT.Copy).then_inc(sem("go"), 1)
            for t in range(8):
                act.wait_ge(sem("go"), t + 1)
                squares96(act, t)
            for h in range(NH):
                act.wait_ge(sem("sum_mix"), 16 + 2 * h + 2)
                nc.scalar.activation(gn[:, h, :], bank[4 + h][0:96, :], ACT.Sqrt, bias=eps[0:96], scale=1.0 / GDV)\
                  .then_inc(sem("norm_mix"), 1)
            nc.scalar.activation(region(2, 2)[0:96], region(2, 2)[0:96], ACT.Silu).then_inc(sem("gg_silu"), 1)
            for t in range(8):
                act.wait_ge(sem("go_out"), 8 + t + 1)
                nc.scalar.activation(xH[0:96, t, :], go[:, t, :], ACT.Copy).then_inc(sem("x_hi"), 1)

        def squares96(act, t):
            act.wait_ge(sem("sum_mix"), 16 + t - 1)
            nc.scalar.activation(sq[0:96, t % 2, :], go[:, t, :], ACT.Square).then_inc(sem("sq_mix"), 1)

        def gla_pe(pe):
            wait_all(pe, stage_end("gla_g") + stage_end("gla_v"))
            for n, w in enumerate(WIDTHS + [0]):
                if w:
                    pe.wait_ge(sem("lvl_w"), 2 * n + 2)
                src = gw.rearrange("p (h s) -> p h s", s=S)
                if n == 0:
                    for h in range(NH):
                        for k in range(2):
                            last = pe.matmul(bank[h][:, 256 * k:256 * k + 256], src[:, h, k * P:(k + 1) * P],
                                             src[:, h, 256:512], start=True, stop=True)
                        last.then_inc(sem("a_sum"), 1)
                elif n == 1:
                    for g in range(2):
                        for u in range(4):
                            h, k = 2 * g + u // 2, 2 * (u % 2)
                            last = pe.matmul(bank[4 + g][:, u * P:(u + 1) * P], src[:, h, k * P:(k + 1) * P],
                                             src[:, h, (k + 1) * P:(k + 2) * P], start=True, stop=True)
                        last.then_inc(sem("a_sum"), 1)
                else:
                    for h in range(NH):
                        b = (4 * n + h) % 8
                        pe.wait_ge(sem("a_out"), (A_AFTER[n - 3] if n >= 3 else 0) + h + 1 if n != 3 else 6)
                        for t in range(TT):
                            x = slice(t * P, (t + 1) * P)
                            a, c = (src[:, h, x], src[:, h, x]) if w else (gk[:, h, x], gq[:, h, x])
                            last = pe.matmul(bank[b][:, x], a, c, start=True, stop=True)
                        last.then_inc(sem("a_sum"), 1)
            pe.wait_ge(sem("a_out"), A_AFTER[-1])
            for t in range(8):
                h, d = divmod(t, 2)
                if t >= 4:
                    pe.wait_ge(sem("go"), t - 3)
                v = slice(GDV * h + 96 * d, GDV * h + 96 * d + 96)
                o = bank[t % 4][0:96]
                for k in range(TT):
                    pe.matmul(o[:, k * P:(k + 1) * P], gv[:, k, v], AD[:, 4 * h + k], start=k == 0, stop=False)
                for k in range(2):
                    pe.matmul(o[:, (2 * k + 1) * P:(2 * k + 2) * P], gv[:, 2 * k, v], A128[:, 2 * h + k],
                              start=False, stop=False)
                for k in range(2):
                    last = pe.matmul(o[:, 256:512], gv[:, k, v], A256[:, h, k], start=False, stop=k == 1)
                last.then_inc(sem("go_sum"), 1)
            for t in range(8):
                pe.wait_ge(sem("sq_mix"), 16 + t + 1)
                pe.matmul(bank[4 + t // 2][0:96, :], ones[0:96, 0:96], sq[0:96, t % 2, :], start=t % 2 == 0,
                          stop=t % 2 == 1).then_inc(sem("sum_mix"), 1)

        def gla_out_dve(dve):
            for h in range(NH):
                dve.wait_ge(sem("norm_mix"), 16 + h + 1)
                nc.vector.reciprocal(gn[:, h, :], gn[:, h, :]).then_inc(sem("inv_mix"), 1)
            for t in range(8):
                dve.wait_ge(sem("inv_mix"), 16 + t // 2 + 1)
                nc.vector.scalar_tensor_tensor(out=go[:, t, :], in0=go[:, t, :], scalar=p96[:, t % 2:t % 2 + 1],
                                               in1=gn[:, t // 2, :], op0=ALU.mult, op1=ALU.mult)\
                  .then_inc(sem("go_out"), 1)
            dve.wait_ge(sem("gg_silu"), 1)
            for t in range(8):
                dve.wait_ge(sem("go_out"), t + 1)
                nc.vector.tensor_tensor(go[:, t, :], go[:, t, :], gg[:, t, :], ALU.mult).then_inc(sem("go_out"), 1)
            for t in range(8):
                dve.wait_ge(sem("x_hi"), xbase(5) + 2 + t + 1)
                nc.vector.tensor_tensor(xL[0:96, t, :], go[:, t, :], xH[0:96, t, :], ALU.subtract)\
                  .then_inc(sem("x_ready"), 1)

        def conv_columns(s, i, t):
            l = {"ffn2_up": 0, "ffn3_up": 1}[s.name]
            f = NF * (t // 2) + 2 * i + t % 2
            w = PAR_AT["conv_w_2"][0] + 3 * 2 * NF * l
            b = PAR_AT["conv_b_2"][0] + 2 * NF * l
            return [par[:, bass.ds(w + 2 * NF * tap + f, 1)] for tap in range(3)] + [par[:, bass.ds(b + f, 1)]]

        def conv_evac_act(act, s, i, t):
            w = conv_columns(s, i, t)
            act.wait_ge(sem("pe_segment"), plan.full(s, i, t))
            act.wait_ge(sem("act_ready"), act_fill(s, i, 2) + CREDIT)
            nc.scalar.activation(cv[:, t, :], bank[t][:], ACT.Identity, bias=w[3], scale=w[2])\
              .then_inc(sem("cv_tap"), 1)
            if t == 3:
                k = conv_index(s, i)
                for u in range(2):
                    act.wait_ge(sem("evac_dve"), plan.evac(s, i, u))
                    nc.scalar.activation(sg[:, u, :], cv[:, u, :], ACT.Silu).then_inc(sem("cv_silu"), 1)
                for u in range(2, 4):
                    act.wait_ge(sem("cv_prod"), 2 * k + u - 1)
                    nc.scalar.activation(gH[:, bass.ds(2 * i + u - 2, 1), :], prod[:, u - 2:u - 1, :], ACT.Copy)\
                      .then_inc(sem("act_hi"), 1)

        def conv_index(s, i):
            return (NF // 2) * {"ffn2_up": 0, "ffn3_up": 1}[s.name] + i

        def conv_evac_dve(dve, s, i, t):
            w = conv_columns(s, i, t)
            k = conv_index(s, i)
            dve.wait_ge(sem("cv_tap"), 4 * k + t + 1)
            nc.vector.scalar_tensor_tensor(out=cv[:, t, 1:], in0=bank[t][:, :S - 1], scalar=w[1],
                                           in1=cv[:, t, 1:], op0=ALU.mult, op1=ALU.add).then_inc(sem("cv_mid"), 1)
            dve.wait_ge(sem("cv_mid"), 4 * k + t + 1)
            nc.vector.scalar_tensor_tensor(out=cv[:, t, 2:], in0=bank[t][:, :S - 2], scalar=w[0],
                                           in1=cv[:, t, 2:], op0=ALU.mult, op1=ALU.add)\
              .then_inc(sem("evac_dve"), 1)
            if t == 3:
                for u in range(2):
                    dve.wait_ge(sem("cv_silu"), 2 * k + u + 1)
                    dve.wait_ge(sem("evac_dve"), plan.evac(s, i, u + 2))
                    nc.vector.tensor_tensor(prod[:, u, :], cv[:, 2 + u, :], sg[:, u, :], ALU.mult)\
                      .then_inc(sem("cv_prod"), 1)
                for u in (2, 3):
                    dve.wait_ge(sem("act_hi"), act_fill(s, i, u) + 1)
                    nc.vector.tensor_tensor(gL[:, bass.ds(2 * i + u - 2, 1), :], prod[:, u - 2:u - 1, :],
                                            gH[:, bass.ds(2 * i + u - 2, 1), :], ALU.subtract)\
                      .then_inc(sem("act_ready"), 1)


        aq = region(0, 2)[:, 0:3072].rearrange("p (t s) -> p t s", s=S)
        misc = region(1)
        gates = misc[:, 1024:1168].rearrange("p (t c) -> p t c", c=36)
        kcT = misc[:, 1200:1262].rearrange("p (g n) -> p g n", n=31)
        vc = misc[0:31, 1280:1536].rearrange("p (g d) -> p g d", d=64)
        hid = misc[:, 1536:1660].rearrange("p (g n) -> p g n", n=31)
        b1c = misc[:, 1664:1666]
        posT = misc[0:64, 1680:1744].rearrange("p (j n) -> p j n", j=2)
        pos = misc[0:32, 1744:1872].rearrange("p (j d) -> p j d", j=2)
        tblT = misc[0:12, 1872:1904]
        tbl = misc[0:32, 1904:1916]
        cw2 = misc[:, 1920:2048].rearrange("p (j d) -> p j d", j=2)
        pre = region(2).rearrange("p (t s) -> p t s", s=S)
        ak = region(3).rearrange("p (t s) -> p t s", s=S)
        av = region(4).rearrange("p (j t c) -> p j t c", j=2, c=256)
        TW = 896
        tab = region(5)[:, 0:2 * TW].rearrange("p (b c) -> p b c", c=TW)
        relrow = region(5)[0:12, 0:1024]
        w1 = [region(9, 2).rearrange("p (q n) -> p q n", n=P), region(12, 2).rearrange("p (q n) -> p q n", n=P)]
        skew = [region(12)[:, 0:TW], region(13)[:, 0:TW]]
        pbuf = [region(8)[:, 0:1024], region(9)[:, 0:1024]]
        ptb = [region(10), region(11)]
        dg = region(7)[:, 0:1024].rearrange("p (b u c) -> p b u c", b=2, c=P)
        nstat = sb("nstat", [P, 2, 4, 4])
        mirror = sb("mirror", [P, P])
        b2 = sb("b2", [P, 1 + 64])
        NCMP, AH = 31, 12
        NEG = -1e30
        rel_dram = nc.dram_tensor("rel_rows", (AH, 1024), F32, kind="Internal").ap()

        def kv_place(i, t):
            return (pre if t < 4 else ak)[:, t % 4, :], P, S, 1.0

        def kvt_place(i, t):
            j, tile = divmod(t, TT)
            return av[:, j, tile, :], P, 256, 1.0

        def aq_place(i, t):
            return aq[:, t, :], P, S, 0.125

        def gate_evac_act(act, s, i, t):
            if t < TT:
                act.wait_ge(sem("pe_segment"), plan.full(s, i, t))
                nc.scalar.activation(gates[:, t, :], bank[t][:, 0:36], ACT.Sigmoid).then_inc(sem("evac_act"), 1)

        def mq_place(i, t):
            return memQ[:, t - TT, :], P, S, 1.0

        def bucket_ranges():
            d = np.arange(S)
            big = 16 + (np.log(np.maximum(d, 1).astype(np.float32) / np.float32(16))
                        / np.float32(np.log(128 / 16)) * np.float32(16)).astype(np.int32)
            bucket = np.where(d < 16, d, np.minimum(big, 31))
            return [(int(d[bucket == b].min()), int(d[bucket == b].max())) for b in range(32)]

        def rel_sp(sp):
            sp.wait_ge(*stage_end("ffn2_down")[0])
            sp.dma_start(tbl, A["rel_bias_2"]).then_inc(sem("nsa_small"), 16)
            for j in range(2):
                sp.dma_start(pos[:, j, :], A["cmp_pos_2"][j]).then_inc(sem("nsa_small"), 16)
                sp.dma_start(cw2[:, j, :], A["cmp_w2_2"][j]).then_inc(sem("nsa_small"), 16)
                sp.dma_start(b2[64 * j:64 * j + 64, 0:1], A["cmp_b2_2"][0].rearrange("(p o) -> p o", o=1))\
                  .then_inc(sem("nsa_small"), 16)
            sp.dma_start(b2[0:1, 1:65], A["cmp_b2_2"][1:2]).then_inc(sem("nsa_small"), 16)

        def w1_sp(sp):
            sp.wait_ge(sem("mem_ready"), 2)
            for j in range(2):
                for half in range(2):
                    sp.dma_start(w1[j][64 * half:64 * half + 64], A["cmp_w1_2"][j].rearrange("(q d) n -> d q n", d=64))\
                      .then_inc(sem("w1_landed"), 16)

        def rel_store(pool):
            pool.wait_ge(sem("rel_row"), 33)
            pool.dma_start(rel_dram, relrow).then_inc(sem("rel_stored"), 16)
            pool.wait_ge(sem("rel_stored"), 16)

        def skew_pool(pool):
            pool.wait_ge(sem("c_dve"), 4)
            for h in range(AH):
                if h >= 2:
                    pool.wait_ge(sem("tab_sum"), 2 * (h - 1))
                pool.dma_start(skew[h % 2], bass.AP(rel_dram.tensor, 1024 * h, [[1, P], [1, TW]]))\
                  .then_inc(sem(f"skew{h % 2}"), 16)

        def rel_pe(pe):
            pe.wait_ge(sem("nsa_small"), 16 * 8)
            wait_all(pe, stage_end("kv_t") + stage_end("kv_f"))
            turn(pe, bank[4][0:AH, 0:32], tbl, 32)
            for j in range(2):
                last = turn(pe, bank[4][0:64, 32 * j + 32:32 * j + 64], pos[:, j, :], 32)
            last.then_inc(sem("small_turned"), 1)

        def rel_dve(dve):
            dve.wait_ge(sem("small_turned"), 1)
            nc.vector.tensor_copy(tblT, bank[4][0:AH, 0:32]).then_inc(sem("small_t"), 1)
            nc.vector.tensor_copy(posT, bank[4][0:64, 32:96].rearrange("p (j n) -> p j n", j=2))\
              .then_inc(sem("small_t"), 1)
            dve.wait_ge(sem("small_t"), 2)
            nc.vector.memset(relrow[:, 512:1024], NEG).then_inc(sem("rel_row"), 1)
            for b, (lo, hi) in enumerate(bucket_ranges()):
                nc.vector.tensor_scalar(relrow[:, 511 - hi:512 - lo], ones[0:AH, 0:1].broadcast_to([AH, hi - lo + 1]),
                                        tblT[:, b:b + 1], None, ALU.mult).then_inc(sem("rel_row"), 1)

        def cmp_pe(pe):
            wait_all(pe, stage_end("nsa_q") + stage_end("nsa_g"))
            pe.wait_ge(sem("w1_landed"), 64)
            pe.wait_ge(sem("small_t"), 2)
            for j in range(2):
                if j:
                    pe.wait_ge(sem("c_dve"), 1)
                    pe.wait_ge(sem("c_hid"), 2)
                for q in range(32):
                    last = pe.matmul(bank[0][:, 0:1], w1[j][0:64, q, :], posT[:, j, q:q + 1], start=q == 0, stop=q == 31)
                last.then_inc(sem("c_pe"), 1)
                for half in range(2):
                    f = slice(64 * half, 64 * half + 64)
                    for g in range(2):
                        for q in range(32):
                            last = pe.matmul(bank[1 + half][:, g * NCMP:(g + 1) * NCMP], w1[j][f, q, :],
                                             pre[f, 2 * j + g, q:q + 16 * (NCMP - 1) + 1:16], start=q == 0, stop=q == 31)
                    last.then_inc(sem("c_pe"), 1)
                pe.wait_ge(sem("c_hid"), 2 * j + 2)
                for g in range(4):
                    if j == 0:
                        last = pe.matmul(bank[3][64 * (g % 2):64 * (g % 2) + 64, (g // 2) * NCMP:(g // 2 + 1) * NCMP],
                                         cw2[:, 0, :], hid[:, g, :], start=True, stop=True)
                    else:
                        o = bank[4][0:NCMP, 64 * g:64 * g + 64]
                        pe.matmul(o, hid[:, g, :], cw2[:, 1, :], start=True, stop=False)
                        last = pe.matmul(o, ones[0:1, 0:NCMP], b2[0:1, 1:65], start=False, stop=True)
                last.then_inc(sem("c_pe"), 1)

        def cmp_dve(dve):
            for j in range(2):
                dve.wait_ge(sem("c_pe"), 4 * j + 1)
                nc.vector.tensor_tensor(b1c[:, j:j + 1], bank[0][:, 0:1], column("cmp_b1_2", j), ALU.add)\
                  .then_inc(sem("c_dve"), 1)
                dve.wait_ge(sem("c_pe"), 4 * j + 4)
                if j == 0:
                    nc.vector.tensor_scalar(kcT[:], bank[3][:, 0:2 * NCMP].rearrange("p (g n) -> p g n", n=NCMP),
                                            b2[:, 0:1], None, ALU.add).then_inc(sem("c_dve"), 1)
                else:
                    nc.vector.tensor_copy(vc[:], bank[4][0:NCMP, 0:256].rearrange("p (g d) -> p g d", d=64))\
                      .then_inc(sem("c_dve"), 1)

        def cmp_act(act):
            for j in range(2):
                act.wait_ge(sem("c_dve"), 2 * j + 1)
                if j:
                    act.wait_ge(sem("c_pe"), 4)
                for half in range(2):
                    act.wait_ge(sem("c_pe"), 4 * j + half + 2)
                    nc.scalar.activation(hid[:, half:4:2, :], bank[1 + half][:, 0:2 * NCMP]
                                         .rearrange("p (g n) -> p g n", n=NCMP), ACT.Silu, bias=b1c[:, j:j + 1])\
                      .then_inc(sem("c_hid"), 1)

        items = [(h, t) for h in range(AH) for t in (None, 0, 1, 2, 3)]

        def head_at(h):
            g = h // 3
            return 3 * (g // 2) + h % 3, slice(64 * (g % 2), 64 * (g % 2) + 64), g, g // 2

        def score_banks(h, t):
            return (bank[0], bank[1]) if t % 2 == 0 else (bank[3], bank[4])

        def attend_pe(pe):
            wait_all(pe, stage_end("nsa_q") + stage_end("nsa_g"))
            pe.wait_ge(sem("x_ready"), xbase(9) + 2)
            pe.wait_ge(sem("c_dve"), 4)
            pe.wait_ge(sem("mirror"), 2)
            for m in range(len(items) + 2):
                if m < len(items):
                    h, t = items[m]
                    tile, f, g, gt = head_at(h)
                    if t is None:
                        pe.wait_ge(sem(f"skew{h % 2}"), 16 * (h // 2 + 1))
                        for u in range(2):
                            if h or u:
                                pe.wait_ge(sem("tab"), 2 * h + u)
                            if h and not u:
                                pe.wait_ge(sem("n_max"), 5 * (h - 1) + 1)
                            pe.matmul(bank[2][:, 0:448], mirror[:], skew[h % 2][:, 448 * u:448 * (u + 1)],
                                      start=True, stop=True).then_inc(sem("tab_sum"), 1)
                        pe.wait_ge(sem("tab"), 2 * h + 2)
                        for u in range(TT):
                            last = pe.matmul(bank[2][:, 32 * u:32 * u + NCMP], aq[f, tile, u * P:(u + 1) * P],
                                             kcT[f, gt, :], start=True, stop=True)
                    else:
                        if m >= 2:
                            pe.wait_ge(sem("n_max"), m - 1 if t >= 2 else max(1, m - 2))
                        n = P * (t + 1)
                        s0, s1 = score_banks(h, t)
                        pe.matmul(s0[:, 0:n], aq[f, tile, t * P:(t + 1) * P], ak[f, gt, 0:n], start=True, stop=True)
                        last = pe.matmul(s1[:, 0:n], aq[f, tile, t * P:(t + 1) * P], ak[f, 2 + gt, 0:n],
                                         start=True, stop=True)
                    last.then_inc(sem("n_scores"), 1)
                if 1 <= m <= len(items):
                    q = m - 1
                    h, t = items[q]
                    pe.wait_ge(sem("n_diag"), q + 1)
                    if q:
                        pe.wait_ge(sem("n_pts"), q)
                    if wcount(q):
                        pe.wait_ge(sem("n_ptw"), wcount(q))
                    if t is None:
                        for u in range(TT):
                            last = pe.matmul(bank[5][0:NCMP, u * P:(u + 1) * P], pbuf[q % 2][:, 32 * u:32 * u + NCMP],
                                             dg[:, q % 2, u, :], start=True, stop=True)
                    else:
                        for br in range(2):
                            for k in range(t + 1):
                                last = pe.matmul(bank[5 + br][:, k * P:(k + 1) * P],
                                                 pbuf[q % 2][:, 512 * br + k * P:512 * br + (k + 1) * P],
                                                 dg[:, q % 2, br, :], start=True, stop=True)
                    last.then_inc(sem("n_turned"), 1)
                if m >= 2:
                    q = m - 2
                    h, t = items[q]
                    _, _, g, _ = head_at(h)
                    o = bank[7][64 * (h % 2):64 * (h % 2) + 64]
                    pe.wait_ge(sem("n_pts"), q + 1)
                    if t is None:
                        if h >= 2:
                            pe.wait_ge(sem("x_ready"), xbase(9) + 2 + h - 1)
                        for u in range(TT):
                            last = pe.matmul(o[:, u * P:(u + 1) * P], vc[:, g, :], ptb[q % 2][0:NCMP, u * P:(u + 1) * P],
                                             start=u == 0, stop=False, skip_group_check=True)
                    else:
                        pe.wait_ge(sem("n_ptw"), wcount(q + 1))
                        for br in range(2):
                            for k in range(t + 1):
                                last = pe.matmul(o[:, t * P:(t + 1) * P], av[:, br, k, 64 * g:64 * g + 64],
                                                 ptb[q % 2][:, 512 * br + k * P:512 * br + (k + 1) * P], start=False,
                                                 stop=t == 3 and br == 1 and k == t, skip_group_check=True)
                    last.then_inc(sem("n_out"), 1)

        def wcount(q):
            return sum(t is not None for _, t in items[:q])

        def attend_dve(dve):
            for m in range(len(items) + 2):
                if m < len(items):
                    h, t = items[m]
                    st = nstat[:, m % 2]
                    dve.wait_ge(sem("n_scores"), m + 1)
                    if m >= 2:
                        dve.wait_ge(sem("n_turned"), m - 1)
                    if t is None:
                        dve.wait_ge(sem("tab"), 2 * h + 2)
                        cut = [(bank[2][:, 32 * u:32 * u + NCMP], tab[:, h % 2, 415 - P * u:415 - P * u + 481:16],
                                pbuf[m % 2][:, 32 * u:32 * u + NCMP]) for u in range(TT)]
                    else:
                        n = P * (t + 1)
                        table = tab[:, h % 2, 384 - P * t:384 - P * t + n]
                        cut = [(b[:, 0:n], table, pbuf[m % 2][:, 512 * br:512 * br + n])
                               for br, b in enumerate(score_banks(h, t))]
                    for u, (a, b, o) in enumerate(cut):
                        last = nc.vector.tensor_tensor_reduce(out=o, in0=a, in1=b, scale=1.0, scalar=-3e38, op0=ALU.add,
                                                              op1=ALU.max, accum_out=st[:, 0, u:u + 1])
                    last.then_inc(sem("n_raw"), 1)
                    dve.wait_ge(sem("n_raw"), m + 1)
                    nc.vector.tensor_scalar(st[:, 1, 0:len(cut)], st[:, 0, 0:len(cut)], -1e29, -1.0, ALU.max, ALU.mult)\
                      .then_inc(sem("n_max"), 1)
                if 1 <= m <= len(items):
                    q = m - 1
                    h, t = items[q]
                    st = nstat[:, q % 2]
                    n = TT if t is None else 2
                    dve.wait_ge(sem("n_exp"), q + 1)
                    nc.vector.tensor_scalar(st[:, 2, 0:n], st[:, 2, 0:n], 1e-30, None, ALU.max)\
                      .then_inc(sem("n_clamp"), 1)
                    dve.wait_ge(sem("n_clamp"), q + 1)
                    nc.vector.reciprocal(st[:, 3, 0:n], st[:, 2, 0:n]).then_inc(sem("n_inv"), 1)
                    dve.wait_ge(sem("n_inv"), q + 1)
                    if q >= 2:
                        dve.wait_ge(sem("n_turned"), q - 1)
                    for u in range(n):
                        gate = gates[:, u, 3 * h:3 * h + 1] if t is None else gates[:, t, 3 * h + 1 + u:3 * h + 2 + u]
                        last = nc.vector.tensor_scalar(dg[:, q % 2, u, :], ident[:], st[:, 3, u:u + 1], gate,
                                                       ALU.mult, ALU.mult)
                    last.then_inc(sem("n_diag"), 1)
                if m >= 2:
                    q = m - 2
                    h, t = items[q]
                    if t is not None:
                        n = P * (t + 1)
                        dve.wait_ge(sem("n_turned"), q + 1)
                        if q >= 2:
                            dve.wait_ge(sem("n_out"), q - 1)
                        nc.vector.tensor_copy(ptb[q % 2][:, 512:512 + n], bank[6][:, 0:n]).then_inc(sem("n_ptw"), 1)
                if m >= 3 and items[m - 3][1] == 3:
                    rest_dve(dve, items[m - 3][0])
            rest_dve(dve, AH - 1)

        def rest_dve(dve, h):
            f = slice(64 * (h % 2), 64 * (h % 2) + 64)
            dve.wait_ge(sem("x_hi"), xbase(9) + 2 + h + 1)
            nc.vector.tensor_tensor(xL[f, h // 2, :], bank[7][f, :], xH[f, h // 2, :], ALU.subtract)\
              .then_inc(sem("x_ready"), 1)

        def attend_act(act):
            for m in range(len(items) + 2):
                if m < len(items):
                    h, t = items[m]
                    if t is None:
                        for u in range(2):
                            act.wait_ge(sem("tab_sum"), 2 * h + u + 1)
                            if h >= 2:
                                act.wait_ge(sem("n_max"), 5 * (h - 1))
                            nc.scalar.activation(tab[:, h % 2, 448 * u:448 * (u + 1)], bank[2][:, 0:448], ACT.Copy)\
                              .then_inc(sem("tab"), 1)
                        cut = [slice(32 * u, 32 * u + NCMP) for u in range(TT)]
                    else:
                        cut = [slice(512 * br, 512 * br + P * (t + 1)) for br in range(2)]
                    act.wait_ge(sem("n_max"), m + 1)
                    if m >= 2:
                        act.wait_ge(sem("n_inv"), m - 1)
                    for u, x in enumerate(cut):
                        last = nc.scalar.activation(pbuf[m % 2][:, x], pbuf[m % 2][:, x], ACT.Exp,
                                                    bias=nstat[:, m % 2, 1, u:u + 1],
                                                    accum_out=nstat[:, m % 2, 2, u:u + 1])
                    last.then_inc(sem("n_exp"), 1)
                if m >= 2:
                    q = m - 2
                    h, t = items[q]
                    act.wait_ge(sem("n_turned"), q + 1)
                    if q >= 2:
                        act.wait_ge(sem("n_out"), q - 1)
                    x, r = (slice(0, 512), NCMP) if t is None else (slice(0, P * (t + 1)), P)
                    nc.scalar.activation(ptb[q % 2][0:r, x], bank[5][0:r, x], ACT.Copy).then_inc(sem("n_pts"), 1)
                if m >= 3 and items[m - 3][1] == 3:
                    upper_act(act, items[m - 3][0])
            upper_act(act, AH - 1)

        def upper_act(act, h):
            f = slice(64 * (h % 2), 64 * (h % 2) + 64)
            act.wait_ge(sem("n_out"), 5 * (h + 1))
            nc.scalar.activation(xH[f, h // 2, :], bank[7][f, :], ACT.Copy).then_inc(sem("x_hi"), 1)

        def result_dve(dve):
            for k in range(KD):
                if k >= 2:
                    dve.wait_ge(sem("y_turned"), k - 1)
                nc.vector.scalar_tensor_tensor(out=xn[:, k % 2, :], in0=hT[:, k, :], in1=rstd[:], op0=ALU.mult,
                                               scalar=column("final_norm_2", k), op1=ALU.mult).then_inc(sem("y"), 1)
                if k >= 1 and (k - 1) % 2 == 1:
                    rows_out(dve, k - 1)
            rows_out(dve, KD - 1)

        def rows_out(eng, k):
            eng.wait_ge(sem("y_turned"), k + 1)
            o, b = rows[:, :, k * P:(k + 1) * P], blocks(bank[k % 4][:])
            if k % 2 == 1:
                nc.vector.tensor_copy(o, b).then_inc(sem("rows_dve"), 1)
            else:
                nc.scalar.activation(o, b, ACT.Copy).then_inc(sem("rows_act"), 1)

        def result_pe(pe):
            wait_all(pe, stage_end("ffn3_down"))
            for k in range(KD):
                pe.wait_ge(sem("y"), Y0 + k + 1)
                if k >= 4:
                    pe.wait_ge(sem("rows_act" if k % 2 == 0 else "rows_dve"), (k - 4) // 2 + 1)
                for t in range(TT):
                    last = turn(pe, bank[k % 4][:, t * P:(t + 1) * P], xn[:, k % 2, t * P:(t + 1) * P])
                last.then_inc(sem("y_turned"), 1)

        def result_act(act):
            for k in range(0, KD, 2):
                rows_out(act, k)

        Y0 = 4 * (LEVELS - 1)

        def result_sp(sp):
            sp.wait_ge(sem("rows_act"), KD // 2)
            sp.wait_ge(sem("rows_dve"), KD // 2)
            sp.dma_start(out[0].rearrange("(t p) c -> p t c", p=P), rows[:, :, :]).then_inc(sem("stored"), 16)
            sp.wait_ge(sem("stored"), 16)


        def h_loaded(k):
            return (sem("h_act" if k % 2 == 0 else "h_dve"), k // 2 + 1)

        @nc_block.sync
        def _(sp):
            sp.dma_start(rows[:, :, :], A["x"][0].rearrange("(t p) c -> p t c", p=P)).then_inc(sem("x_landed"), 16)
            load_sp(sp)
            for i, name in enumerate(("gdn_A_log", "gdn_dt_bias")):
                sp.dma_start(hv[:, i:i + 1], A[name][0].rearrange("(p o) -> p o", o=1)).then_inc(sem("hv_landed"), 16)
            sp.dma_start(gate_up[:], A["gla_w_gate_up_2"][0]).then_inc(sem("gate_landed"), 16)
            for c in range(6):
                name, k = ("gla_out_norm_2", c) if c < 2 else ("gla_b_gate_2", c - 2)
                sp.dma_start(p96[:, c:c + 1], A[name][0, 96 * k:96 * (k + 1)].rearrange("(p o) -> p o", o=1))\
                  .then_inc(sem("gate_landed"), 16)
            for s in plan.order:
                load_panels(sp, s.name)
                if s.name == "ffn1_up":
                    mem_load(sp, 0, stage_end("mix_out")[0])
                if s.name == "ffn2_up":
                    mem_load(sp, 1, stage_end("gla_out")[0])
                if s.name == "mem1_kv":
                    rel_sp(sp)
                    w1_sp(sp)
            result_sp(sp)

        @nc_block.gpsimd
        def _(pool):
            constants_pool(pool)
            pool.sem_inc(sem("w_lo"), CREDIT)
            split_lo(pool, "ffn0_up")
            constants2_pool(pool)
            split_lo(pool, "ffn0_down")
            split_lo(pool, "mix_ba")
            split_lo(pool, "mix_in")
            gdn_pool(pool)
            split_lo(pool, "mix_out")
            split_lo(pool, "ffn1_up")
            split_lo(pool, "ffn1_down")
            for name in ("mem0_kv", "gla_rest", "gla_q", "gla_k"):
                split_lo(pool, name)
            wait_all(pool, stage_end("mem0_kv"))
            nc.gpsimd.memset(AD[:], 0.0).then_inc(sem("ad_zero"), 1)
            nc.gpsimd.memset(mirror[:], 0.0).then_inc(sem("mirror"), 1)
            pool.wait_ge(sem("mirror"), 1)
            nc.gpsimd.affine_select(out=mirror[:], in_=mirror[:], compare_op=ALU.not_equal, fill=1.0, base=1 - P,
                                    pattern=[[1, P]], channel_multiplier=1).then_inc(sem("mirror"), 1)
            for name in ("gla_v", "gla_g", "gla_out", "ffn2_up", "ffn2_down", "mem1_kv", "kv_f", "kv_t", "nsa_q",
                         "nsa_g", "nsa_out", "ffn3_up", "ffn3_down"):
                split_lo(pool, name)
                if name == "nsa_g":
                    rel_store(pool)
                    skew_pool(pool)

        @nc_block.scalar
        def _(act):
            load_act(act)
            split_hi(act, plan.order[0].slot[0], plan.landed(plan.order[0], 0, 0), 0, CREDIT_PE)
            norm_act(act, 0, h_loaded)
            scaled_act(act, 0)
            dense_act(act, "ffn0_up", up_evac_act)
            dense_act(act, "ffn0_down", nothing)
            norm_act(act, 1, h_from("ffn0_down"))
            scaled_act(act, 1)
            dense_act(act, "mix_ba", ba_evac_act)
            dense_act(act, "mix_in", in_evac("act"))
            gdn_act(act)
            dense_act(act, "mix_out", nothing)
            norm_act(act, 2, h_from("mix_out"))
            scaled_act(act, 3)
            dense_act(act, "ffn1_up", up_evac_act)
            dense_act(act, "ffn1_down", nothing)
            norm_act(act, 3, h_from("ffn1_down"))
            mem_act(act, 0)
            norm_act(act, 4, lambda k: (sem("h_final"), k + 1))
            scaled_act(act, 4)
            dense_act(act, "mem0_kv", evac_to("act", mem_place))
            dense_act(act, "gla_rest", evac_to("act", rest_place))
            gate_act(act)
            dense_act(act, "gla_q", evac_to("act", lambda i, t: (gq[:, t, :], 96, S, GDK ** -0.5)))
            dense_act(act, "gla_k", nothing)
            dense_act(act, "gla_v", evac_to("act", v_place))
            dense_act(act, "gla_g", evac_to("act", lambda i, t: (gg[:, bass.ds(4 * i + t, 1), :], 96, S, 1.0)))
            mem_attn_act(act, 0, 5, 8)
            gla_act(act)
            dense_act(act, "gla_out", nothing)
            norm_act(act, 5, h_from("gla_out"))
            scaled_act(act, 6)
            dense_act(act, "ffn2_up", conv_evac_act)
            dense_act(act, "ffn2_down", nothing)
            norm_act(act, 6, h_from("ffn2_down"))
            scaled_act(act, 7)
            mem_act(act, 1)
            dense_act(act, "mem1_kv", evac_to("act", mem_place))
            dense_act(act, "kv_f", evac_to("act", kv_place))
            dense_act(act, "kv_t", evac_to("act", kvt_place))
            scaled_act(act, 8, plan.full(plan.stages["kv_t"], 0, 7))
            dense_act(act, "nsa_q", evac_to("act", aq_place))
            dense_act(act, "nsa_g", gate_evac_act)
            cmp_act(act)
            mem_attn_act(act, 1, 9, 6)
            attend_act(act)
            dense_act(act, "nsa_out", nothing)
            norm_act(act, 7, h_from("nsa_out"))
            scaled_act(act, 10)
            dense_act(act, "ffn3_up", conv_evac_act)
            dense_act(act, "ffn3_down", nothing)
            norm_act(act, 8, h_from("ffn3_down"))
            result_act(act)

        @nc_block.vector
        def _(dve):
            load_dve(dve)
            norm_dve(dve, 0)
            scaled_dve(dve, 0, "ffn1_norm")
            dense_dve(dve, "ffn0_up", up_evac_dve)
            dense_dve(dve, "ffn0_down", residual(0.5))
            norm_dve(dve, 1)
            scaled_dve(dve, 1, "mix_norm")
            dense_dve(dve, "mix_ba", ba_evac_dve)
            dense_dve(dve, "mix_in", in_evac("dve"))
            gdn_dve(dve)
            dense_dve(dve, "mix_out", residual(1.0))
            norm_dve(dve, 2)
            scaled_dve(dve, 3, "ffn2_norm")
            dense_dve(dve, "ffn1_up", up_evac_dve)
            dense_dve(dve, "ffn1_down", residual(0.5))
            norm_dve(dve, 3)
            final_dve(dve)
            mem_dve(dve, 0)
            norm_dve(dve, 4)
            scaled_dve(dve, 4, "norm_mix_2")
            dense_dve(dve, "mem0_kv", evac_to("dve", mem_place))
            dense_dve(dve, "gla_rest", evac_to("dve", rest_place))
            gate_dve(dve)
            dense_dve(dve, "gla_k", evac_to("dve", lambda i, t: (gk[:, t, :], 96, S, 1.0)))
            dense_dve(dve, "gla_v", evac_to("dve", v_place))
            mem_attn_dve(dve, 0, 5, 8, xbase(5))
            gla_dve(dve)
            gla_out_dve(dve)
            dense_dve(dve, "gla_out", residual(1.0))
            norm_dve(dve, 5)
            scaled_dve(dve, 6, "norm_ffn_2")
            dense_dve(dve, "ffn2_up", conv_evac_dve)
            dense_dve(dve, "ffn2_down", residual(1.0))
            norm_dve(dve, 6)
            scaled_dve(dve, 7, "kv_norm_2")
            mem_dve(dve, 1)
            dense_dve(dve, "mem1_kv", evac_to("dve", mem_place))
            dense_dve(dve, "kv_f", evac_to("dve", kv_place))
            dense_dve(dve, "kv_t", evac_to("dve", kvt_place))
            scaled_dve(dve, 8, "norm_mix_2", KD)
            dense_dve(dve, "nsa_q", evac_to("dve", aq_place))
            rel_dve(dve)
            dense_dve(dve, "nsa_g", evac_to("dve", mq_place))
            cmp_dve(dve)
            mem_attn_dve(dve, 1, 9, 6, xbase(9))
            attend_dve(dve)
            dense_dve(dve, "nsa_out", residual(1.0))
            norm_dve(dve, 7)
            scaled_dve(dve, 10, "norm_ffn_2", KD)
            dense_dve(dve, "ffn3_up", conv_evac_dve)
            dense_dve(dve, "ffn3_down", residual(1.0))
            norm_dve(dve, 8)
            result_dve(dve)

        @nc_block.tensor
        def _(pe):
            load_pe(pe)
            norm_pe(pe, 0)
            dense_pe(pe, "ffn0_up")
            dense_pe(pe, "ffn0_down")
            norm_pe(pe, 1)
            dense_pe(pe, "mix_ba")
            dense_pe(pe, "mix_in")
            gdn_pe(pe)
            dense_pe(pe, "mix_out")
            norm_pe(pe, 2)
            dense_pe(pe, "ffn1_up")
            dense_pe(pe, "ffn1_down")
            norm_pe(pe, 3)
            mem_pe(pe, 0)
            norm_pe(pe, 4)
            dense_pe(pe, "mem0_kv")
            dense_pe(pe, "gla_rest")
            gate_pe(pe)
            dense_pe(pe, "gla_q")
            dense_pe(pe, "gla_k")
            dense_pe(pe, "gla_v")
            dense_pe(pe, "gla_g")
            mem_attn_pe(pe, 0, stage_end("mem0_kv") + stage_end("gla_rest") + stage_end("gla_g") + stage_end("gla_v"))
            gla_pe(pe)
            dense_pe(pe, "gla_out")
            norm_pe(pe, 5)
            dense_pe(pe, "ffn2_up")
            dense_pe(pe, "ffn2_down")
            norm_pe(pe, 6)
            mem_pe(pe, 1)
            dense_pe(pe, "mem1_kv")
            dense_pe(pe, "kv_f")
            dense_pe(pe, "kv_t")
            rel_pe(pe)
            dense_pe(pe, "nsa_q")
            dense_pe(pe, "nsa_g")
            cmp_pe(pe)
            mem_attn_pe(pe, 1, stage_end("mem1_kv") + stage_end("nsa_q") + stage_end("nsa_g") + [(sem("c_dve"), 4)])
            attend_pe(pe)
            dense_pe(pe, "nsa_out")
            norm_pe(pe, 7)
            dense_pe(pe, "ffn3_up")
            dense_pe(pe, "ffn3_down")
            norm_pe(pe, 8)
            result_pe(pe)


def kernel(**inputs):
    import numpy as _np
    import concourse.bacc as _bacc
    from concourse import mybir as _mybir
    from concourse.bass_utils import run_bass_kernel_spmd as _run

    nc = _bacc.Bacc("TRN2", target_bir_lowering=False, num_devices=1)
    arrays, args = {}, {}
    for name in inputs:
        a = _np.ascontiguousarray(inputs[name])
        arrays[f"in_{name}"] = a
        args[name] = nc.dram_tensor(f"in_{name}", a.shape, _mybir.dt.from_np(a.dtype), kind="ExternalInput").ap()
    out = nc.dram_tensor("out", (1, S, D), _mybir.dt.float32, kind="ExternalOutput").ap()
    build(nc, args, out)
    r = _run(nc, [arrays], core_ids=[0])
    return r.results[0]["out"]
```

```python
import concourse.bass as bass
import numpy as np
from concourse import mybir
from contextlib import ExitStack

ALU = mybir.AluOpType
ACT = mybir.ActivationFunctionType
AX = mybir.AxisListType.X
F32 = mybir.dt.float32
F32R = mybir.dt.float32r

P = 128
S = 512
D = 1024
KD = D // P
TT = S // P
FF = 2816
NF = FF // P
M = 256
EPS = 1e-6
SLOT = 1024
SLOTS = 4
CREDIT = 2
CREDIT_PE = 8
CREDIT_EV = 8


class Dense:

    def __init__(self, name, iters, panels, tiles, xs, need):
        self.name, self.iters, self.panels, self.tiles, self.xs, self.need = name, iters, panels, tiles, xs, need
        self.split = len(xs) == 2
        self.segments = []
        for t, tile in enumerate(tiles):
            for j in sorted({term[0] for term in tile["terms"]}):
                self.segments.append((t, j))


class Plan:

    def __init__(self, stages):
        self.order = stages
        self.stages = {s.name: s for s in stages}
        n, splits, segments, landed = 0, 0, 0, [0] * SLOTS
        evac = {"act": 0, "dve": 0}
        bank_last = {}
        for s in stages:
            assert s.iters == 1 or len(s.panels) % SLOTS == 0, s.name
            s.split0 = splits
            s.panel0, s.seg0, s.landed0, s.evac0 = n, segments, list(landed), dict(evac)
            s.slot = [(n + j) % SLOTS for j in range(len(s.panels))]
            s.landed_step = [16 * sum(len(p) for p, q in zip(s.panels, s.slot) if q == k) for k in range(SLOTS)]
            s.evac_step = {e: sum(t["by"] == e for t in s.tiles) for e in evac}
            s.before = {t["bank"]: bank_last[t["bank"]] for t in s.tiles if t["bank"] in bank_last}
            for t, tile in enumerate(s.tiles):
                bank_last[tile["bank"]] = (tile["by"], self.evac(s, s.iters - 1, t))
            n += s.iters * len(s.panels)
            splits += s.iters * len(s.panels) * s.split
            segments += s.iters * len(s.segments)
            landed = [a + s.iters * b for a, b in zip(landed, s.landed_step)]
            evac = {e: evac[e] + s.iters * s.evac_step[e] for e in evac}
        self.panels = n

    def where(self, n):
        s = max((s for s in self.order if s.panel0 <= n), key=lambda s: s.panel0)
        return s, (n - s.panel0) // len(s.panels), (n - s.panel0) % len(s.panels)

    def ahead(self, s, i, j, by):
        if isinstance(i, int):
            return self.where(s.panel0 + i * len(s.panels) + j + by)
        step, k = divmod(j + by, len(s.panels))
        return s, i + step, k

    def landed(self, s, i, j):
        here = 16 * sum(len(s.panels[q]) for q in range(j + 1) if s.slot[q] == s.slot[j])
        return s.landed0[s.slot[j]] + i * s.landed_step[s.slot[j]] + here

    def full(self, s, i, t):
        at = max(k for k, (u, _) in enumerate(s.segments) if u == t)
        return CREDIT_PE + s.seg0 + i * len(s.segments) + at + 1

    def used(self, s, i, j):
        at = max(k for k, (_, p) in enumerate(s.segments) if p == j)
        return CREDIT_PE + s.seg0 + i * len(s.segments) + at + 1

    def split(self, s, i, j):
        return s.split0 + i * len(s.panels) + j + 1

    def evac(self, s, i, t):
        e = s.tiles[t]["by"]
        return CREDIT_EV + s.evac0[e] + i * s.evac_step[e] + sum(x["by"] == e for x in s.tiles[:t + 1])


def param_layout():
    names = [("ffn1_norm", 8), ("mix_norm", 8), ("ffn2_norm", 8), ("final_norm", 8), ("norm_mix_2", 16),
             ("norm_mem_2", 16), ("norm_ffn_2", 16), ("kv_norm_2", 8), ("final_norm_2", 8), ("cmp_b1_2", 2),
             ("gdn_out_norm", 1), ("conv_short_w", 12), ("conv_out_norm", 4),
             ("gdn_conv_w", 48), ("conv_w_2", 264), ("conv_b_2", 88)]
    at, first = {}, 0
    for name, n in names:
        at[name] = (first, n)
        first += n
    return at, first


PAR_AT, NPAR = param_layout()
NPT = -(-NPAR // P)
NPAR_DMA = sum((f + n - 1) // P - f // P + 1 for f, n in PAR_AT.values())


def build(nc, A, out):
    with ExitStack() as ctx:
        sems = {}

        def sem(name):
            if name not in sems:
                sems[name] = ctx.enter_context(nc.semaphore(name))
            return sems[name]

        def sb(name, shape, dt=F32):
            return ctx.enter_context(nc.sbuf_tensor(name, shape, dt))

        hT = sb("hT", [P, KD, S])
        xH = sb("xH", [P, KD, S], F32R)
        xL = sb("xL", [P, KD, S], F32R)
        raw = sb("raw", [P, SLOTS, SLOT])
        wH = sb("wH", [P, 2, SLOT], F32R)
        wL = sb("wL", [P, 2, SLOT], F32R)
        xHf = xH[:].bitcast(F32)
        par = sb("par", [P, NPAR])
        ident = sb("ident", [P, P])
        ones = sb("ones", [P, P])
        eps = sb("eps", [P, 1])
        ones64 = sb("ones64", [P, P])
        lvl = sb("lvl", [P, 7, P])
        hv = sb("hv", [4, 4])
        col = sb("col", [P, 8, 16])
        sq = sb("sq", [P, 2, S])
        rstd = sb("rstd", [P, S])
        xn = sq
        R = 2048
        arena = sb("arena", [P, 14 * R])

        def region(a, n=1):
            return arena[:, a * R:(a + n) * R]

        g = region(0, 6)[:, 0:NF * S].rearrange("p (f s) -> p f s", s=S)
        sg = region(6).rearrange("p (b s) -> p b s", s=S)
        cv = region(8).rearrange("p (b s) -> p b s", s=S)
        rows = region(9, 2).rearrange("p (t c) -> p t c", c=D)
        stage = region(13)[:, 0:NPT * P].rearrange("p (t c) -> p t c", c=P)

        bank = [ctx.enter_context(nc.psum_tensor(f"bank{b}", [P, S], F32)) for b in range(8)]

        def panel(w, k, c0, cols, step=0, row0=0, nrow=P, first=0, pitch=None):
            def src(i):
                at = c0 + i * step if step else c0
                return w[row0:row0 + k * nrow, bass.ds(at, cols)].rearrange("(k p) n -> p k n", p=nrow)
            return (nrow, first, (k, cols, pitch), src)

        def features(b, j, cols, at, width=P, k=KD, nk=P, x0=0, by="dve"):
            return {"bank": b, "rows": width, "cols": S, "token": False, "by": by,
                    "terms": [(j, nk, q * cols + at, width, x0 + q) for q in range(k)]}

        def up_stage(k, w, f, by=("act", "act", "dve", "dve")):
            return Dense(f"ffn{k}_up", NF // 2, [[panel(w, KD, c + P * u, P, 2 * P)] for c in (0, FF) for u in range(2)],
                         [features(b, b, P, 0, by=by[b]) for b in range(4)], (xH, xL), xfill(f))

        def down_stage(k, w, need):
            panels, tiles = [], []
            for m in range(2):
                terms, first = [], 0
                for j, n in enumerate((6, 6, 5, 5)):
                    panels.append([panel(w, n, P * m, P, 2 * P, row0=first * P)])
                    terms += [(4 * m + j, P, q * P, P, first + q) for q in range(n)]
                    first += n
                tiles.append({"bank": m, "rows": P, "cols": S, "token": False, "by": "dve", "terms": terms})
            return Dense(f"ffn{k}_down", KD // 2, panels, tiles, (g,), need)

        def hidden(k):
            return ("cv_prod", NF * (k - 1) + CREDIT) if k >= 2 else None

        def ffn(k, w_in, w_out, f):
            up = up_stage(k, w_in, f) if k < 2 else up_stage(k, w_in, f, ("dve",) * 4)
            return [up, down_stage(k, w_out, hidden(k))]

        def tokens(b, j, cols, t, by="dve"):
            return {"bank": b, "rows": P, "at": 0, "token": True, "by": by, "x": slice(t * P, (t + 1) * P),
                    "terms": [(j + q // 4, P, q % 4 * cols, cols, q) for q in range(KD)]}

        def halves_of(w, c, cols):
            return [[panel(w, 4, c, cols, row0=4 * P * u)] for u in range(2)]

        def mem_stage(l):
            w = A["w_mem_kv_2"][l]
            tiles = [features(u, u, P, 0, by="act") for u in range(2)]
            for tile in tiles:
                tile["cols"] = M
            return Dense(f"mem{l}_kv", 1, [[panel(w, KD, P * u, P)] for u in range(2)] + halves_of(w, M, M),
                         tiles + [tokens(2 + u, 2, M, u, by="dve") for u in range(2)],
                         (mem_sq,), ("mem_dve", 13 * (l + 1)))

        def out_stage(name, w, f):
            return Dense(name, 2, [[panel(w, KD, P * j, P, 4 * P)] for j in range(4)],
                         [features(b, b, P, 0) for b in range(4)], (xH, xL), xfill(f))

        mem_sq = region(11).rearrange("p (k m) -> p k m", m=M)
        mixed = arena[:, 5 * R + R // 2:8 * R].rearrange("p (t s) -> p t s", s=S)
        XFILL = [8, 8, 8, 8, 8, 0, 8, 8, 8, 14, 8]

        def xfill(k):
            return ("x_ready", sum(XFILL[:k + 1]))

        w_mix = A["w_mix_in"][0]
        stages = ffn(0, A["ffn1_w_in"][0], A["ffn1_w_out"][0], 0)
        stages += [
            Dense("mix_ba", 1, [[panel(w_mix, KD, 7 * 512, 8)]],
                  [features(0, 0, 8, 0, width=4, by="act"), features(1, 0, 8, 4, width=4, by="dve")],
                  (xH, xL), xfill(1)),
            Dense("mix_in", 7, [[panel(w_mix, KD, P * j, P, 4 * P)] for j in range(4)],
                  [features(b, b, P, 0, by=("act", "dve")[b % 2]) for b in range(4)], (xH, xL), xfill(1)),
            out_stage("mix_out", A["w_mix_out"][0], 2)]
        stages += ffn(1, A["ffn2_w_in"][0], A["ffn2_w_out"][0], 3)
        w_gla = A["gla_w_in_2"][0]
        GQ, GK, GV, GG, GR, GM = 0, 384, 768, 1536, 2304, 2320
        stages += [
            mem_stage(0),
            Dense("gla_rest", 1, [[panel(w_gla, KD, GR, 16)]] + [[panel(w_gla, KD, GM + P * u, P)] for u in range(2)],
                  [features(0, 0, 16, 0, width=16, by="act")] +
                  [features(1 + u, 1 + u, P, 0, by="dve") for u in range(2)], (xH, xL), xfill(4)),
            Dense("gla_q", 1, [[panel(w_gla, KD, GQ + 96 * j, 96)] for j in range(4)],
                  [features(b, b, 96, 0, width=96, by="act") for b in range(4)], (xH, xL), xfill(4)),
            Dense("gla_k", 1, [[panel(w_gla, KD, GK + 96 * j, 96)] for j in range(4)],
                  [features(b, b, 96, 0, width=96, by="dve") for b in range(4)], (xH, xL), xfill(4)),
            Dense("gla_v", 1, [p for j in range(3) for p in halves_of(w_gla, GV + 256 * j, 256)],
                  [tokens(t, 2 * j, 256, t, by=("act", "dve")[t % 2]) for j in range(3) for t in range(TT)],
                  (xH, xL), xfill(4)),
            Dense("gla_g", 2, [[panel(w_gla, KD, GG + 96 * j, 96, 384)] for j in range(4)],
                  [features(b, b, 96, 0, width=96, by="act") for b in range(4)],
                  (xH, xL), xfill(4)),
            Dense("gla_out", 4, [p for j in range(2) for p in (
                                 [panel(A["w_out_2"][0], 8, P * j, P, 2 * P, nrow=96)],
                                 [panel(A["w_out_2"][0], 2, P * j, P, 2 * P, row0=768)])],
                  [{"bank": j, "rows": P, "cols": S, "token": False, "by": "dve",
                    "terms": [(2 * j, 96, q * P, P, q) for q in range(8)] +
                             [(2 * j + 1, P, q * P, P, 8 + q) for q in range(2)]} for j in range(2)],
                  (mixed,), ("mixed", 10))]
        stages += ffn(2, A["w_up_2"][0], A["w_down_2"][0], 6)
        w_kv, w_nsa = A["w_kv_shared_2"], A["nsa_w_in_2"][0]

        def head_pair(t):
            first = t + 3 * (t // 3)
            return [panel(w_nsa, KD, 64 * (first + 3 * half), 64, first=64 * half, pitch=P) for half in range(2)]

        stages += [
            mem_stage(1),
            Dense("kv_f", 1, [[panel(w_kv, KD, c + P * u, P)] for c in (0, 256, 512, 1024) for u in range(2)],
                  [features(t % 4, t, P, 0, by=("act", "dve")[t % 2]) for t in range(8)],
                  (xH, xL), xfill(7)),
            Dense("kv_t", 1, [p for c in (768, 1280) for p in halves_of(w_kv, c, 256)],
                  [tokens(t, 2 * j, 256, t, by=("act", "dve")[t % 2]) for j in range(2) for t in range(TT)],
                  (xH, xL), xfill(7)),
            Dense("nsa_q", 1, [head_pair(t) for t in range(6)],
                  [features(t % 4, t, P, 0, by=("act", "dve")[t % 2]) for t in range(6)],
                  (xH, xL), xfill(8)),
            Dense("nsa_g", 1, halves_of(w_nsa, 768, 36) + [[panel(w_nsa, KD, 804 + P * u, P)] for u in range(2)],
                  [tokens(t, 0, 36, t, by="act") for t in range(TT)] +
                  [features(t, 2 + t, P, 0, by="dve") for t in range(2)], (xH, xL), xfill(8)),
            out_stage("nsa_out", A["w_out_2"][1], 9)]
        stages += ffn(3, A["w_up_2"][1], A["w_down_2"][1], 10)
        plan = Plan(stages)
        nc_block = ctx.enter_context(nc.Block())

        FILLS = ["norm", "norm", "mixer", "norm", "norm", "mixer", "norm", "norm", "norm", "mixer", "norm"]

        def xbase(f):
            return sum(XFILL[:f])

        def nfill(f):
            return sum(n for n, kind in zip(XFILL[:f], FILLS[:f]) if kind == "norm")

        def h_from(name):
            s = plan.stages[name]
            n = len(s.tiles)
            return lambda k: (sem("evac_dve"), plan.evac(s, k // n, k % n))

        def rounds(eng, s, body):
            if s.iters == 1:
                body(0)
            else:
                with eng.Fori(0, s.iters) as i:
                    body(i)

        def load_panels(sp, name):
            s = plan.stages[name]

            def body(i):
                for j, dmas in enumerate(s.panels):
                    if not isinstance(i, int) or s.panel0 + i * len(s.panels) + j >= SLOTS:
                        before = plan.ahead(s, i, j, -SLOTS)
                        if before[0].split:
                            sp.wait_ge(sem("w_lo"), plan.split(*before))
                        else:
                            sp.wait_ge(sem("pe_segment"), plan.used(*before))
                    for nrow, first, shape, src in dmas:
                        k, cols, pitch = shape
                        if pitch:
                            dst = raw[0:nrow, s.slot[j], 0:k * pitch].rearrange("p (k n) -> p k n", n=pitch)
                            dst = dst[:, :, first:first + cols]
                        else:
                            dst = raw[0:nrow, s.slot[j], first:first + k * cols]
                            dst = dst.rearrange("p (k n) -> p k n", n=cols)
                        sp.dma_start(dst, src(i))\
                          .then_inc(sem(f"w_landed{s.slot[j]}"), 16)
            body(0)
            if s.iters > 1:
                with sp.Fori(1, s.iters) as i:
                    body(i)

        def extent(s, j):
            return max(k * (pitch or cols) for _, _, (k, cols, pitch), _ in s.panels[j])

        def half_slot(s, i, j):
            return (s.split0 + j) % 2

        def split_hi(act, s, i, j):
            k, n = s.slot[j], extent(s, j)
            act.wait_ge(sem(f"w_landed{k}"), plan.landed(s, i, j))
            before = two_before(s, i, j)
            if before:
                act.wait_ge(sem("pe_segment"), plan.used(*before))
            nc.scalar.activation(wH[:, half_slot(s, i, j), 0:n], raw[:, k, 0:n], ACT.Copy).then_inc(sem("w_hi"), 1)

        def two_before(s, i, j):
            if not isinstance(i, int) or i * len(s.panels) + j >= 2:
                step, k = divmod(j - 2, len(s.panels))
                return s, i + step, k
            split = [(q, a, b) for q in plan.order if q.split and q.panel0 < s.panel0
                     for a in range(q.iters) for b in range(len(q.panels))] + [(s, 0, 0)] * j
            return split[-2] if len(split) >= 2 else None

        def split_first(act, name):
            split_hi(act, plan.stages[name], 0, 0)

        def split_ahead(act, s, i, j):
            if not isinstance(i, int):
                split_hi(act, *plan.ahead(s, i, j, 1))
            elif s.panel0 + i * len(s.panels) + j + 1 < plan.panels:
                q = plan.ahead(s, i, j, 1)
                if q[0].split:
                    split_hi(act, *q)

        def split_lo(pool, name):
            s = plan.stages[name]
            if not s.split:
                return

            def body(i):
                for j in range(len(s.panels)):
                    k, h, n = s.slot[j], half_slot(s, i, j), extent(s, j)
                    pool.wait_ge(sem("w_hi"), plan.split(s, i, j))
                    nc.gpsimd.tensor_tensor(wL[:, h, 0:n], raw[:, k, 0:n], wH[:, h, 0:n].bitcast(F32), ALU.subtract)\
                      .then_inc(sem("w_lo"), 1)
            rounds(pool, s, body)

        GRADUAL = ("ffn0_up", "mix_ba", "ffn1_up", "gla_rest", "ffn2_up", "kv_f", "nsa_q", "ffn3_up")

        def dense_pe(pe, name):
            s = plan.stages[name]
            xh, xl = s.xs[0], s.xs[-1]
            gradual = name in GRADUAL
            if gradual:
                pass
            elif s.need:
                pe.wait_ge(sem(s.need[0]), s.need[1])
            else:
                p = plan.order[plan.order.index(s) - 1]
                pe.wait_ge(sem("evac_dve"), plan.evac(p, p.iters - 1, len(p.tiles) - 1))
            for by, value in s.before.values():
                pe.wait_ge(sem("evac_" + by), value)

            def body(i):
                seen = -1
                for t, tile in enumerate(s.tiles):
                    acc = bank[tile["bank"]]
                    earlier = [u for u in range(t) if s.tiles[u]["bank"] == tile["bank"]]
                    later = [u for u in range(t, len(s.tiles)) if s.tiles[u]["bank"] == tile["bank"]]
                    if earlier:
                        pe.wait_ge(sem("evac_" + s.tiles[earlier[-1]]["by"]), plan.evac(s, i, earlier[-1]))
                    elif s.iters > 1:
                        pe.wait_ge(sem("evac_" + s.tiles[later[-1]]["by"]), plan.evac(s, i - 1, later[-1]))
                    terms = tile["terms"]
                    for q, (j, nrow, first, width, x) in enumerate(terms):
                        if j > seen:
                            if s.split:
                                pe.wait_ge(sem("w_lo"), plan.split(s, i, j))
                            else:
                                pe.wait_ge(sem(f"w_landed{s.slot[j]}"), plan.landed(s, i, j))
                            seen = j
                        if gradual and t == 0:
                            pe.wait_ge(sem(s.need[0]), s.need[1] - KD + x + 1)
                        a, z = q == 0, q == len(terms) - 1
                        if not s.split:
                            w = raw[0:nrow, s.slot[j], first:first + width]
                            if tile["token"]:
                                last = pe.matmul(acc[0:tile["rows"], 0:width], xh[0:nrow, x, tile["x"]], w,
                                                 start=a, stop=z)
                            else:
                                last = pe.matmul(acc[0:width, 0:tile["cols"]], w, xh[0:nrow, x, 0:tile["cols"]],
                                                 start=a, stop=z)
                            if z or terms[q + 1][0] != j:
                                last.then_inc(sem("pe_segment"), 1)
                            continue
                        h = half_slot(s, i, j)
                        wh, wl = wH[0:nrow, h, first:first + width], wL[0:nrow, h, first:first + width]
                        if tile["token"]:
                            o = acc[0:tile["rows"], tile["at"]:tile["at"] + width]
                            xa, xb = xh[0:nrow, x, tile["x"]], xl[0:nrow, x, tile["x"]]
                            pe.matmul(o, xa, wh, start=a, stop=False)
                            pe.matmul(o, xa, wl, start=False, stop=False)
                            last = pe.matmul(o, xb, wh, start=False, stop=z)
                        else:
                            o = acc[0:width, 0:tile["cols"]]
                            xa, xb = xh[0:nrow, x, 0:tile["cols"]], xl[0:nrow, x, 0:tile["cols"]]
                            pe.matmul(o, wh, xa, start=a, stop=False)
                            pe.matmul(o, wh, xb, start=False, stop=False)
                            last = pe.matmul(o, wl, xa, start=False, stop=z)
                        if z or terms[q + 1][0] != j:
                            last.then_inc(sem("pe_segment"), 1)
            rounds(pe, s, body)

        def dense_act(act, name, evac):
            s = plan.stages[name]

            def body(i):
                for j in range(len(s.panels)):
                    if s.split:
                        split_ahead(act, s, i, j)
                    for t, tile in enumerate(s.tiles):
                        if max(term[0] for term in tile["terms"]) == j:
                            evac(act, s, i, t)
            if s.iters > 1:
                with act.Fori(0, s.iters - 1) as i:
                    body(i)
            body(s.iters - 1)

        def dense_dve(dve, name, evac):
            s = plan.stages[name]

            def body(i):
                for t in range(len(s.tiles)):
                    evac(dve, s, i, t)
            rounds(dve, s, body)

        def load_table(act, n, function):
            if n:
                act.wait_ge(sem("table"), n)
            nc.scalar.activation(table[:], eps[:], function).then_inc(sem("table"), 1)

        def nothing(eng, s, i, t):
            pass

        def up_evac_act(act, s, i, t):
            if t < 2:
                act.wait_ge(sem("evac_dve"), plan.evac(s, i - 1, t + 2))
                act.wait_ge(sem("pe_segment"), plan.full(s, i, t))
                nc.scalar.activation(sg[:, t, :], bank[t][:], ACT.Silu).then_inc(sem("evac_act"), 1)

        def up_evac_dve(dve, s, i, t):
            if t < 2:
                return
            dve.wait_ge(sem("pe_segment"), plan.full(s, i, t))
            dve.wait_ge(sem("evac_act"), plan.evac(s, i, t - 2))
            nc.vector.tensor_tensor(g[:, bass.ds(2 * i + t - 2, 1), :], bank[t][:].rearrange("p (o s) -> p o s", o=1),
                                    sg[:, t - 2:t - 1, :], ALU.mult).then_inc(sem("evac_dve"), 1)

        def residual(scale):
            def evac(dve, s, i, t):
                dve.wait_ge(sem("pe_segment"), plan.full(s, i, t))
                h = hT[:, bass.ds(len(s.tiles) * i + t, 1), :]
                b = bank[s.tiles[t]["bank"]][:].rearrange("p (o s) -> p o s", o=1)
                nc.vector.scalar_tensor_tensor(out=h, in0=b, scalar=scale, in1=h, op0=ALU.mult, op1=ALU.add)\
                  .then_inc(sem("evac_dve"), 1)
            return evac

        def norm_act(act, r, ready):
            for k in range(KD):
                act.wait_ge(*ready(k))
                if k >= 2:
                    act.wait_ge(sem("sq_added"), 7 * r + max(1, k - 2))
                nc.scalar.activation(sq[:, k % 2, :], hT[:, k, :], ACT.Square).then_inc(sem("sq"), 1)
            act.wait_ge(sem("sq_summed"), r + 1)
            nc.scalar.activation(rstd[:], bank[7][:], ACT.Ln, bias=eps[:], scale=1.0 / D).then_inc(sem("rms"), 1)
            act.wait_ge(sem("rms"), 2 * r + 1)
            nc.scalar.activation(rstd[:], rstd[:], ACT.Exp, scale=-0.5).then_inc(sem("rms"), 1)

        def norm_pool(pool, r):
            for k in range(1, KD):
                pool.wait_ge(sem("sq"), 8 * r + k + 1)
                if k >= 2:
                    pool.wait_ge(sem("sq_added"), 7 * r + k - 1)
                nc.gpsimd.tensor_tensor(rstd[:], sq[:, 0, :] if k == 1 else rstd[:], sq[:, k % 2, :], ALU.add)\
                  .then_inc(sem("sq_added"), 1)

        def norm_pe(pe, r):
            pe.wait_ge(sem("sq_added"), 7 * r + 7)
            pe.matmul(bank[7][:], ones[:], rstd[:], start=True, stop=True).then_inc(sem("sq_summed"), 1)

        def norm_dve(dve, r):
            dve.wait_ge(sem("rms"), 2 * r + 2)

        def scaled_act(act, f, free=None):
            if free:
                act.wait_ge(sem("pe_segment"), free)
            for k in range(KD):
                act.wait_ge(sem("xn"), nfill(f) + k + 1)
                nc.scalar.activation(xH[:, k, :], xn[:, k % 2, :], ACT.Copy).then_inc(sem("x_hi"), 1)

        def scaled_dve(dve, f, gain, at=0):
            def norm(k):
                if k >= 2:
                    dve.wait_ge(sem("x_ready"), xbase(f) + k - 1)
                nc.vector.scalar_tensor_tensor(out=xn[:, k % 2, :], in0=hT[:, k, :], in1=rstd[:], op0=ALU.mult,
                                               scalar=column(gain, at + k), op1=ALU.mult).then_inc(sem("xn"), 1)
            norm(0)
            for k in range(KD):
                if k + 1 < KD:
                    norm(k + 1)
                dve.wait_ge(sem("x_hi"), xbase(f) + k + 1)
                nc.vector.tensor_tensor(xL[:, k, :], xn[:, k % 2, :], xHf[:, k, :], ALU.subtract)\
                  .then_inc(sem("x_ready"), 1)

        def column(name, k=0):
            c = PAR_AT[name][0] + k
            return par[:, c:c + 1]

        def load_sp(sp):
            for name, (first, n) in PAR_AT.items():
                src = A[name]
                dims = " ".join("abcd"[:len(src.shape)])
                flat = src.rearrange(f"{dims} -> ({dims})") if len(src.shape) > 1 else src
                flat = flat.rearrange("(r c) -> r c", c=P)
                at = 0
                while at < n:
                    tile, row = divmod(first + at, P)
                    k = min(n - at, P - row)
                    sp.dma_start(stage[row:row + k, tile, :], flat[at:at + k]).then_inc(sem("par_staged"), 16)
                    at += k

        def constants_pool(pool):
            nc.gpsimd.memset(ident[:], 0.0).then_inc(sem("zeroed"), 1)
            nc.gpsimd.memset(ones[:], 1.0).then_inc(sem("const"), 1)
            nc.gpsimd.memset(eps[:], EPS).then_inc(sem("const"), 1)
            pool.wait_ge(sem("zeroed"), 1)
            nc.gpsimd.affine_select(out=ident[:], in_=ident[:], compare_op=ALU.not_equal, fill=1.0, base=0,
                                    pattern=[[-1, P]], channel_multiplier=1).then_inc(sem("const"), 1)

        NCONST = 3

        def turn(pe, o, i, k=P):
            return pe.transpose(o, i, ident[0:k, 0:k])

        def load_pe(pe):
            pe.wait_ge(sem("const"), NCONST)
            pe.wait_ge(sem("x_landed"), 16)
            for k in range(KD):
                if k >= 4:
                    pe.wait_ge(sem("h_act" if k % 2 == 0 else "h_dve"), (k - 4) // 2 + 1)
                for t in range(TT):
                    last = turn(pe, bank[4 + k % 4][:, t * P:(t + 1) * P], rows[:, t, k * P:(k + 1) * P])
                last.then_inc(sem("x_turned"), 1)
            pe.wait_ge(sem("par_staged"), 16 * NPAR_DMA)
            for t in range(NPT):
                k = min(P, NPAR - t * P)
                last = turn(pe, bank[t // 4][:, t % 4 * P:t % 4 * P + k], stage[0:k, t, :], k)
            last.then_inc(sem("par_turned"), 1)
            pe.wait_ge(sem("h_dve"), KD // 2)

        def load_act(act):
            act.sem_inc(sem("evac_act"), CREDIT_EV)
            for k in range(0, KD, 2):
                act.wait_ge(sem("x_turned"), k + 1)
                nc.scalar.activation(hT[:, k, :], bank[4 + k % 4][:], ACT.Copy).then_inc(sem("h_act"), 1)

        def load_dve(dve):
            dve.sem_inc(sem("evac_dve"), CREDIT_EV)
            dve.sem_inc(sem("pe_segment"), CREDIT_PE)
            dve.sem_inc(sem("cv_prod"), CREDIT)
            for k in range(1, KD, 2):
                dve.wait_ge(sem("x_turned"), k + 1)
                nc.vector.tensor_copy(hT[:, k, :], bank[4 + k % 4][:]).then_inc(sem("h_dve"), 1)
            dve.wait_ge(sem("par_turned"), 1)
            for t in range(0, NPT, 4):
                n = min(4 * P, NPAR - t * P)
                nc.vector.tensor_copy(par[:, t * P:t * P + n], bank[t // 4][:, 0:n]).then_inc(sem("par"), 1)
            dve.wait_ge(sem("par"), -(-NPT // 4))

        ab = region(13)[0:4].rearrange("p (r s) -> p r s", s=S)
        U = region(0, 14).rearrange("p (t s) -> p t s", s=S)
        B = region(0, 14).rearrange("p (r b c) -> p r b c", b=16, c=P)
        H4 = region(0, 14).rearrange("p (r h s) -> p r h s", h=4, s=S)
        Q, K, V, Z = 7, 8, 9, 6
        GBC, DEC, KB, NT, AT = 10, 11, 12, 13, 12
        T0, T1, YR, NM = 1, 2, 3, 4
        KBG, KDEC, UU, WT, OT, QD = 8, 11, 3, 4, 13, 10
        BETA, GC, EG, BG, DL, GL = range(6)
        HD = 128

        def constants2_pool(pool):
            nc.gpsimd.memset(ones64[:], 0.0).then_inc(sem("zeroed"), 1)
            nc.gpsimd.memset(lvl[:], 0.0).then_inc(sem("zeroed"), 1)
            pool.wait_ge(sem("zeroed"), 3)
            for half in range(2):
                nc.gpsimd.memset(ones64[64 * half:64 * half + 64, 64 * half:64 * half + 64], 1.0)\
                  .then_inc(sem("const2"), 1)
                pool.wait_ge(sem("const2"), half + 1)
            for n in range(7):
                w = 1 << n
                v = lvl[:, n, :].rearrange("p (b h r) -> p b h r", h=2, r=w)[:, :, 1, :]
                nb = P // (2 * w)
                nc.gpsimd.memset(v, 1.0).then_inc(sem("lvl"), 1)
                pool.wait_ge(sem("lvl"), 3 * n + 1)
                nc.gpsimd.affine_select(out=v, in_=v, compare_op=ALU.is_ge, fill=0.0, base=0,
                                        pattern=[[-2 * w, nb], [0, w]], channel_multiplier=1).then_inc(sem("lvl"), 1)
                pool.wait_ge(sem("lvl"), 3 * n + 2)
                nc.gpsimd.affine_select(out=v, in_=v, compare_op=ALU.is_ge, fill=0.0, base=w - 1,
                                        pattern=[[2 * w, nb], [0, w]], channel_multiplier=-1)\
                  .then_inc(sem("lvl"), 1)

        def ba_evac_act(act, s, i, t):
            if t == 0:
                act.wait_ge(sem("pe_segment"), plan.full(s, i, t))
                nc.scalar.activation(ab[:, 0, :], bank[0][0:4, :], ACT.Sigmoid).then_inc(sem("evac_act"), 1)
            else:
                act.wait_ge(sem("hv_landed"), 32)
                nc.scalar.activation(hv[:, 2:3], hv[:, 0:1], ACT.Exp).then_inc(sem("decay_act"), 1)
                act.wait_ge(sem("evac_dve"), plan.evac(s, i, t))
                nc.scalar.activation(ab[:, 2, :], ab[:, 1, :], ACT.Abs).then_inc(sem("decay_act"), 1)
                act.wait_ge(sem("decay_act"), 2)
                nc.scalar.activation(ab[:, 2, :], ab[:, 2, :], ACT.Exp, scale=-1.0).then_inc(sem("decay_act"), 1)
                act.wait_ge(sem("decay_act"), 3)
                nc.scalar.activation(ab[:, 2, :], ab[:, 2, :], ACT.Ln, bias=1.0).then_inc(sem("decay_act"), 1)

        def ba_evac_dve(dve, s, i, t):
            if t == 0:
                return
            dve.wait_ge(sem("pe_segment"), plan.full(s, i, t))
            dve.wait_ge(sem("hv_landed"), 32)
            nc.vector.tensor_scalar(ab[:, 1, :], bank[1][0:4, :], hv[:, 1:2], None, ALU.add)\
              .then_inc(sem("evac_dve"), 1)
            dve.wait_ge(sem("decay_act"), 1)
            nc.vector.tensor_scalar(hv[:, 3:4], hv[:, 2:3], -1.0, None, ALU.mult).then_inc(sem("decay_dve"), 1)
            dve.wait_ge(sem("decay_act"), 4)
            nc.vector.scalar_tensor_tensor(out=ab[:, 1, :], in0=ab[:, 1, :], scalar=0.0, in1=ab[:, 2, :],
                                           op0=ALU.max, op1=ALU.add).then_inc(sem("decay_dve"), 1)
            dve.wait_ge(sem("decay_dve"), 2)
            nc.vector.tensor_scalar(ab[:, 2, :], ab[:, 1, :], hv[:, 3:4], None, ALU.mult)\
              .then_inc(sem("decay_dve"), 1)
            dve.wait_ge(sem("decay_dve"), 3)
            for c in range(TT):
                nc.vector.tensor_tensor_scan(ab[:, 3, c * P:(c + 1) * P], ones[0:4, 0:P],
                                             ab[:, 2, c * P:(c + 1) * P], 0.0, ALU.mult, ALU.add)\
                  .then_inc(sem("decay_dve"), 1)

        DECAY = 3 + TT

        def in_evac(eng_name):
            def evac(eng, s, i, t):
                if s.tiles[t]["by"] != eng_name:
                    return
                eng.wait_ge(sem("pe_segment"), plan.full(s, i, t))
                o = U[:, bass.ds(4 * i + t, 1), :]
                b = bank[t][:].rearrange("p (o s) -> p o s", o=1)
                if eng_name == "act":
                    nc.scalar.activation(o, b, ACT.Copy).then_inc(sem("evac_act"), 1)
                else:
                    nc.vector.tensor_copy(o, b).then_inc(sem("evac_dve"), 1)
            return evac

        def stage_end(name):
            s = plan.stages[name]
            ends = {}
            for t, tile in enumerate(s.tiles):
                ends[tile["by"]] = plan.evac(s, s.iters - 1, t)
            return [(sem("evac_" + by), v) for by, v in ends.items()]

        def wait_all(eng, pairs):
            for p in pairs:
                eng.wait_ge(*p)

        def squares(act, n, src):
            if n >= 2:
                act.wait_ge(sem("sum_mix"), n - 1)
            nc.scalar.activation(sq[:, n % 2, :], src, ACT.Square).then_inc(sem("sq_mix"), 1)

        def inverse_root(act, n, tile):
            act.wait_ge(sem("norm_mix"), n + 1)
            nc.scalar.activation(tile, tile, ACT.Exp, scale=-0.5).then_inc(sem("inv_mix"), 1)

        def sum_features(pe, n, b, weights):
            pe.wait_ge(sem("sq_mix"), n + 1)
            pe.matmul(b[:], weights[:], sq[:, n % 2, :], start=True, stop=True).then_inc(sem("sum_mix"), 1)

        def blocks(ap, n=4):
            return ap.rearrange("p (b c) -> p b c", b=n)

        def repeat(ap, n):
            return ap.unsqueeze(1).broadcast_to([P, n, P])

        OUTB = [0, 1, 6, 7]
        LEVELS = 7

        def gdn_act(act):
            wait_all(act, stage_end("mix_in"))
            for t in range(12):
                nc.scalar.activation(U[:, 28 + t, :], U[:, 12 + t, :], ACT.Copy,
                                     scale=column("gdn_conv_w", 36 + t)).then_inc(sem("qkv_tap"), 1)
                if t % 3 == 2:
                    c = t // 3
                    act.wait_ge(sem("sc_in"), c + 1)
                    nc.scalar.activation(U[:, 4 + c, :], U[:, 8 + c, :], ACT.Copy,
                                         scale=column("conv_short_w", 8 + c)).then_inc(sem("sc_tap"), 1)
            nc.scalar.activation(H4[:, Z], H4[:, Z], ACT.Silu).then_inc(sem("z_silu"), 1)
            for t in range(12):
                act.wait_ge(sem("qkv_conv"), 12 * (t // 4 + 1))
                nc.scalar.activation(U[:, 28 + t, :], U[:, 28 + t, :], ACT.Silu).then_inc(sem("qkv_silu"), 1)
            for t in range(8):
                act.wait_ge(sem("qkv_silu"), t + 1)
                squares(act, t, U[:, 28 + t, :])
            for t in range(4):
                act.wait_ge(sem("sc_y"), t + 1)
                squares(act, 8 + t, U[:, t, :])
                if t == 0:
                    for u in range(8):
                        act.wait_ge(sem("sum_mix"), u + 1)
                        nc.scalar.activation(U[:, 12 + u, :], bank[u][:], ACT.Ln, bias=eps[:], scale=1.0)\
                          .then_inc(sem("norm_mix"), 1)
                    for u in range(8):
                        inverse_root(act, u, U[:, 12 + u, :])
            for t in range(4):
                act.wait_ge(sem("sum_mix"), 8 + t + 1)
                nc.scalar.activation(U[:, 4 + t, :], bank[t][:], ACT.Ln, bias=eps[:], scale=1.0 / 64)\
                  .then_inc(sem("norm_mix"), 1)
            for t in range(4):
                inverse_root(act, 8 + t, U[:, 4 + t, :])
            for h in range(4):
                act.wait_ge(sem("gdn_sum"), h + 1)
                nc.scalar.activation(H4[:, GBC, h], bank[4 + h][:], ACT.Copy).then_inc(sem("gbc"), 1)
            act.wait_ge(sem("gdn_sum"), 9)
            nc.scalar.activation(col[:, BETA:GC + 1, :].rearrange("p a (h c) -> p a h c", h=4),
                                 bank[7][:, 0:32].rearrange("p (a c h) -> p a h c", a=2, c=4),
                                 ACT.Copy).then_inc(sem("cols"), 1)
            act.wait_ge(sem("cols"), 1)
            nc.scalar.activation(col[:, EG, :], col[:, GC, :], ACT.Exp).then_inc(sem("cols"), 1)
            act.wait_ge(sem("gbc"), 4)
            nc.scalar.activation(col[:, GL, :].rearrange("p (h c) -> p h c", h=4),
                                 H4[:, GBC].rearrange("p h (c s) -> p h c s", s=P)[:, :, :, P - 1],
                                 ACT.Exp).then_inc(sem("cols"), 1)
            act.wait_ge(sem("col_dl"), 1)
            nc.scalar.activation(col[:, DL, :], col[:, DL, :], ACT.Exp).then_inc(sem("cols"), 1)
            act.wait_ge(sem("dec_arg"), 16)
            nc.scalar.activation(B[:, DEC], B[:, DEC], ACT.Exp).then_inc(sem("dec_exp"), 1)
            act.wait_ge(sem("cols"), 4)
            nc.scalar.activation(H4[:, GBC], H4[:, GBC], ACT.Exp).then_inc(sem("gbc_exp"), 1)
            for t in range(4):
                act.wait_ge(sem("sc_out"), t + 1)
                nc.scalar.activation(xH[:, t, :], U[:, t, :], ACT.Copy).then_inc(sem("x_hi"), 1)
            act.wait_ge(sem("cols"), 4)
            for h in range(4):
                act.wait_ge(sem("v_turned"), h + 1)
                for c in range(4):
                    nc.scalar.activation(B[:, V, 4 * h + c], bank[7][:, c * P:(c + 1) * P], ACT.Copy,
                                         scale=col[:, BETA, 4 * h + c:4 * h + c + 1]).then_inc(sem("vb"), 1)
            for n in range(1, LEVELS):
                for g in range(4):
                    act.wait_ge(sem("y_sum"), 4 * n + g + 1)
                    nc.scalar.activation(B[:, YR, 4 * g:4 * g + 4], blocks(bank[g % 2][:]), ACT.Copy)\
                      .then_inc(sem("y"), 1)
            for h in range(4):
                act.wait_ge(sem("uw_sum"), 4 + h + 1)
                nc.scalar.activation(H4[:, WT, h], bank[4 + h][:], ACT.Copy).then_inc(sem("wt"), 1)
            for c in range(TT):
                act.wait_ge(sem("o_sum"), c + 1)
                nc.scalar.activation(H4[:, OT, :, c * P:(c + 1) * P], blocks(bank[2 + c % 2][:]), ACT.Copy)\
                  .then_inc(sem("o_mix"), 1)
            act.wait_ge(sem("o_mix"), 4)
            for h in range(4):
                squares(act, 12 + h, H4[:, OT, h])
            for h in range(4):
                act.wait_ge(sem("sum_mix"), 12 + h + 1)
                nc.scalar.activation(U[:, 20 + h, :], bank[OUTB[h]][:], ACT.Ln, bias=eps[:], scale=1.0 / HD)\
                  .then_inc(sem("norm_mix"), 1)
            for h in range(4):
                inverse_root(act, 12 + h, U[:, 20 + h, :])
            for h in range(4):
                act.wait_ge(sem("gdn_out"), 4 + h + 1)
                nc.scalar.activation(xH[:, 4 + h, :], H4[:, OT, h], ACT.Copy).then_inc(sem("x_hi"), 1)

        def gdn_dve(dve):
            wait_all(dve, stage_end("mix_in"))
            for t in range(4):
                nc.vector.tensor_tensor(U[:, 8 + t, :], U[:, 4 + t, :], U[:, 8 + t, :], ALU.mult)\
                  .then_inc(sem("sc_in"), 1)
            n = 0
            for g in range(3):
                for tap in range(1, 4):
                    for t in range(4 * g, 4 * g + 4):
                        dve.wait_ge(sem("qkv_tap"), t + 1)
                        if tap > 1:
                            dve.wait_ge(sem("qkv_conv"), n - 3)
                        nc.vector.scalar_tensor_tensor(
                            out=U[:, 28 + t, tap:], in0=U[:, 12 + t, :S - tap],
                            scalar=column("gdn_conv_w", 12 * (3 - tap) + t), in1=U[:, 28 + t, tap:],
                            op0=ALU.mult, op1=ALU.add).then_inc(sem("qkv_conv"), 1)
                        n += 1
            for tap in range(1, 3):
                for t in range(4):
                    dve.wait_ge(sem("sc_tap"), t + 1)
                    if tap > 1:
                        dve.wait_ge(sem("sc_conv"), t + 1)
                    nc.vector.scalar_tensor_tensor(
                        out=U[:, 4 + t, tap:], in0=U[:, 8 + t, :S - tap],
                        scalar=column("conv_short_w", 4 * (2 - tap) + t), in1=U[:, 4 + t, tap:],
                        op0=ALU.mult, op1=ALU.add).then_inc(sem("sc_conv"), 1)
            for t in range(4):
                dve.wait_ge(sem("sc_conv"), 4 + t + 1)
                nc.vector.tensor_tensor(U[:, t, :], U[:, t, :], U[:, 4 + t, :], ALU.mult).then_inc(sem("sc_y"), 1)
            for t in range(8):
                dve.wait_ge(sem("inv_mix"), t + 1)
                nc.vector.scalar_tensor_tensor(out=U[:, 28 + t, :], in0=U[:, 28 + t, :],
                                               scalar=HD ** -0.5 if t < 4 else 1.0, in1=U[:, 12 + t, :],
                                               op0=ALU.mult, op1=ALU.mult).then_inc(sem("qk_unit"), 1)
            for h in range(4):
                dve.wait_ge(sem("gdn_sum"), 4 + h + 1)
                dve.wait_ge(sem("qk_unit"), 4 + h + 1)
                nc.vector.tensor_tensor(H4[:, KB, h], H4[:, K, h], bank[h][:], ALU.mult).then_inc(sem("kb"), 1)
            dve.wait_ge(sem("gbc"), 4)
            dve.wait_ge(sem("cols"), 1)
            nc.vector.tensor_tensor(col[:, DL, :].rearrange("p (h c) -> p h c", h=4),
                                    H4[:, GBC].rearrange("p h (c s) -> p h c s", s=P)[:, :, :, P - 1],
                                    col[:, GC, :].rearrange("p (h c) -> p h c", h=4), ALU.subtract)\
              .then_inc(sem("col_dl"), 1)
            for b in range(16):
                nc.vector.tensor_scalar(B[:, DEC, b], B[:, GBC, b], col[:, GC, b:b + 1], 0.0,
                                        ALU.subtract, ALU.min).then_inc(sem("dec_arg"), 1)
            dve.wait_ge(sem("cols"), 2)
            nc.vector.tensor_tensor(col[:, BG, :], col[:, BETA, :], col[:, EG, :], ALU.mult)\
              .then_inc(sem("col_bg"), 1)
            for t in range(4):
                dve.wait_ge(sem("inv_mix"), 8 + t + 1)
                nc.vector.scalar_tensor_tensor(out=U[:, t, :], in0=U[:, t, :], scalar=column("conv_out_norm", t),
                                               in1=U[:, 4 + t, :], op0=ALU.mult, op1=ALU.mult)\
                  .then_inc(sem("sc_out"), 1)
            for t in range(4):
                dve.wait_ge(sem("x_hi"), xbase(2) + t + 1)
                nc.vector.tensor_tensor(xL[:, t, :], U[:, t, :], xHf[:, t, :], ALU.subtract)\
                  .then_inc(sem("x_ready"), 1)
            dve.wait_ge(sem("dec"), 1)
            for h in range(4):
                dve.wait_ge(sem("gdn_sum"), 9 + h + 1)
                nc.vector.tensor_tensor(H4[:, NT, h], bank[h][:], H4[:, DEC, h], ALU.mult).then_inc(sem("nt"), 1)
            for h in range(4):
                dve.wait_ge(sem("gdn_sum"), 13 + h + 1)
                nc.vector.tensor_tensor(H4[:, AT, h], bank[4 + h][:], H4[:, DEC, h], ALU.mult).then_inc(sem("at"), 1)
            dve.wait_ge(sem("gbc_exp"), 1)
            nc.vector.tensor_tensor(H4[:, QD], H4[:, Q], H4[:, QD], ALU.mult).then_inc(sem("qd"), 1)
            dve.wait_ge(sem("at"), 4)
            dve.wait_ge(sem("cols"), 4)
            dve.wait_ge(sem("col_bg"), 1)
            for h in range(4):
                dve.wait_ge(sem("k_turned"), h + 1)
                for c in range(4):
                    b = 4 * h + c
                    nc.vector.tensor_scalar(B[:, KBG, b], bank[6][:, c * P:(c + 1) * P], col[:, BG, b:b + 1],
                                            None, ALU.mult)
                    nc.vector.tensor_scalar(B[:, KDEC, b], bank[6][:, c * P:(c + 1) * P], col[:, DL, b:b + 1],
                                            None, ALU.mult).then_inc(sem("kdec"), 1)
            for g in range(4):
                dve.wait_ge(sem("y_sum"), g + 1)
                nc.vector.scalar_tensor_tensor(out=B[:, T0, 4 * g:4 * g + 4], in0=blocks(bank[g % 2][:]), scalar=-1.0,
                                               in1=repeat(ident[:], 4), op0=ALU.mult, op1=ALU.add)\
                  .then_inc(sem("t_new"), 1)
                nc.vector.scalar_tensor_tensor(out=B[:, T1, 4 * g:4 * g + 4], in0=B[:, NM, 4 * g:4 * g + 4],
                                               scalar=-1.0, in1=repeat(ident[:], 4), op0=ALU.mult, op1=ALU.add)\
                  .then_inc(sem("tt_new"), 1)
            for n in range(1, LEVELS):
                for g in range(4):
                    if n < LEVELS - 1:
                        dve.wait_ge(sem("ty_sum"), 4 * (n - 1) + g + 1)
                        o = B[:, T0, 4 * g:4 * g + 4]
                        nc.vector.tensor_tensor(o, o, blocks(bank[2 + g % 2][:]), ALU.subtract)\
                          .then_inc(sem("t_new"), 1)
                    dve.wait_ge(sem("yt_sum"), 4 * (n - 1) + g + 1)
                    o = B[:, T1, 4 * g:4 * g + 4]
                    nc.vector.tensor_tensor(o, o, blocks(bank[4 + g % 2][:]), ALU.subtract)\
                      .then_inc(sem("tt_new"), 1)
            for h in range(4):
                dve.wait_ge(sem("uw_sum"), h + 1)
                nc.vector.tensor_copy(H4[:, UU, h], bank[h][:]).then_inc(sem("uu"), 1)
            VN, ST = H4[:, T0], H4[:, T1]
            dve.wait_ge(sem("uw_sum"), 8)
            for c in range(TT):
                u = B[:, UU, c:16:4]
                if c == 0:
                    dve.wait_ge(sem("uu"), 4)
                    nc.vector.tensor_copy(blocks(VN[:, 0]), u).then_inc(sem("vn"), 1)
                else:
                    dve.wait_ge(sem("ws_sum"), c)
                    nc.vector.tensor_tensor(blocks(VN[:, c % 2]), u, blocks(bank[c % 2][:]), ALU.subtract)\
                      .then_inc(sem("vn"), 1)
                if c == TT - 1:
                    break
                dve.wait_ge(sem("kv_sum"), c + 1)
                for h in range(4):
                    o, b = ST[:, c % 2, h * P:(h + 1) * P], bank[4 + c % 2][:, h * P:(h + 1) * P]
                    if c == 0:
                        nc.vector.tensor_copy(o, b).then_inc(sem("state"), 1)
                    else:
                        if h == 0:
                            dve.wait_ge(sem("state"), 4 * c)
                        nc.vector.scalar_tensor_tensor(out=o, in0=ST[:, (c - 1) % 2, h * P:(h + 1) * P],
                                                       scalar=col[:, GL, 4 * h + c:4 * h + c + 1], in1=b,
                                                       op0=ALU.mult, op1=ALU.add).then_inc(sem("state"), 1)
            for h in range(4):
                dve.wait_ge(sem("inv_mix"), 12 + h + 1)
                nc.vector.scalar_tensor_tensor(out=H4[:, OT, h], in0=H4[:, OT, h], scalar=column("gdn_out_norm"),
                                               in1=U[:, 20 + h, :], op0=ALU.mult, op1=ALU.mult)\
                  .then_inc(sem("gdn_out"), 1)
            dve.wait_ge(sem("z_silu"), 1)
            for h in range(4):
                dve.wait_ge(sem("gdn_out"), h + 1)
                nc.vector.tensor_tensor(H4[:, OT, h], H4[:, OT, h], H4[:, Z, h], ALU.mult).then_inc(sem("gdn_out"), 1)
            for h in range(4):
                dve.wait_ge(sem("x_hi"), xbase(2) + 4 + h + 1)
                nc.vector.tensor_tensor(xL[:, 4 + h, :], H4[:, OT, h], xHf[:, 4 + h, :], ALU.subtract)\
                  .then_inc(sem("x_ready"), 1)

        def gdn_pool(pool):
            pool.wait_ge(sem("dec_exp"), 1)
            nc.gpsimd.affine_select(out=B[:, DEC], in_=B[:, DEC], compare_op=ALU.is_ge, fill=0.0, base=0,
                                    pattern=[[0, 16], [1, P]], channel_multiplier=-1).then_inc(sem("dec"), 1)
            pool.wait_ge(sem("nt"), 4)
            for n in range(LEVELS):
                if n >= 2:
                    pool.wait_ge(sem("y_sum"), 4 * (n - 1))
                    pool.wait_ge(sem("tt_new"), 4)
                nc.gpsimd.tensor_tensor(B[:, NM + n % 2], B[:, NT], repeat(lvl[:, n, :], 16), ALU.mult)\
                  .then_inc(sem("nm"), 1)

        def gdn_pe(pe):
            wait_all(pe, stage_end("mix_in"))
            pe.wait_ge(sem("const2"), 2)
            for t in range(8):
                sum_features(pe, t, bank[t], ones)
            for t in range(4):
                pe.wait_ge(sem("norm_mix"), t + 1)
                sum_features(pe, 8 + t, bank[t], ones64)
            pe.wait_ge(sem("decay_dve"), DECAY)
            pe.wait_ge(sem("evac_act"), plan.evac(plan.stages["mix_ba"], 0, 0))
            for h in range(4):
                pe.wait_ge(sem("norm_mix"), 4 + h + 1)
                pe.matmul(bank[4 + h][:], ident[0:4, h:h + 1].broadcast_to([4, P]), ab[:, 3, :], start=True, stop=True)\
                  .then_inc(sem("gdn_sum"), 1)
            for h in range(4):
                pe.wait_ge(sem("norm_mix"), 8 + h + 1)
                pe.matmul(bank[h][:], ident[0:4, h:h + 1].broadcast_to([4, P]), ab[:, 0, :], start=True, stop=True)\
                  .then_inc(sem("gdn_sum"), 1)
            pe.wait_ge(sem("gbc"), 4)
            for a, row in ((0, 0), (1, 3)):
                for c in range(TT):
                    last = turn(pe, bank[7][:, 16 * a + 4 * c:16 * a + 4 * c + 4], ab[:, row, c * P:(c + 1) * P], 4)
            last.then_inc(sem("gdn_sum"), 1)
            pe.wait_ge(sem("kb"), 4)
            for h in range(4):
                for c in range(TT):
                    x = slice(c * P, (c + 1) * P)
                    last = pe.matmul(bank[h][:, x], H4[:, K, h, x], H4[:, KB, h, x], start=True, stop=True)
                last.then_inc(sem("gdn_sum"), 1)
            pe.wait_ge(sem("cols"), 1)
            for h in range(4):
                for c in range(TT):
                    x = slice(c * P, (c + 1) * P)
                    last = pe.matmul(bank[4 + h][:, x], H4[:, K, h, x], H4[:, Q, h, x], start=True, stop=True)
                last.then_inc(sem("gdn_sum"), 1)
            pe.wait_ge(sem("at"), 4)
            pe.wait_ge(sem("qkv_silu"), 12)
            for h in range(4):
                if h:
                    pe.wait_ge(sem("kdec"), 4 * h)
                for c in range(TT):
                    last = turn(pe, bank[6][:, c * P:(c + 1) * P], H4[:, K, h, c * P:(c + 1) * P])
                last.then_inc(sem("k_turned"), 1)
                if h:
                    pe.wait_ge(sem("vb"), 4 * h)
                for c in range(TT):
                    last = turn(pe, bank[7][:, c * P:(c + 1) * P], H4[:, V, h, c * P:(c + 1) * P])
                last.then_inc(sem("v_turned"), 1)
            for g in range(4):
                pe.wait_ge(sem("nm"), 1)
                if g >= 2:
                    pe.wait_ge(sem("t_new"), g - 1)
                for b in range(4):
                    last = pe.matmul(bank[g % 2][:, b * P:(b + 1) * P], B[:, NM, 4 * g + b], ident[:],
                                     start=True, stop=True)
                last.then_inc(sem("y_sum"), 1)
            for n in range(1, LEVELS):
                pe.wait_ge(sem("nm"), n + 1)
                for g in range(4):
                    pe.wait_ge(sem("t_new"), 4 * (n - 1) + g + 1)
                    if g >= 2:
                        pe.wait_ge(sem("y"), 4 * (n - 1) + g - 1)
                    elif n == 1:
                        pe.wait_ge(sem("t_new"), 4)
                    for b in range(4):
                        last = pe.matmul(bank[g % 2][:, b * P:(b + 1) * P], B[:, NM + n % 2, 4 * g + b],
                                         B[:, T0, 4 * g + b], start=True, stop=True)
                    last.then_inc(sem("y_sum"), 1)
                for g in range(4):
                    pe.wait_ge(sem("y"), 4 * (n - 1) + g + 1)
                    pe.wait_ge(sem("tt_new"), 4 * (n - 1) + g + 1)
                    if n < LEVELS - 1:
                        pe.wait_ge(sem("t_new"), 4 * n + g - 1)
                        for b in range(4):
                            last = pe.matmul(bank[2 + g % 2][:, b * P:(b + 1) * P], B[:, T1, 4 * g + b],
                                             B[:, YR, 4 * g + b], start=True, stop=True)
                        last.then_inc(sem("ty_sum"), 1)
                    pe.wait_ge(sem("tt_new"), 4 * n + g - 1)
                    for b in range(4):
                        last = pe.matmul(bank[4 + g % 2][:, b * P:(b + 1) * P], B[:, YR, 4 * g + b],
                                         B[:, T1, 4 * g + b], start=True, stop=True)
                    last.then_inc(sem("yt_sum"), 1)
            pe.wait_ge(sem("vb"), 16)
            pe.wait_ge(sem("y"), 4 * (LEVELS - 1))
            pe.wait_ge(sem("tt_new"), 4 * LEVELS)
            pe.wait_ge(sem("kdec"), 16)
            for h in range(4):
                for c in range(TT):
                    last = pe.matmul(bank[h][:, c * P:(c + 1) * P], B[:, T1, 4 * h + c], B[:, V, 4 * h + c],
                                     start=True, stop=True)
                last.then_inc(sem("uw_sum"), 1)
            for h in range(4):
                for c in range(TT):
                    last = pe.matmul(bank[4 + h][:, c * P:(c + 1) * P], B[:, KBG, 4 * h + c], B[:, T1, 4 * h + c],
                                     start=True, stop=True)
                last.then_inc(sem("uw_sum"), 1)
            VN, ST = H4[:, T0], H4[:, T1]
            pe.wait_ge(sem("qd"), 1)
            pe.wait_ge(sem("uu"), 4)
            pe.wait_ge(sem("wt"), 4)
            for c in range(TT):
                if c:
                    pe.wait_ge(sem("state"), 4 * c)
                    if c >= 3:
                        pe.wait_ge(sem("vn"), c - 1)
                    for h in range(4):
                        last = pe.matmul(bank[c % 2][:, h * P:(h + 1) * P], B[:, WT, 4 * h + c],
                                         ST[:, (c - 1) % 2, h * P:(h + 1) * P], start=True, stop=True)
                    last.then_inc(sem("ws_sum"), 1)
                pe.wait_ge(sem("vn"), c + 1)
                if c < TT - 1:
                    for h in range(4):
                        last = pe.matmul(bank[4 + c % 2][:, h * P:(h + 1) * P], B[:, KDEC, 4 * h + c],
                                         VN[:, c % 2, h * P:(h + 1) * P], start=True, stop=True)
                    last.then_inc(sem("kv_sum"), 1)
                if c >= 2:
                    pe.wait_ge(sem("o_mix"), c - 1)
                for h in range(4):
                    o = bank[2 + c % 2][:, h * P:(h + 1) * P]
                    if c:
                        pe.matmul(o, ST[:, (c - 1) % 2, h * P:(h + 1) * P], B[:, QD, 4 * h + c],
                                  start=True, stop=False)
                    last = pe.matmul(o, VN[:, c % 2, h * P:(h + 1) * P], B[:, AT, 4 * h + c], start=c == 0, stop=True)
                last.then_inc(sem("o_sum"), 1)
            for h in range(4):
                sum_features(pe, 12 + h, bank[OUTB[h]], ones)


        def final_dve(dve):
            for k in range(KD):
                nc.vector.scalar_tensor_tensor(out=hT[:, k, :], in0=hT[:, k, :], scalar=column("final_norm", k),
                                               in1=rstd[:], op0=ALU.mult, op1=ALU.mult).then_inc(sem("h_final"), 1)
            dve.wait_ge(sem("h_final"), KD)

        memT = region(7).rearrange("p (k m) -> p k m", m=M)
        mem_rows = region(9).rearrange("p (t c) -> p t c", c=D)
        mem_rstd = region(10)[:, 0:M]
        memK = region(6)[:, 1024:1536].rearrange("p (j m) -> p j m", m=M)
        memV = region(6)[:, 1536:2048].rearrange("p (t c) -> p t c", c=M)
        memQ = region(6)[:, 0:1024].rearrange("p (j s) -> p j s", s=S)

        def mem_load(pool, l, after):
            pool.wait_ge(*after)
            pool.dma_start(mem_rows, A["mem_2"][0].rearrange("(t p) c -> p t c", p=P))\
              .then_inc(sem("mem_landed"), 16)

        MEMB = (4, 5, 6, 7)

        def mem_turn_pe(pe, l, r):
            pe.wait_ge(sem("mem_landed"), 16 * (l + 1))
            pe.wait_ge(sem("rms"), 2 * r + 1)
            for b in range(4):
                for u in range(4):
                    k, t = 2 * b + u // 2, u % 2
                    last = turn(pe, bank[MEMB[b]][:, u * P:(u + 1) * P], mem_rows[:, t, k * P:(k + 1) * P])
                last.then_inc(sem("mem_pe"), 1)

        def mem_sum_pe(pe, l):
            pe.wait_ge(sem("mem_dve"), 13 * l + 5)
            for k in range(KD):
                last = pe.matmul(bank[4][:, 0:M], ones[:], mem_sq[:, k, :], start=k == 0, stop=k == KD - 1)
            last.then_inc(sem("mem_pe"), 1)

        def mem_turn_dve(dve, l):
            for b in range(4):
                dve.wait_ge(sem("mem_pe"), 5 * l + b + 1)
                nc.vector.tensor_copy(memT[:, 2 * b:2 * b + 2, :], bank[MEMB[b]][:].rearrange("p (k m) -> p k m", m=M))\
                  .then_inc(sem("mem_dve"), 1)
            dve.wait_ge(sem("mem_dve"), 13 * l + 4)
            nc.vector.tensor_tensor(mem_sq[:], memT[:], memT[:], ALU.mult).then_inc(sem("mem_dve"), 1)

        def mem_norm_act(act, l):
            act.wait_ge(sem("mem_pe"), 5 * l + 5)
            nc.scalar.activation(mem_rstd, bank[4][:, 0:M], ACT.Ln, bias=eps[:], scale=1.0 / D)\
              .then_inc(sem("mem_act"), 1)
            act.wait_ge(sem("mem_act"), 2 * l + 1)
            nc.scalar.activation(mem_rstd, mem_rstd, ACT.Exp, scale=-0.5).then_inc(sem("mem_act"), 1)

        def mem_norm_dve(dve, l):
            dve.wait_ge(sem("mem_act"), 2 * l + 2)
            for k in range(KD):
                nc.vector.scalar_tensor_tensor(out=mem_sq[:, k, :], in0=memT[:, k, :],
                                               scalar=column("norm_mem_2", KD * l + k), in1=mem_rstd,
                                               op0=ALU.mult, op1=ALU.mult).then_inc(sem("mem_dve"), 1)

        def copy_out(eng, by, dst, src, scale=1.0):
            if by == "act":
                nc.scalar.activation(dst, src, ACT.Copy, scale=scale).then_inc(sem("evac_act"), 1)
            elif scale == 1.0:
                nc.vector.tensor_copy(dst, src).then_inc(sem("evac_dve"), 1)
            else:
                nc.vector.tensor_scalar(dst, src, scale, None, ALU.mult).then_inc(sem("evac_dve"), 1)

        def evac_to(by, place):
            def evac(eng, s, i, t):
                if s.tiles[t]["by"] != by:
                    return
                eng.wait_ge(sem("pe_segment"), plan.full(s, i, t))
                dst, nrow, ncol, scale = place(i, t)
                src = bank[s.tiles[t]["bank"]][0:nrow, 0:ncol]
                if len(dst.shape) == 3:
                    src = src.rearrange("p (o s) -> p o s", o=1)
                copy_out(eng, by, dst, src, scale)
            return evac

        def mem_place(i, t):
            return (memK[:, t, :], P, M, 1.0) if t < 2 else (memV[:, t - 2, :], P, M, 1.0)

        mem_p = region(10).rearrange("p (u m) -> p u m", m=M)
        mem_pt = region(11).rearrange("p (u s) -> p u s", s=S)
        diag = region(7).rearrange("p (u c) -> p u c", c=P)
        table = sb("table", [P, 1])
        mstat = sb("mstat", [P, 2, 3, 4])
        NROUND = 4

        def mem_attn_pe(pe, l, first_wait):
            wait_all(pe, first_wait)
            for r in range(NROUND + 2):
                if r < NROUND:
                    j, tp = divmod(r, 2)
                    n = NROUND * l + r
                    for half in range(2):
                        if n:
                            pe.wait_ge(sem("m_exp"), 4 * n)
                        f = slice(64 * half, 64 * half + 64)
                        for t in range(2):
                            at = (2 * tp + t) * P
                            last = pe.matmul(bank[4 + half][:, t * M:(t + 1) * M], memQ[f, j, at:at + P],
                                             memK[f, j, :], start=True, stop=True)
                        last.then_inc(sem("m_scores"), 1)
                if 1 <= r <= NROUND:
                    q = r - 1
                    n = NROUND * l + q
                    pe.wait_ge(sem("m_diag"), 4 * n + 4)
                    for half in range(2):
                        if n:
                            pe.wait_ge(sem("m_pt"), 2 * (n - 1) + half + 1)
                        for t in range(2):
                            for k in range(2):
                                u = 2 * t + k
                                last = pe.matmul(bank[6 + half][:, u * P:(u + 1) * P],
                                                 mem_p[:, 4 * (q % 2) + 2 * half + t, k * P:(k + 1) * P],
                                                 diag[:, 4 * (q % 2) + 2 * half + t, :], start=True, stop=True)
                        last.then_inc(sem("m_turned"), 1)
                if r >= 2:
                    q = r - 2
                    j, tp = divmod(q, 2)
                    n = NROUND * l + q
                    pe.wait_ge(sem("m_pt"), 2 * n + 2)
                    for half in range(2):
                        for t in range(2):
                            at = (2 * tp + t) * P
                            for k in range(2):
                                c = 64 * (2 * j + half)
                                last = pe.matmul(bank[2 + j][64 * half:64 * half + 64, at:at + P],
                                                 memV[:, k, c:c + 64],
                                                 mem_pt[:, 2 * (q % 2) + half, (2 * t + k) * P:(2 * t + k + 1) * P],
                                                 start=k == 0, stop=k == 1)
                    last.then_inc(sem("m_out"), 1)

        def mem_attn_act(act, l, f, x0):
            for r in range(NROUND + 1):
                if r < NROUND:
                    n = NROUND * l + r
                    for half in range(2):
                        act.wait_ge(sem("m_max"), 2 * n + half + 1)
                        if n >= 2:
                            act.wait_ge(sem("m_turned"), 2 * (n - 1))
                        for t in range(2):
                            u = 2 * half + t
                            nc.scalar.activation(mem_p[:, 4 * (r % 2) + u, :], bank[4 + half][:, t * M:(t + 1) * M],
                                                 ACT.Exp, bias=mstat[:, r % 2, 0, u:u + 1], scale=0.125,
                                                 accum_out=mstat[:, r % 2, 1, u:u + 1]).then_inc(sem("m_exp"), 1)
                if r >= 1:
                    q = r - 1
                    n = NROUND * l + q
                    for half in range(2):
                        act.wait_ge(sem("m_turned"), 2 * n + half + 1)
                        if n >= 2:
                            act.wait_ge(sem("m_out"), n - 1)
                        nc.scalar.activation(mem_pt[:, 2 * (q % 2) + half, :], bank[6 + half][:], ACT.Copy)\
                          .then_inc(sem("m_pt"), 1)
            for j in range(2):
                act.wait_ge(sem("m_out"), NROUND * l + 2 * j + 2)
                if l == 0:
                    nc.scalar.activation(mixed[:, x0 + j, :], bank[2 + j][:], ACT.Copy).then_inc(sem("mixed"), 1)
                    continue
                nc.scalar.activation(xH[:, x0 + j, :], bank[2 + j][:], ACT.Copy).then_inc(sem("x_hi"), 1)

        def mem_attn_dve(dve, l, f, x0, base):
            for r in range(NROUND):
                n = NROUND * l + r
                st = mstat[:, r % 2]
                for half in range(2):
                    dve.wait_ge(sem("m_scores"), 2 * n + half + 1)
                    if n >= 2:
                        dve.wait_ge(sem("m_exp"), 4 * (n - 1))
                    nc.vector.tensor_reduce(st[:, 0, 2 * half:2 * half + 2],
                                            bank[4 + half][:].rearrange("p (t m) -> p t m", m=M), AX, ALU.max)\
                      .then_inc(sem("m_raw"), 1)
                    dve.wait_ge(sem("m_raw"), 2 * n + half + 1)
                    nc.vector.tensor_scalar(st[:, 0, 2 * half:2 * half + 2], st[:, 0, 2 * half:2 * half + 2],
                                            -0.125, None, ALU.mult).then_inc(sem("m_max"), 1)
                dve.wait_ge(sem("m_exp"), 4 * n + 4)
                nc.vector.reciprocal(st[:, 2, :], st[:, 1, :]).then_inc(sem("m_inv"), 1)
                dve.wait_ge(sem("m_inv"), n + 1)
                if n >= 2:
                    dve.wait_ge(sem("m_turned"), 2 * (n - 1))
                for u in range(4):
                    nc.vector.tensor_scalar(diag[:, 4 * (r % 2) + u, :], ident[:], st[:, 2, u:u + 1], None,
                                            ALU.mult).then_inc(sem("m_diag"), 1)
            dve.wait_ge(sem("m_out"), NROUND * (l + 1))
            for j in range(2 if l else 0):
                dve.wait_ge(sem("x_hi"), base + j + 1)
                nc.vector.tensor_tensor(xL[:, x0 + j, :], bank[2 + j][:], xHf[:, x0 + j, :], ALU.subtract)\
                  .then_inc(sem("x_ready"), 1)

        p96 = sb("p96", [96, 6])
        gate_up = sb("gate_up", [16, 384])
        GDK, GDV, NH = 96, 192, 4
        gq = region(0)[0:GDK].rearrange("p (h s) -> p h s", s=S)
        gk = region(1)[0:GDK].rearrange("p (h s) -> p h s", s=S)
        gg = region(2, 2)[0:96].rearrange("p (t s) -> p t s", s=S)
        gv = region(4, 2)[:, 0:3072].rearrange("p (t c) -> p t c", c=768)
        lr = region(5)[0:16, 1024:1536]
        gb = region(9)[0:GDK]
        gx = region(10)[0:GDK]
        gw = region(11)[0:GDK]
        AD = region(12).rearrange("p (b c) -> p b c", c=P)
        A256 = region(13).rearrange("p (h k s) -> p h k s", h=NH, k=2)
        A128 = region(8)[:, 0:1024].rearrange("p (b c) -> p b c", c=P)
        go = mixed[0:96]
        gn = region(9)[0:96].rearrange("p (h s) -> p h s", s=S)
        WIDTHS = [256, 128, 64, 32, 16, 8, 4, 2, 1]

        def v_place(i, t):
            j, tile = divmod(t, TT)
            return (gv[:, tile, 256 * j:256 * j + 256], P, 256, 1.0)

        def rest_place(i, t):
            return (lr, 16, S, 1.0) if t == 0 else (memQ[:, t - 1, :], P, S, 1.0)

        def gate_pe(pe):
            pe.wait_ge(*stage_end("gla_rest")[0])
            pe.wait_ge(sem("gate_landed"), 16 * 7)
            for h in range(NH):
                pe.matmul(bank[4 + h][0:GDK, :], gate_up[:, GDK * h:GDK * (h + 1)], lr, start=True, stop=True)\
                  .then_inc(sem("gate_sum"), 1)

        def gate_dve(dve):
            dve.wait_ge(sem("gate_landed"), 16 * 7)
            for h in range(NH):
                dve.wait_ge(sem("gate_sum"), h + 1)
                nc.vector.tensor_scalar(gb[:, h * S:(h + 1) * S], bank[4 + h][0:GDK, :], p96[:, 2 + h:3 + h], None,
                                        ALU.add).then_inc(sem("gate_dve"), 1)
            dve.wait_ge(sem("gate_act"), 3)
            nc.vector.scalar_tensor_tensor(out=gx, in0=gb, scalar=0.0, in1=gx, op0=ALU.min, op1=ALU.subtract)\
              .then_inc(sem("gate_dve"), 1)
            dve.wait_ge(sem("gate_dve"), NH + 1)
            for h in range(NH):
                nc.vector.tensor_tensor_scan(gb[:, h * S:(h + 1) * S],
                                             ones[0:GDK, 0:1].broadcast_to([GDK, S]),
                                             gx[:, h * S:(h + 1) * S], 0.0, ALU.mult, ALU.add)\
                  .then_inc(sem("gate_dve"), 1)
            dve.wait_ge(sem("gate_dve"), 2 * NH + 1)

        def gate_act(act):
            act.wait_ge(sem("gate_dve"), NH)
            nc.scalar.activation(gx, gb, ACT.Abs).then_inc(sem("gate_act"), 1)
            act.wait_ge(sem("gate_act"), 1)
            nc.scalar.activation(gx, gx, ACT.Exp, scale=-1.0).then_inc(sem("gate_act"), 1)
            act.wait_ge(sem("gate_act"), 2)
            nc.scalar.activation(gx, gx, ACT.Ln, bias=1.0).then_inc(sem("gate_act"), 1)

        def halves(ap, w):
            v = ap.rearrange("p (b h r) -> p b h r", h=2, r=w)
            return v[:, :, 0, :], v[:, :, 1, :]

        def gla_dve(dve):
            wait_all(dve, stage_end("gla_k") + stage_end("gla_q"))
            for n, w in enumerate(WIDTHS):
                nb = NH * S // (2 * w)
                b0, b1 = halves(gb, w)
                x0, x1 = halves(gx, w)
                ref = b0[:, :, w - 1:w].broadcast_to([GDK, nb, w])
                if n:
                    dve.wait_ge(sem("lvl_w"), 2 * n)
                nc.vector.tensor_tensor(x1, b1, ref, ALU.subtract).then_inc(sem("lvl_x"), 1)
                nc.vector.tensor_tensor(x0, ref, b0, ALU.subtract).then_inc(sem("lvl_x"), 1)
                dve.wait_ge(sem("lvl_exp"), n + 1)
                if n:
                    dve.wait_ge(sem("a_sum"), A_AFTER[n - 1])
                q1 = halves(region(0)[0:GDK], w)[1]
                k0 = halves(region(1)[0:GDK], w)[0]
                w0, w1 = halves(gw, w)
                nc.vector.tensor_tensor(w1, q1, x1, ALU.mult).then_inc(sem("lvl_w"), 1)
                nc.vector.tensor_tensor(w0, k0, x0, ALU.mult).then_inc(sem("lvl_w"), 1)
                if n:
                    take_levels(dve, n - 1)
            take_levels(dve, len(WIDTHS) - 1)
            take_levels(dve, len(WIDTHS))

        def take_levels(dve, n):
            base = A_AFTER[n - 1] if n else 0
            if n == 0:
                for h in range(NH):
                    dve.wait_ge(sem("a_sum"), base + h + 1)
                    nc.vector.tensor_copy(A256[:, h], bank[h][:].rearrange("p (k s) -> p k s", k=2))\
                      .then_inc(sem("a_out"), 1)
            elif n == 1:
                for g in range(2):
                    dve.wait_ge(sem("a_sum"), base + g + 1)
                    nc.vector.tensor_copy(A128[:, 4 * g:4 * g + 4], blocks(bank[4 + g][:])).then_inc(sem("a_out"), 1)
            else:
                mask = lvl[:, 8 - n, :] if n < len(WIDTHS) else ident[:]
                for h in range(NH):
                    dve.wait_ge(sem("a_sum"), base + h + 1)
                    if n == 2:
                        dve.wait_ge(sem("ad_zero"), 1)
                    else:
                        dve.wait_ge(sem("a_out"), A_AFTER[n - 2] + h + 1)
                    nc.vector.copy_predicated(AD[:, 4 * h:4 * h + 4], repeat(mask.bitcast(mybir.dt.uint32), 4),
                                              blocks(bank[(4 * n + h) % 8][:])).then_inc(sem("a_out"), 1)

        A_AFTER = [4, 6]
        for _ in range(len(WIDTHS) - 1):
            A_AFTER.append(A_AFTER[-1] + NH)

        def gla_act(act):
            for n in range(len(WIDTHS)):
                act.wait_ge(sem("lvl_x"), 2 * n + 2)
                nc.scalar.activation(gx, gx, ACT.Exp, scale=1.0 / 16).then_inc(sem("lvl_exp"), 1)
            nc.scalar.activation(region(2, 2)[0:96], region(2, 2)[0:96], ACT.Silu).then_inc(sem("gg_silu"), 1)
            for t in range(8):
                act.wait_ge(sem("go_sum"), t + 1)
                nc.scalar.activation(go[:, t, :], bank[t % 4][0:96, :], ACT.Copy).then_inc(sem("go"), 1)
            for t in range(8):
                act.wait_ge(sem("go"), t + 1)
                squares96(act, t)
            for h in range(NH):
                act.wait_ge(sem("sum_mix"), 16 + 2 * h + 2)
                nc.scalar.activation(gn[:, h, :], bank[4 + h][0:96, :], ACT.Ln, bias=eps[0:96], scale=1.0 / GDV)\
                  .then_inc(sem("norm_mix"), 1)
            for h in range(NH):
                inverse_root(act, 16 + h, gn[:, h, :])

        def squares96(act, t):
            act.wait_ge(sem("sum_mix"), 16 + t - 1)
            nc.scalar.activation(sq[0:96, t % 2, :], go[:, t, :], ACT.Square).then_inc(sem("sq_mix"), 1)

        def gla_pe(pe):
            wait_all(pe, stage_end("gla_g") + stage_end("gla_v"))
            for n, w in enumerate(WIDTHS + [0]):
                if w:
                    pe.wait_ge(sem("lvl_w"), 2 * n + 2)
                src = gw.rearrange("p (h s) -> p h s", s=S)
                if n == 0:
                    for h in range(NH):
                        for k in range(2):
                            last = pe.matmul(bank[h][:, 256 * k:256 * k + 256], src[:, h, k * P:(k + 1) * P],
                                             src[:, h, 256:512], start=True, stop=True)
                        last.then_inc(sem("a_sum"), 1)
                elif n == 1:
                    for g in range(2):
                        for u in range(4):
                            h, k = 2 * g + u // 2, 2 * (u % 2)
                            last = pe.matmul(bank[4 + g][:, u * P:(u + 1) * P], src[:, h, k * P:(k + 1) * P],
                                             src[:, h, (k + 1) * P:(k + 2) * P], start=True, stop=True)
                        last.then_inc(sem("a_sum"), 1)
                else:
                    for h in range(NH):
                        b = (4 * n + h) % 8
                        pe.wait_ge(sem("a_out"), (A_AFTER[n - 3] if n >= 3 else 0) + h + 1 if n != 3 else 6)
                        for t in range(TT):
                            x = slice(t * P, (t + 1) * P)
                            a, c = (src[:, h, x], src[:, h, x]) if w else (gk[:, h, x], gq[:, h, x])
                            last = pe.matmul(bank[b][:, x], a, c, start=True, stop=True)
                        last.then_inc(sem("a_sum"), 1)
            pe.wait_ge(sem("a_out"), A_AFTER[-1])
            for t in range(8):
                h, d = divmod(t, 2)
                if t >= 4:
                    pe.wait_ge(sem("go"), t - 3)
                v = slice(GDV * h + 96 * d, GDV * h + 96 * d + 96)
                o = bank[t % 4][0:96]
                for k in range(TT):
                    pe.matmul(o[:, k * P:(k + 1) * P], gv[:, k, v], AD[:, 4 * h + k], start=k == 0, stop=False)
                for k in range(2):
                    pe.matmul(o[:, (2 * k + 1) * P:(2 * k + 2) * P], gv[:, 2 * k, v], A128[:, 2 * h + k],
                              start=False, stop=False)
                for k in range(2):
                    last = pe.matmul(o[:, 256:512], gv[:, k, v], A256[:, h, k], start=False, stop=k == 1)
                last.then_inc(sem("go_sum"), 1)
            for t in range(8):
                pe.wait_ge(sem("sq_mix"), 16 + t + 1)
                pe.matmul(bank[4 + t // 2][0:96, :], ones[0:96, 0:96], sq[0:96, t % 2, :], start=t % 2 == 0,
                          stop=t % 2 == 1).then_inc(sem("sum_mix"), 1)

        def gla_out_dve(dve):
            for t in range(8):
                dve.wait_ge(sem("inv_mix"), 16 + t // 2 + 1)
                nc.vector.scalar_tensor_tensor(out=go[:, t, :], in0=go[:, t, :], scalar=p96[:, t % 2:t % 2 + 1],
                                               in1=gn[:, t // 2, :], op0=ALU.mult, op1=ALU.mult)\
                  .then_inc(sem("go_out"), 1)
            dve.wait_ge(sem("gg_silu"), 1)
            for t in range(8):
                dve.wait_ge(sem("go_out"), t + 1)
                nc.vector.tensor_tensor(go[:, t, :], go[:, t, :], gg[:, t, :], ALU.mult).then_inc(sem("mixed"), 1)

        def conv_columns(s, i, t):
            l = int(s.name[3]) - 2
            f = NF * (t // 2) + 2 * i + t % 2
            w = PAR_AT["conv_w_2"][0] + 3 * 2 * NF * l
            b = PAR_AT["conv_b_2"][0] + 2 * NF * l
            return [par[:, bass.ds(w + 2 * NF * tap + f, 1)] for tap in range(3)] + [par[:, bass.ds(b + f, 1)]]

        def conv_evac_act(act, s, i, t):
            w = conv_columns(s, i, t)
            act.wait_ge(sem("pe_segment"), plan.full(s, i, t))
            act.wait_ge(sem("cv_prod"), 2 * conv_index(s, i) + CREDIT)
            nc.scalar.activation(cv[:, t, :], bank[t][:], ACT.Copy, scale=w[2])\
              .then_inc(sem("cv_tap"), 1)
            if t == 2:
                for u in range(2):
                    act.wait_ge(sem("evac_dve"), plan.evac(s, i, u))
                    nc.scalar.activation(sg[:, u, :], cv[:, u, :], ACT.Silu, bias=conv_columns(s, i, u)[3]).then_inc(sem("cv_silu"), 1)

        def conv_index(s, i):
            return NF // 2 * (int(s.name[3]) - 2) + i

        def conv_evac_dve(dve, s, i, t):
            w = conv_columns(s, i, t)
            k = conv_index(s, i)
            dve.wait_ge(sem("cv_tap"), 4 * k + t + 1)
            nc.vector.scalar_tensor_tensor(out=cv[:, t, 1:], in0=bank[t][:, :S - 1], scalar=w[1],
                                           in1=cv[:, t, 1:], op0=ALU.mult, op1=ALU.add).then_inc(sem("cv_mid"), 1)
            dve.wait_ge(sem("cv_mid"), 4 * k + t + 1)
            nc.vector.scalar_tensor_tensor(out=cv[:, t, 2:], in0=bank[t][:, :S - 2], scalar=w[0],
                                           in1=cv[:, t, 2:], op0=ALU.mult, op1=ALU.add)\
              .then_inc(sem("evac_dve"), 1)
            if t == 3:
                for u in range(2):
                    dve.wait_ge(sem("cv_silu"), 2 * k + u + 1)
                    dve.wait_ge(sem("evac_dve"), plan.evac(s, i, u + 2))
                    nc.vector.scalar_tensor_tensor(out=g[:, bass.ds(2 * i + u, 1), :], in0=cv[:, 2 + u:3 + u, :],
                                                   scalar=conv_columns(s, i, u + 2)[3], in1=sg[:, u:u + 1, :],
                                                   op0=ALU.add, op1=ALU.mult).then_inc(sem("cv_prod"), 1)

        aq = region(0, 2)[:, 0:3072].rearrange("p (t s) -> p t s", s=S)
        misc = region(1)
        gates = misc[:, 1024:1168].rearrange("p (t c) -> p t c", c=36)
        kcT = misc[:, 1200:1262].rearrange("p (g n) -> p g n", n=31)
        vc = misc[0:31, 1280:1536].rearrange("p (g d) -> p g d", d=64)
        hid = misc[:, 1536:1784].rearrange("p (j g n) -> p j g n", j=2, n=31)
        posT = misc[:, 1784:1848].rearrange("p (j n) -> p j n", j=2)
        pos = region(5)[0:32, 1024:1152].rearrange("p (j d) -> p j d", j=2)
        tblT = region(5)[0:12, 1152:1184]
        tbl = region(5)[0:32, 1184:1196]
        cw2 = misc[:, 1920:2048].rearrange("p (j d) -> p j d", j=2)
        pre = region(2).rearrange("p (t s) -> p t s", s=S)
        pre2 = region(12).rearrange("p (t s) -> p t s", s=S)
        ak = region(3).rearrange("p (t s) -> p t s", s=S)
        av = region(4).rearrange("p (j t c) -> p j t c", j=2, c=256)
        TW = 896
        tab = region(2)[:, 0:2 * TW].rearrange("p (b c) -> p b c", c=TW)
        relrow = region(5)[0:12, 0:1024]
        w1 = [region(9, 2).rearrange("p (q n) -> p q n", n=P), region(7, 2).rearrange("p (q n) -> p q n", n=P)]
        skew = [region(12)[:, 0:TW], region(13)[:, 0:TW]]
        pbuf = [region(8)[:, 0:1024], region(9)[:, 0:1024], region(8)[:, 1024:2048]]
        ptb = [region(10), region(11)]
        dg = region(7)[:, 0:1024].rearrange("p (b u c) -> p b u c", b=2, c=P)
        nstat = sb("nstat", [P, 3, 4, 4])
        mirror = region(13)[:, 1024:1024 + P]
        b2 = sb("b2", [P, 1 + 64])
        NCMP, AH = 31, 12
        NEG = -1e30
        rel_dram = nc.dram_tensor("rel_rows", (AH, 1024), F32, kind="Internal").ap()

        def kv_place(i, t):
            return (pre if t < 4 else ak)[:, t % 4, :], P, S, 1.0

        def kvt_place(i, t):
            j, tile = divmod(t, TT)
            return av[:, j, tile, :], P, 256, 1.0

        def aq_place(i, t):
            return aq[:, t, :], P, S, 0.125

        def gate_evac_act(act, s, i, t):
            if t < TT:
                act.wait_ge(sem("pe_segment"), plan.full(s, i, t))
                nc.scalar.activation(gates[:, t, :], bank[t][:, 0:36], ACT.Sigmoid).then_inc(sem("evac_act"), 1)

        def mq_place(i, t):
            return memQ[:, t - TT, :], P, S, 1.0

        def bucket_ranges():
            d = np.arange(S)
            big = 16 + (np.log(np.maximum(d, 1).astype(np.float32) / np.float32(16))
                        / np.float32(np.log(128 / 16)) * np.float32(16)).astype(np.int32)
            bucket = np.where(d < 16, d, np.minimum(big, 31))
            return [(int(d[bucket == b].min()), int(d[bucket == b].max())) for b in range(32)]

        def rel_sp(sp):
            sp.wait_ge(*stage_end("ffn2_down")[0])
            sp.dma_start(tbl, A["rel_bias_2"]).then_inc(sem("nsa_small"), 16)
            for j in range(2):
                sp.dma_start(pos[:, j, :], A["cmp_pos_2"][j]).then_inc(sem("nsa_small"), 16)
                sp.dma_start(cw2[:, j, :], A["cmp_w2_2"][j]).then_inc(sem("nsa_small"), 16)
                sp.dma_start(b2[64 * j:64 * j + 64, 0:1], A["cmp_b2_2"][0].rearrange("(p o) -> p o", o=1))\
                  .then_inc(sem("nsa_small"), 16)
            sp.dma_start(b2[0:1, 1:65], A["cmp_b2_2"][1:2]).then_inc(sem("nsa_small"), 16)

        def w1_sp(sp, j):
            if j == 0:
                sp.wait_ge(sem("mem_dve"), 26)
            else:
                wait_all(sp, stage_end("mem1_kv"))
            for half in range(2):
                sp.dma_start(w1[j][64 * half:64 * half + 64], A["cmp_w1_2"][j].rearrange("(q d) n -> d q n", d=64))\
                  .then_inc(sem("w1_landed"), 16)

        def rel_store(pool):
            pool.wait_ge(sem("rel_row"), 33)
            pool.dma_start(rel_dram, relrow).then_inc(sem("rel_stored"), 16)
            pool.wait_ge(sem("rel_stored"), 16)

        def skew_pool(pool):
            pool.wait_ge(sem("c_dve"), 2)
            for h in range(AH):
                if h >= 2:
                    pool.wait_ge(sem("tab_sum"), 2 * (h - 1))
                pool.dma_start(skew[h % 2], bass.AP(rel_dram.tensor, 1024 * h, [[1, P], [1, TW]]))\
                  .then_inc(sem(f"skew{h % 2}"), 16)

        def rel_pe(pe):
            pe.wait_ge(sem("nsa_small"), 16 * 8)
            wait_all(pe, stage_end("kv_t") + stage_end("kv_f"))
            turn(pe, bank[4][0:AH, 0:32], tbl, 32)
            for j in range(2):
                for half in range(2):
                    f = slice(64 * half, 64 * half + 64)
                    last = pe.matmul(bank[4][f, 32 * j + 32:32 * j + 64], pos[:, j, :], ident[0:32, 0:32], start=True, stop=True)
            last.then_inc(sem("small_turned"), 1)

        def rel_dve(dve):
            dve.wait_ge(sem("small_turned"), 1)
            nc.vector.tensor_copy(tblT, bank[4][0:AH, 0:32]).then_inc(sem("small_t"), 1)
            nc.vector.tensor_copy(posT, bank[4][:, 32:96].rearrange("p (j n) -> p j n", j=2))\
              .then_inc(sem("small_t"), 1)
            dve.wait_ge(sem("small_t"), 2)
            nc.vector.memset(relrow[:, 512:1024], NEG).then_inc(sem("rel_row"), 1)
            for b, (lo, hi) in enumerate(bucket_ranges()):
                nc.vector.tensor_scalar(relrow[:, 511 - hi:512 - lo], ones[0:AH, 0:1].broadcast_to([AH, hi - lo + 1]),
                                        tblT[:, b:b + 1], None, ALU.mult).then_inc(sem("rel_row"), 1)

        def cmp_pe(pe):
            pe.wait_ge(sem("w1_landed"), 64)
            pe.wait_ge(sem("pre"), 4)
            wait_all(pe, stage_end("nsa_q") + stage_end("nsa_g"))
            for j in range(2):
                for half in range(2):
                    f = slice(64 * half, 64 * half + 64)
                    for q in range(32):
                        x = (pre if q < 16 else pre2)[f, 2 * j:2 * j + 2, q:q + 16 * (NCMP - 1) + 1:16]
                        last = pe.matmul(bank[1 + 4 * j + half][:, 0:2 * NCMP].rearrange("p (g n) -> p g n", g=2),
                                         w1[j][f, q, :], x, start=q == 0, stop=q == 31)
                    last.then_inc(sem("c_pe"), 1)
            for j in range(2):
                pe.wait_ge(sem("c_hid"), 2 * j + 2)
                for g in range(4):
                    if j == 0:
                        last = pe.matmul(bank[3][64 * (g % 2):64 * (g % 2) + 64, (g // 2) * NCMP:(g // 2 + 1) * NCMP],
                                         cw2[:, 0, :], hid[:, 0, g, :], start=True, stop=True)
                    else:
                        o = bank[4][0:NCMP, 64 * g:64 * g + 64]
                        pe.matmul(o, hid[:, 1, g, :], cw2[:, 1, :], start=True, stop=False)
                        last = pe.matmul(o, ones[0:1, 0:NCMP], b2[0:1, 1:65], start=False, stop=True)
                last.then_inc(sem("c_pe"), 1)

        def pos_dve(dve):
            wait_all(dve, stage_end("kv_f"))
            dve.wait_ge(sem("small_t"), 2)
            for j in range(2):
                for u, o in ((1, pre2), (0, pre)):
                    p16 = posT[:, j, 16 * u:16 * u + 16].unsqueeze(1).broadcast_to([P, S // 16, 16])
                    for t in (2 * j, 2 * j + 1):
                        last = nc.vector.tensor_tensor(o[:, t, :].rearrange("p (n q) -> p n q", q=16),
                                                       pre[:, t, :].rearrange("p (n q) -> p n q", q=16), p16, ALU.add)
                    last.then_inc(sem("pre"), 1)
                    dve.wait_ge(sem("pre"), 2 * j + 2 - u)

        def cmp_dve(dve):
            dve.wait_ge(sem("c_pe"), 5)
            nc.vector.tensor_scalar(kcT[:], bank[3][:, 0:2 * NCMP].rearrange("p (g n) -> p g n", n=NCMP),
                                    b2[:, 0:1], None, ALU.add).then_inc(sem("c_dve"), 1)
            dve.wait_ge(sem("c_pe"), 6)
            nc.vector.tensor_copy(vc[:], bank[4][0:NCMP, 0:256].rearrange("p (g d) -> p g d", d=64))\
              .then_inc(sem("c_dve"), 1)

        def cmp_act(act):
            for j in range(2):
                for half in range(2):
                    act.wait_ge(sem("c_pe"), 2 * j + half + 1)
                    nc.scalar.activation(hid[:, j, half:4:2, :], bank[1 + 4 * j + half][:, 0:2 * NCMP]
                                         .rearrange("p (g n) -> p g n", n=NCMP), ACT.Silu,
                                         bias=column("cmp_b1_2", j)).then_inc(sem("c_hid"), 1)

        items = [(h, t) for h in range(AH) for t in (None, 0, 1, 2, 3)]

        def head_at(h):
            g = h // 3
            return 3 * (g // 2) + h % 3, slice(64 * (g % 2), 64 * (g % 2) + 64), g, g // 2

        def score_banks(h, t):
            return (bank[0], bank[1]) if t % 2 == 0 else (bank[3], bank[4])

        def table_pe(pe, h, u):
            if u == 0:
                pe.wait_ge(sem(f"skew{h % 2}"), 16 * (h // 2 + 1))
            if h or u:
                pe.wait_ge(sem("tab"), 2 * h + u)
            if h and not u:
                pe.wait_ge(sem("n_max"), 5 * (h - 1) + 1)
            pe.matmul(bank[2][:, 0:448], mirror[:], skew[h % 2][:, 448 * u:448 * (u + 1)],
                      start=True, stop=True).then_inc(sem("tab_sum"), 1)

        def table_act(act, h, u):
            act.wait_ge(sem("tab_sum"), 2 * h + u + 1)
            if h >= 2:
                act.wait_ge(sem("n_max"), 5 * (h - 1))
            nc.scalar.activation(tab[:, h % 2, 448 * u:448 * (u + 1)], bank[2][:, 0:448], ACT.Copy)\
              .then_inc(sem("tab"), 1)

        def attend_pe(pe):
            wait_all(pe, stage_end("nsa_q") + stage_end("nsa_g"))
            pe.wait_ge(sem("x_ready"), xbase(9) + 2)
            pe.wait_ge(sem("c_dve"), 2)
            pe.wait_ge(sem("mirror"), 2)
            for m in range(len(items) + 3):
                if m < len(items):
                    h, t = items[m]
                    tile, f, g, gt = head_at(h)
                    if m == 0:
                        table_pe(pe, 0, 0)
                        table_pe(pe, 0, 1)
                    if t in (1, 2) and h + 1 < AH:
                        table_pe(pe, h + 1, t - 1)
                    if t is None:
                        pe.wait_ge(sem("tab"), 2 * h + 2)
                        for u in range(TT):
                            last = pe.matmul(bank[2][:, 32 * u:32 * u + NCMP], aq[f, tile, u * P:(u + 1) * P],
                                             kcT[f, gt, :], start=True, stop=True)
                    else:
                        if m >= 2:
                            pe.wait_ge(sem("n_max"), m - 1 if t >= 2 else max(1, m - 2))
                        n = P * (t + 1)
                        s0, s1 = score_banks(h, t)
                        pe.matmul(s0[:, 0:n], aq[f, tile, t * P:(t + 1) * P], ak[f, gt, 0:n], start=True, stop=True)
                        last = pe.matmul(s1[:, 0:n], aq[f, tile, t * P:(t + 1) * P], ak[f, 2 + gt, 0:n],
                                         start=True, stop=True)
                    last.then_inc(sem("n_scores"), 1)
                if 2 <= m <= len(items) + 1:
                    q = m - 2
                    h, t = items[q]
                    pe.wait_ge(sem("n_diag"), q + 1)
                    if q:
                        pe.wait_ge(sem("n_pts"), q)
                    if wcount(q):
                        pe.wait_ge(sem("n_ptw"), wcount(q))
                    if t is None:
                        for u in range(TT):
                            last = pe.matmul(bank[5][0:NCMP, u * P:(u + 1) * P], pbuf[q % 3][:, 32 * u:32 * u + NCMP],
                                             dg[:, q % 2, u, :], start=True, stop=True)
                    else:
                        for br in range(2):
                            for k in range(t + 1):
                                last = pe.matmul(bank[5 + br][:, k * P:(k + 1) * P],
                                                 pbuf[q % 3][:, 512 * br + k * P:512 * br + (k + 1) * P],
                                                 dg[:, q % 2, br, :], start=True, stop=True)
                    last.then_inc(sem("n_turned"), 1)
                if m >= 3:
                    q = m - 3
                    h, t = items[q]
                    _, _, g, _ = head_at(h)
                    o = bank[7][64 * (h % 2):64 * (h % 2) + 64]
                    pe.wait_ge(sem("n_pts"), q + 1)
                    if t is None:
                        if h >= 2:
                            pe.wait_ge(sem("x_ready"), xbase(9) + 2 + h - 1)
                        for u in range(TT):
                            last = pe.matmul(o[:, u * P:(u + 1) * P], vc[:, g, :], ptb[q % 2][0:NCMP, u * P:(u + 1) * P],
                                             start=u == 0, stop=False, skip_group_check=True)
                    else:
                        pe.wait_ge(sem("n_ptw"), wcount(q + 1))
                        for br in range(2):
                            for k in range(t + 1):
                                last = pe.matmul(o[:, t * P:(t + 1) * P], av[:, br, k, 64 * g:64 * g + 64],
                                                 ptb[q % 2][:, 512 * br + k * P:512 * br + (k + 1) * P], start=False,
                                                 stop=t == 3 and br == 1 and k == t, skip_group_check=True)
                    last.then_inc(sem("n_out"), 1)

        def wcount(q):
            return sum(t is not None for _, t in items[:q])

        def attend_dve(dve):
            for m in range(len(items) + 3):
                if m < len(items):
                    h, t = items[m]
                    st = nstat[:, m % 3]
                    dve.wait_ge(sem("n_scores"), m + 1)
                    if m >= 3:
                        dve.wait_ge(sem("n_turned"), m - 2)
                    if t is None:
                        dve.wait_ge(sem("tab"), 2 * h + 2)
                        cut = [(bank[2][:, 32 * u:32 * u + NCMP], tab[:, h % 2, 415 - P * u:415 - P * u + 481:16],
                                pbuf[m % 3][:, 32 * u:32 * u + NCMP]) for u in range(TT)]
                    else:
                        n = P * (t + 1)
                        table = tab[:, h % 2, 384 - P * t:384 - P * t + n]
                        cut = [(b[:, 0:n], table, pbuf[m % 3][:, 512 * br:512 * br + n])
                               for br, b in enumerate(score_banks(h, t))]
                    for u, (a, b, o) in enumerate(cut):
                        last = nc.vector.tensor_tensor_reduce(out=o, in0=a, in1=b, scale=1.0, scalar=-3e38, op0=ALU.add,
                                                              op1=ALU.max, accum_out=st[:, 0, u:u + 1])
                    last.then_inc(sem("n_raw"), 1)
                    dve.wait_ge(sem("n_raw"), m + 1)
                    nc.vector.tensor_scalar(st[:, 1, 0:len(cut)], st[:, 0, 0:len(cut)], -1e29, -1.0, ALU.max, ALU.mult)\
                      .then_inc(sem("n_max"), 1)
                if 1 <= m <= len(items):
                    q = m - 1
                    h, t = items[q]
                    st = nstat[:, q % 3]
                    n = TT if t is None else 2
                    dve.wait_ge(sem("n_exp"), q + 1)
                    nc.vector.tensor_scalar(st[:, 2, 0:n], st[:, 2, 0:n], 1e-30, None, ALU.max)\
                      .then_inc(sem("n_clamp"), 1)
                    dve.wait_ge(sem("n_clamp"), q + 1)
                    nc.vector.reciprocal(st[:, 3, 0:n], st[:, 2, 0:n]).then_inc(sem("n_inv"), 1)
                    dve.wait_ge(sem("n_inv"), q + 1)
                    if q >= 2:
                        dve.wait_ge(sem("n_turned"), q - 1)
                    for u in range(n):
                        gate = gates[:, u, 3 * h:3 * h + 1] if t is None else gates[:, t, 3 * h + 1 + u:3 * h + 2 + u]
                        last = nc.vector.tensor_scalar(dg[:, q % 2, u, :], ident[:], st[:, 3, u:u + 1], gate,
                                                       ALU.mult, ALU.mult)
                    last.then_inc(sem("n_diag"), 1)
                if 2 <= m <= len(items) + 1:
                    q = m - 2
                    h, t = items[q]
                    if t is not None:
                        n = P * (t + 1)
                        dve.wait_ge(sem("n_turned"), q + 1)
                        if q >= 2:
                            dve.wait_ge(sem("n_out"), q - 1)
                        nc.vector.tensor_copy(ptb[q % 2][:, 512:512 + n], bank[6][:, 0:n]).then_inc(sem("n_ptw"), 1)
                if m >= 4 and items[m - 4][1] == 3:
                    rest_dve(dve, items[m - 4][0])
            rest_dve(dve, AH - 1)

        def rest_dve(dve, h):
            f = slice(64 * (h % 2), 64 * (h % 2) + 64)
            dve.wait_ge(sem("x_hi"), xbase(9) + 2 + h + 1)
            nc.vector.tensor_tensor(xL[f, h // 2, :], bank[7][f, :], xHf[f, h // 2, :], ALU.subtract)\
              .then_inc(sem("x_ready"), 1)

        def attend_act(act):
            for m in range(len(items) + 3):
                if m < len(items):
                    h, t = items[m]
                    if m == 0:
                        table_act(act, 0, 0)
                        table_act(act, 0, 1)
                    if t is None:
                        cut = [slice(32 * u, 32 * u + NCMP) for u in range(TT)]
                    else:
                        cut = [slice(512 * br, 512 * br + P * (t + 1)) for br in range(2)]
                    act.wait_ge(sem("n_max"), m + 1)
                    if m >= 3:
                        act.wait_ge(sem("n_inv"), m - 2)
                    for u, x in enumerate(cut):
                        last = nc.scalar.activation(pbuf[m % 3][:, x], pbuf[m % 3][:, x], ACT.Exp,
                                                    bias=nstat[:, m % 3, 1, u:u + 1],
                                                    accum_out=nstat[:, m % 3, 2, u:u + 1])
                    last.then_inc(sem("n_exp"), 1)
                    if t in (1, 2) and h + 1 < AH:
                        table_act(act, h + 1, t - 1)
                if 2 <= m <= len(items) + 1:
                    q = m - 2
                    h, t = items[q]
                    act.wait_ge(sem("n_turned"), q + 1)
                    if q >= 2:
                        act.wait_ge(sem("n_out"), q - 1)
                    x, r = (slice(0, 512), NCMP) if t is None else (slice(0, P * (t + 1)), P)
                    nc.scalar.activation(ptb[q % 2][0:r, x], bank[5][0:r, x], ACT.Copy).then_inc(sem("n_pts"), 1)
                if m >= 4 and items[m - 4][1] == 3:
                    upper_act(act, items[m - 4][0])
            upper_act(act, AH - 1)

        def upper_act(act, h):
            f = slice(64 * (h % 2), 64 * (h % 2) + 64)
            act.wait_ge(sem("n_out"), 5 * (h + 1))
            nc.scalar.activation(xH[f, h // 2, :], bank[7][f, :], ACT.Copy).then_inc(sem("x_hi"), 1)

        def result_dve(dve):
            for k in range(KD):
                if k >= 2:
                    dve.wait_ge(sem("y_turned"), k - 1)
                nc.vector.scalar_tensor_tensor(out=xn[:, k % 2, :], in0=hT[:, k, :], in1=rstd[:], op0=ALU.mult,
                                               scalar=column("final_norm_2", k), op1=ALU.mult).then_inc(sem("y"), 1)
                if k >= 1 and (k - 1) % 2 == 1:
                    rows_out(dve, k - 1)
            rows_out(dve, KD - 1)

        def rows_out(eng, k):
            eng.wait_ge(sem("y_turned"), k + 1)
            o, b = rows[:, :, k * P:(k + 1) * P], blocks(bank[k % 4][:])
            if k % 2 == 1:
                nc.vector.tensor_copy(o, b).then_inc(sem("rows_dve"), 1)
            else:
                nc.scalar.activation(o, b, ACT.Copy).then_inc(sem("rows_act"), 1)

        def result_pe(pe):
            wait_all(pe, stage_end("ffn3_down"))
            for k in range(KD):
                pe.wait_ge(sem("y"), Y0 + k + 1)
                if k >= 4:
                    pe.wait_ge(sem("rows_act" if k % 2 == 0 else "rows_dve"), (k - 4) // 2 + 1)
                for t in range(TT):
                    last = turn(pe, bank[k % 4][:, t * P:(t + 1) * P], xn[:, k % 2, t * P:(t + 1) * P])
                last.then_inc(sem("y_turned"), 1)

        def result_act(act):
            for k in range(0, KD, 2):
                rows_out(act, k)

        Y0 = 4 * (LEVELS - 1)

        def result_sp(sp):
            sp.wait_ge(sem("rows_act"), KD // 2)
            sp.wait_ge(sem("rows_dve"), KD // 2)
            sp.dma_start(out[0].rearrange("(t p) c -> p t c", p=P), rows[:, :, :]).then_inc(sem("stored"), 16)
            sp.wait_ge(sem("stored"), 16)


        def h_loaded(k):
            return (sem("h_act" if k % 2 == 0 else "h_dve"), k // 2 + 1)

        @nc_block.sync
        def _(sp):
            sp.dma_start(rows[:, :, :], A["x"][0].rearrange("(t p) c -> p t c", p=P)).then_inc(sem("x_landed"), 16)
            load_sp(sp)
            for i, name in enumerate(("gdn_A_log", "gdn_dt_bias")):
                sp.dma_start(hv[:, i:i + 1], A[name][0].rearrange("(p o) -> p o", o=1)).then_inc(sem("hv_landed"), 16)
            sp.dma_start(gate_up[:], A["gla_w_gate_up_2"][0]).then_inc(sem("gate_landed"), 16)
            for c in range(6):
                name, k = ("gla_out_norm_2", c) if c < 2 else ("gla_b_gate_2", c - 2)
                sp.dma_start(p96[:, c:c + 1], A[name][0, 96 * k:96 * (k + 1)].rearrange("(p o) -> p o", o=1))\
                  .then_inc(sem("gate_landed"), 16)
            for s in plan.order:
                load_panels(sp, s.name)
                if s.name == "mem1_kv":
                    rel_sp(sp)
                    w1_sp(sp, 0)
                if s.name == "kv_f":
                    w1_sp(sp, 1)
            result_sp(sp)

        @nc_block.gpsimd
        def _(pool):
            constants_pool(pool)
            norm_pool(pool, 0)
            split_lo(pool, "ffn0_up")
            constants2_pool(pool)
            norm_pool(pool, 1)
            split_lo(pool, "mix_ba")
            split_lo(pool, "mix_in")
            gdn_pool(pool)
            mem_load(pool, 0, (sem("uw_sum"), 4))
            split_lo(pool, "mix_out")
            norm_pool(pool, 2)
            split_lo(pool, "ffn1_up")
            norm_pool(pool, 3)
            pool.wait_ge(sem("h_final"), KD)
            norm_pool(pool, 4)
            for name in ("gla_rest", "gla_q", "gla_k", "gla_v", "gla_g"):
                split_lo(pool, name)
            wait_all(pool, stage_end("gla_g"))
            nc.gpsimd.memset(AD[:], 0.0).then_inc(sem("ad_zero"), 1)
            mem_load(pool, 1, (sem("go_out"), 8))
            norm_pool(pool, 5)
            split_lo(pool, "ffn2_up")
            norm_pool(pool, 6)
            for name in ("kv_f", "kv_t", "nsa_q", "nsa_g"):
                split_lo(pool, name)
            nc.gpsimd.memset(mirror[:], 0.0).then_inc(sem("mirror"), 1)
            pool.wait_ge(sem("mirror"), 1)
            nc.gpsimd.affine_select(out=mirror[:], in_=mirror[:], compare_op=ALU.not_equal, fill=1.0, base=1 - P,
                                    pattern=[[1, P]], channel_multiplier=1).then_inc(sem("mirror"), 1)
            rel_store(pool)
            skew_pool(pool)
            split_lo(pool, "nsa_out")
            norm_pool(pool, 7)
            split_lo(pool, "ffn3_up")
            norm_pool(pool, 8)

        @nc_block.scalar
        def _(act):
            load_act(act)
            split_first(act, "ffn0_up")
            norm_act(act, 0, h_loaded)
            scaled_act(act, 0)
            load_table(act, 0, ACT.Silu)
            dense_act(act, "ffn0_up", up_evac_act)
            dense_act(act, "ffn0_down", nothing)
            split_first(act, "mix_ba")
            norm_act(act, 1, h_from("ffn0_down"))
            scaled_act(act, 1)
            dense_act(act, "mix_ba", ba_evac_act)
            dense_act(act, "mix_in", in_evac("act"))
            gdn_act(act)
            dense_act(act, "mix_out", nothing)
            norm_act(act, 2, h_from("mix_out"))
            scaled_act(act, 3)
            load_table(act, 1, ACT.Silu)
            dense_act(act, "ffn1_up", up_evac_act)
            mem_norm_act(act, 0)
            dense_act(act, "ffn1_down", nothing)
            norm_act(act, 3, h_from("ffn1_down"))
            norm_act(act, 4, lambda k: (sem("h_final"), k + 1))
            scaled_act(act, 4)
            dense_act(act, "mem0_kv", evac_to("act", mem_place))
            split_first(act, "gla_rest")
            dense_act(act, "gla_rest", evac_to("act", rest_place))
            gate_act(act)
            dense_act(act, "gla_q", evac_to("act", lambda i, t: (gq[:, t, :], 96, S, GDK ** -0.5)))
            dense_act(act, "gla_k", nothing)
            dense_act(act, "gla_v", evac_to("act", v_place))
            dense_act(act, "gla_g", evac_to("act", lambda i, t: (gg[:, bass.ds(4 * i + t, 1), :], 96, S, 1.0)))
            mem_attn_act(act, 0, 5, 8)
            gla_act(act)
            dense_act(act, "gla_out", nothing)
            split_first(act, "ffn2_up")
            norm_act(act, 5, h_from("gla_out"))
            scaled_act(act, 6)
            load_table(act, 2, ACT.Silu)
            dense_act(act, "ffn2_up", conv_evac_act)
            mem_norm_act(act, 1)
            dense_act(act, "ffn2_down", nothing)
            norm_act(act, 6, h_from("ffn2_down"))
            scaled_act(act, 7)
            dense_act(act, "mem1_kv", evac_to("act", mem_place))
            split_first(act, "kv_f")
            dense_act(act, "kv_f", evac_to("act", kv_place))
            dense_act(act, "kv_t", evac_to("act", kvt_place))
            scaled_act(act, 8, plan.full(plan.stages["kv_t"], 0, 7))
            dense_act(act, "nsa_q", evac_to("act", aq_place))
            dense_act(act, "nsa_g", gate_evac_act)
            cmp_act(act)
            mem_attn_act(act, 1, 9, 6)
            attend_act(act)
            dense_act(act, "nsa_out", nothing)
            norm_act(act, 7, h_from("nsa_out"))
            scaled_act(act, 10)
            load_table(act, 3, ACT.Silu)
            dense_act(act, "ffn3_up", conv_evac_act)
            dense_act(act, "ffn3_down", nothing)
            norm_act(act, 8, h_from("ffn3_down"))
            result_act(act)

        @nc_block.vector
        def _(dve):
            load_dve(dve)
            norm_dve(dve, 0)
            scaled_dve(dve, 0, "ffn1_norm")
            dense_dve(dve, "ffn0_up", up_evac_dve)
            dense_dve(dve, "ffn0_down", residual(0.5))
            norm_dve(dve, 1)
            scaled_dve(dve, 1, "mix_norm")
            dense_dve(dve, "mix_ba", ba_evac_dve)
            dense_dve(dve, "mix_in", in_evac("dve"))
            gdn_dve(dve)
            dense_dve(dve, "mix_out", residual(1.0))
            norm_dve(dve, 2)
            scaled_dve(dve, 3, "ffn2_norm")
            mem_turn_dve(dve, 0)
            dense_dve(dve, "ffn1_up", up_evac_dve)
            mem_norm_dve(dve, 0)
            dense_dve(dve, "ffn1_down", residual(0.5))
            norm_dve(dve, 3)
            final_dve(dve)
            norm_dve(dve, 4)
            scaled_dve(dve, 4, "norm_mix_2")
            dense_dve(dve, "mem0_kv", evac_to("dve", mem_place))
            dense_dve(dve, "gla_rest", evac_to("dve", rest_place))
            gate_dve(dve)
            dense_dve(dve, "gla_k", evac_to("dve", lambda i, t: (gk[:, t, :], 96, S, 1.0)))
            dense_dve(dve, "gla_v", evac_to("dve", v_place))
            mem_attn_dve(dve, 0, 5, 8, xbase(5))
            gla_dve(dve)
            gla_out_dve(dve)
            dense_dve(dve, "gla_out", residual(1.0))
            norm_dve(dve, 5)
            scaled_dve(dve, 6, "norm_ffn_2")
            mem_turn_dve(dve, 1)
            dense_dve(dve, "ffn2_up", conv_evac_dve)
            mem_norm_dve(dve, 1)
            dense_dve(dve, "ffn2_down", residual(1.0))
            norm_dve(dve, 6)
            scaled_dve(dve, 7, "kv_norm_2")
            dense_dve(dve, "mem1_kv", evac_to("dve", mem_place))
            dense_dve(dve, "kv_f", evac_to("dve", kv_place))
            dense_dve(dve, "kv_t", evac_to("dve", kvt_place))
            scaled_dve(dve, 8, "norm_mix_2", KD)
            dense_dve(dve, "nsa_q", evac_to("dve", aq_place))
            rel_dve(dve)
            pos_dve(dve)
            dense_dve(dve, "nsa_g", evac_to("dve", mq_place))
            cmp_dve(dve)
            mem_attn_dve(dve, 1, 9, 6, xbase(9))
            attend_dve(dve)
            dense_dve(dve, "nsa_out", residual(1.0))
            norm_dve(dve, 7)
            scaled_dve(dve, 10, "norm_ffn_2", KD)
            dense_dve(dve, "ffn3_up", conv_evac_dve)
            dense_dve(dve, "ffn3_down", residual(1.0))
            norm_dve(dve, 8)
            result_dve(dve)

        @nc_block.tensor
        def _(pe):
            load_pe(pe)
            norm_pe(pe, 0)
            dense_pe(pe, "ffn0_up")
            dense_pe(pe, "ffn0_down")
            norm_pe(pe, 1)
            dense_pe(pe, "mix_ba")
            dense_pe(pe, "mix_in")
            gdn_pe(pe)
            dense_pe(pe, "mix_out")
            norm_pe(pe, 2)
            mem_turn_pe(pe, 0, 2)
            dense_pe(pe, "ffn1_up")
            mem_sum_pe(pe, 0)
            dense_pe(pe, "ffn1_down")
            norm_pe(pe, 3)
            norm_pe(pe, 4)
            dense_pe(pe, "mem0_kv")
            dense_pe(pe, "gla_rest")
            gate_pe(pe)
            dense_pe(pe, "gla_q")
            dense_pe(pe, "gla_k")
            dense_pe(pe, "gla_v")
            dense_pe(pe, "gla_g")
            mem_attn_pe(pe, 0, stage_end("mem0_kv") + stage_end("gla_rest") + stage_end("gla_g") + stage_end("gla_v"))
            gla_pe(pe)
            dense_pe(pe, "gla_out")
            norm_pe(pe, 5)
            mem_turn_pe(pe, 1, 5)
            dense_pe(pe, "ffn2_up")
            mem_sum_pe(pe, 1)
            dense_pe(pe, "ffn2_down")
            norm_pe(pe, 6)
            dense_pe(pe, "mem1_kv")
            dense_pe(pe, "kv_f")
            dense_pe(pe, "kv_t")
            rel_pe(pe)
            dense_pe(pe, "nsa_q")
            dense_pe(pe, "nsa_g")
            cmp_pe(pe)
            mem_attn_pe(pe, 1, stage_end("mem1_kv") + stage_end("nsa_q") + stage_end("nsa_g") + [(sem("c_dve"), 2)])
            attend_pe(pe)
            dense_pe(pe, "nsa_out")
            norm_pe(pe, 7)
            dense_pe(pe, "ffn3_up")
            dense_pe(pe, "ffn3_down")
            norm_pe(pe, 8)
            result_pe(pe)


def kernel(**inputs):
    import numpy as _np
    import concourse.bacc as _bacc
    from concourse import mybir as _mybir
    from concourse.bass_utils import run_bass_kernel_spmd as _run

    nc = _bacc.Bacc("TRN2", target_bir_lowering=False, num_devices=1)
    arrays, args = {}, {}
    for name in inputs:
        a = _np.ascontiguousarray(inputs[name])
        arrays[f"in_{name}"] = a
        args[name] = nc.dram_tensor(f"in_{name}", a.shape, _mybir.dt.from_np(a.dtype), kind="ExternalInput").ap()
    out = nc.dram_tensor("out", (1, S, D), _mybir.dt.float32, kind="ExternalOutput").ap()
    build(nc, args, out)
    r = _run(nc, [arrays], core_ids=[0])
    return r.results[0]["out"]
```
